# Optimizing a Trainium2 kernel written in Bass

```python
import math
import jax, jax.numpy as jnp
from jax import lax
import numpy as np

D_MODEL = 2048
BATCH = 1
SEQ = 256
DEPTH = 1

N_MIXERS = 4
MEM_LEN = 256
RMS_EPS = 1e-6
NEG = -1e30
BIG = 1e30

SSD_EXPAND = 2
SSD_D_INNER = SSD_EXPAND * D_MODEL
SSD_HEAD_DIM = 64
SSD_N_HEADS = SSD_D_INNER // SSD_HEAD_DIM
SSD_N_GROUPS = 8
SSD_HPG = SSD_N_HEADS // SSD_N_GROUPS
SSD_D_STATE = 128
SSD_CONV = 4
SSD_CHUNK = 128
SSD_CONV_DIM = SSD_D_INNER + 2 * SSD_N_GROUPS * SSD_D_STATE
SSD_IN_DIM = SSD_D_INNER + SSD_CONV_DIM + SSD_N_HEADS

NSA_HEAD_DIM = 128
NSA_N_HEADS = D_MODEL // NSA_HEAD_DIM
NSA_KV_GROUPS = 4
NSA_HPG = NSA_N_HEADS // NSA_KV_GROUPS
NSA_KV_DIM = NSA_KV_GROUPS * NSA_HEAD_DIM
NSA_CMP_BLOCK = 32
NSA_CMP_STRIDE = 16
NSA_CMP_HIDDEN = 256
NSA_SLC_BLOCK = 64
NSA_TOPK = 16
NSA_N_LOCAL = 2
NSA_WINDOW = 512
NSA_Q_BLOCK = 64
NSA_WIN_Q_BLOCK = 128
NSA_IN_DIM = NSA_N_HEADS * NSA_HEAD_DIM + 6 * NSA_KV_DIM + 3 * NSA_N_HEADS

SGU_CHUNK = 128
SGU_WIDTH = 2 * D_MODEL
SGU_GROUPS = 8
SGU_GROUP_DIM = SGU_WIDTH // SGU_GROUPS

POOL_WINDOWS = (2, 4, 8, 16)
POOL_GROUPS = len(POOL_WINDOWS)
POOL_GROUP_DIM = D_MODEL // POOL_GROUPS

XA_HEADS = 4
XA_HEAD_DIM = 128
XA_DIM = XA_HEADS * XA_HEAD_DIM

FFN_HIDDEN = 5632
FFN_CONV = 3


def _rmsnorm(x, g):
    xf = x.astype(jnp.float32)
    y = xf * lax.rsqrt(jnp.mean(xf * xf, axis=-1, keepdims=True) + RMS_EPS)
    return (y * g.astype(jnp.float32)).astype(x.dtype)

def _layernorm(x, g):
    xf = x.astype(jnp.float32)
    mu = jnp.mean(xf, axis=-1, keepdims=True)
    xc = xf - mu
    y = xc * lax.rsqrt(jnp.mean(xc * xc, axis=-1, keepdims=True) + RMS_EPS)
    return (y * g.astype(jnp.float32)).astype(x.dtype)

def _causal_dwconv(x, w, b):
    k_w, L = w.shape[0], x.shape[1]
    xp = jnp.pad(x, ((0, 0), (k_w - 1, 0), (0, 0)))
    y = b + xp[:, 0:L] * w[0]
    for k in range(1, k_w):
        y = y + xp[:, k:k + L] * w[k]
    return y

def _ssd_mixer(h, w_in, conv_w, conv_b, dt_bias, a_log, d_skip, norm_g, w_out):
    f32 = jnp.float32
    bsz, L, _ = h.shape
    G, J, P, N, Q = SSD_N_GROUPS, SSD_HPG, SSD_HEAD_DIM, SSD_D_STATE, SSD_CHUNK
    nc = L // Q
    proj = h @ w_in
    z, xbc, dt = jnp.split(proj, [SSD_D_INNER, SSD_D_INNER + SSD_CONV_DIM], axis=-1)
    xbc = jax.nn.silu(_causal_dwconv(xbc, conv_w, conv_b)).astype(f32)
    xs, bm, cm = jnp.split(xbc, [SSD_D_INNER, SSD_D_INNER + G * N], axis=-1)
    xs = xs.reshape(bsz, nc, Q, G, J, P)
    bm = bm.reshape(bsz, nc, Q, G, N)
    cm = cm.reshape(bsz, nc, Q, G, N)
    dt = jax.nn.softplus(dt.astype(f32) + dt_bias.astype(f32)).reshape(bsz, nc, Q, G, J)
    a = dt * (-jnp.exp(a_log.astype(f32))).reshape(G, J)
    a_cs = jnp.cumsum(a.transpose(0, 3, 4, 1, 2), axis=-1)
    xdt = xs * dt[..., None]
    causal = jnp.tril(jnp.ones((Q, Q), dtype=bool))
    decay = jnp.exp(jnp.where(causal, a_cs[..., :, None] - a_cs[..., None, :], -jnp.inf))
    cb = jnp.einsum('bclgn,bcsgn->bgcls', cm, bm)
    y_diag = jnp.einsum('bgjcls,bcsgjp->bclgjp', cb[:, :, None] * decay, xdt)
    decay_to_end = jnp.exp(a_cs[..., -1:] - a_cs)
    states = jnp.einsum('bcsgn,bgjcs,bcsgjp->bcgjpn', bm, decay_to_end, xdt)
    chunk_decay = jnp.exp(a_cs[..., -1])

    def step(carry, inp):
        st, dec = inp
        return carry * dec[..., None, None] + st, carry

    init = jnp.zeros((bsz, G, J, P, N), f32)
    _, prev = lax.scan(step, init, (jnp.moveaxis(states, 1, 0), jnp.moveaxis(chunk_decay, 3, 0)))
    y_off = jnp.einsum('bclgn,cbgjpn,bgjcl->bclgjp', cm, prev, jnp.exp(a_cs))
    y = y_diag + y_off + xs * d_skip.astype(f32).reshape(G, J)[:, :, None]
    y = y.reshape(bsz, L, SSD_D_INNER)
    y = _rmsnorm(y * jax.nn.silu(z.astype(f32)), norm_g)
    return y.astype(h.dtype) @ w_out

def _nsa_mixer(h, w_in, cmp_pos, cmp_w1, cmp_w2, w_out):
    f32 = jnp.float32
    bsz, L, _ = h.shape
    G, J, Dh = NSA_KV_GROUPS, NSA_HPG, NSA_HEAD_DIM
    scale = Dh ** -0.5
    proj = h @ w_in
    offs = np.cumsum([NSA_N_HEADS * Dh] + [NSA_KV_DIM] * 6).tolist()
    q, kc_in, vc_in, ks, vs, kw, vw, gate_logits = jnp.split(proj, offs, axis=-1)
    q = q.reshape(bsz, L, G, J, Dh)
    kc_in, vc_in, ks, vs, kw, vw = [t.reshape(bsz, L, G, Dh) for t in (kc_in, vc_in, ks, vs, kw, vw)]
    gates = jax.nn.sigmoid(gate_logits.astype(f32)).reshape(bsz, L, G, J, 3).astype(h.dtype)
    t_pos = jnp.arange(L)

    ncmp = (L - NSA_CMP_BLOCK) // NSA_CMP_STRIDE + 1
    cmp_idx = np.arange(ncmp)[:, None] * NSA_CMP_STRIDE + np.arange(NSA_CMP_BLOCK)[None, :]

    def compress(t, pos, w1, w2):
        blk = t[:, cmp_idx] + pos[None, None, :, None, :]
        flat = blk.transpose(0, 1, 3, 2, 4).reshape(bsz, ncmp, G, NSA_CMP_BLOCK * Dh)
        return jax.nn.gelu(flat @ w1) @ w2

    kc = compress(kc_in, cmp_pos[0], cmp_w1[0], cmp_w2[0])
    vc = compress(vc_in, cmp_pos[1], cmp_w1[1], cmp_w2[1])
    s_c = jnp.einsum('btgjd,bigd->bgjti', q, kc).astype(f32) * scale
    cmp_end = jnp.arange(ncmp) * NSA_CMP_STRIDE + NSA_CMP_BLOCK - 1
    valid_c = cmp_end[None, :] <= t_pos[:, None]
    p_c = jnp.where(valid_c, jax.nn.softmax(jnp.where(valid_c, s_c, NEG), axis=-1), 0.0)
    o_cmp = jnp.einsum('bgjti,bigd->btgjd', p_c.astype(vc.dtype), vc)

    nslc = L // NSA_SLC_BLOCK
    ci = np.arange(ncmp)[:, None] * NSA_CMP_STRIDE
    sj = np.arange(nslc)[None, :] * NSA_SLC_BLOCK
    cover = jnp.asarray(((ci <= sj + NSA_SLC_BLOCK - 1) & (ci + NSA_CMP_BLOCK - 1 >= sj)).astype(np.float32))
    imp = jnp.einsum('bgjti,ik->bgtk', p_c, cover)
    blk = jnp.arange(nslc)[None, :]
    cur = (t_pos // NSA_SLC_BLOCK)[:, None]
    forced = (blk == 0) | ((blk <= cur) & (blk > cur - 1 - NSA_N_LOCAL))
    future = blk * NSA_SLC_BLOCK > t_pos[:, None]
    sel_score = jnp.where(forced, BIG, jnp.where(future, NEG, imp))
    topk = min(NSA_TOPK, nslc)
    _, sel_idx = lax.top_k(sel_score, topk)

    ks_blk = ks.reshape(bsz, nslc, NSA_SLC_BLOCK, G, Dh).transpose(0, 3, 1, 2, 4)
    vs_blk = vs.reshape(bsz, nslc, NSA_SLC_BLOCK, G, Dh).transpose(0, 3, 1, 2, 4)
    nqb = L // NSA_Q_BLOCK
    q_blocks = q.reshape(bsz, nqb, NSA_Q_BLOCK, G, J, Dh).transpose(1, 0, 2, 3, 4, 5)
    idx_blocks = sel_idx.reshape(bsz, G, nqb, NSA_Q_BLOCK, topk).transpose(2, 0, 1, 3, 4)
    starts = jnp.arange(nqb, dtype=jnp.int32) * NSA_Q_BLOCK
    b_i = jnp.arange(bsz)[:, None, None, None]
    g_i = jnp.arange(G)[None, :, None, None]
    in_blk = jnp.arange(NSA_SLC_BLOCK)

    def sel_block(args):
        qb, ib, t0 = args
        kg = ks_blk[b_i, g_i, ib]
        vg = vs_blk[b_i, g_i, ib]
        s = jnp.einsum('bqgjd,bgqksd->bgjqks', qb, kg).astype(f32) * scale
        pos = ib[..., None] * NSA_SLC_BLOCK + in_blk
        tq = t0 + jnp.arange(NSA_Q_BLOCK)
        valid = (pos <= tq[None, None, :, None, None])[:, :, None]
        p = jax.nn.softmax(jnp.where(valid, s, NEG), axis=(-2, -1))
        return jnp.einsum('bgjqks,bgqksd->bqgjd', p.astype(vg.dtype), vg)

    o_slc = lax.map(sel_block, (q_blocks, idx_blocks, starts))
    o_slc = o_slc.transpose(1, 0, 2, 3, 4, 5).reshape(bsz, L, G, J, Dh)

    WB = NSA_WIN_Q_BLOCK
    nb = L // WB
    nslab = NSA_WINDOW // WB + 1
    slab_len = nslab * WB
    slab_idx = np.arange(nb)[:, None] + np.arange(nslab)[None, :]
    kp = jnp.pad(kw, ((0, 0), (NSA_WINDOW, 0), (0, 0), (0, 0))).reshape(bsz, nb + nslab - 1, WB, G, Dh)
    vp = jnp.pad(vw, ((0, 0), (NSA_WINDOW, 0), (0, 0), (0, 0))).reshape(bsz, nb + nslab - 1, WB, G, Dh)
    k_slab = kp[:, slab_idx].reshape(bsz, nb, slab_len, G, Dh)
    v_slab = vp[:, slab_idx].reshape(bsz, nb, slab_len, G, Dh)
    qw = q.reshape(bsz, nb, WB, G, J, Dh)
    s_w = jnp.einsum('bnqgjd,bnkgd->bgjnqk', qw, k_slab).astype(f32) * scale
    spos = jnp.arange(nb)[:, None] * WB - NSA_WINDOW + jnp.arange(slab_len)[None, :]
    tpos = jnp.arange(nb)[:, None] * WB + jnp.arange(WB)[None, :]
    diff = tpos[:, :, None] - spos[:, None, :]
    valid_w = (spos[:, None, :] >= 0) & (diff >= 0) & (diff < NSA_WINDOW)
    p_w = jax.nn.softmax(jnp.where(valid_w, s_w, NEG), axis=-1)
    o_win = jnp.einsum('bgjnqk,bnkgd->bnqgjd', p_w.astype(v_slab.dtype), v_slab).reshape(bsz, L, G, J, Dh)

    o = gates[..., 0:1] * o_cmp + gates[..., 1:2] * o_slc + gates[..., 2:3] * o_win
    return o.reshape(bsz, L, NSA_N_HEADS * Dh) @ w_out

def _sgu_mixer(h, w_in, b_in, ln_g, w_spatial, b_spatial, w_out):
    bsz, L, _ = h.shape
    nc = L // SGU_CHUNK
    proj = jax.nn.gelu(h @ w_in + b_in)
    u, v = jnp.split(proj, 2, axis=-1)
    v = _layernorm(v, ln_g).reshape(bsz, nc, SGU_CHUNK, SGU_GROUPS, SGU_GROUP_DIM)
    tri = jnp.tril(jnp.ones((SGU_CHUNK, SGU_CHUNK), dtype=bool))
    w_m = jnp.where(tri[None], w_spatial, 0.0).astype(v.dtype)
    sv = jnp.einsum('gts,bcsgd->bctgd', w_m, v) + b_spatial.T[:, :, None]
    return (u * sv.reshape(bsz, L, SGU_WIDTH)) @ w_out

def _pool_mixer(h, w_in, w_group, scale, w_out):
    bsz, L, _ = h.shape
    z = (h @ w_in).reshape(bsz, L, POOL_GROUPS, POOL_GROUP_DIM).astype(jnp.float32)
    cs0 = jnp.concatenate([jnp.zeros_like(z[:, :1]), jnp.cumsum(z, axis=1)], axis=1)
    t_pos = jnp.arange(L)
    outs = []
    for gi, win in enumerate(POOL_WINDOWS):
        c = cs0[:, :, gi]
        lower = jnp.concatenate([jnp.zeros_like(c[:, :win - 1]), c[:, :L + 1 - win]], axis=1)
        count = jnp.minimum(t_pos + 1, win).astype(jnp.float32)[None, :, None]
        outs.append((c[:, 1:] - lower) / count - z[:, :, gi])
    pooled = jnp.stack(outs, axis=2).astype(h.dtype)
    y = jnp.einsum('blgd,gde->blge', pooled, w_group) * scale
    return y.reshape(bsz, L, D_MODEL) @ w_out

def _memory_cross_attention(h, mem_n, w_q, w_kv, w_o):
    bsz, L, _ = h.shape
    q = (h @ w_q).reshape(bsz, L, XA_HEADS, XA_HEAD_DIM)
    k, v = jnp.split(mem_n @ w_kv, 2, axis=-1)
    k = k.reshape(bsz, -1, XA_HEADS, XA_HEAD_DIM)
    v = v.reshape(bsz, -1, XA_HEADS, XA_HEAD_DIM)
    s = jnp.einsum('bthd,bmhd->bhtm', q, k).astype(jnp.float32) * (XA_HEAD_DIM ** -0.5)
    p = jax.nn.softmax(s, axis=-1).astype(v.dtype)
    o = jnp.einsum('bhtm,bmhd->bthd', p, v).reshape(bsz, L, XA_DIM)
    return o @ w_o

def _conv_ffn(h, w_up, conv_w, conv_b, w_down):
    u = _causal_dwconv(h @ w_up, conv_w, conv_b)
    gate, val = jnp.split(u, 2, axis=-1)
    return (jax.nn.silu(gate) * val) @ w_down

def first_inputs(seed: int = 0) -> dict:
    key = jax.random.key(seed)
    keys = iter(jax.random.split(key, 64))
    f32 = jnp.float32

    def nrm(shape, fan_in):
        return jax.random.normal(next(keys), shape, f32) * (fan_in ** -0.5)

    def gain(shape):
        return 1.0 + 0.05 * jax.random.normal(next(keys), shape, f32)

    def small(shape, s=0.02):
        return s * jax.random.normal(next(keys), shape, f32)

    n_a, n_b, n_c, n_d = [len(range(m, DEPTH, N_MIXERS)) for m in range(N_MIXERS)]
    x = jax.random.normal(next(keys), (BATCH, SEQ, D_MODEL), f32)
    mem = jax.random.normal(next(keys), (BATCH, MEM_LEN, D_MODEL), f32)
    norm_pre = gain((DEPTH, 3, D_MODEL))
    norm_post = gain((DEPTH, 3, D_MODEL))
    norm_mem = gain((DEPTH, D_MODEL))
    ssd_w_in = nrm((n_a, D_MODEL, SSD_IN_DIM), D_MODEL)
    ssd_conv_w = nrm((n_a, SSD_CONV, SSD_CONV_DIM), SSD_CONV)
    ssd_conv_b = small((n_a, SSD_CONV_DIM))
    dt0 = jnp.exp(jax.random.uniform(next(keys), (n_a, SSD_N_HEADS), f32, math.log(1e-3), math.log(1e-1)))
    ssd_dt_bias = dt0 + jnp.log(-jnp.expm1(-dt0))
    ssd_a_log = jnp.log(jax.random.uniform(next(keys), (n_a, SSD_N_HEADS), f32, 1.0, 16.0))
    ssd_d = gain((n_a, SSD_N_HEADS))
    ssd_norm_g = gain((n_a, SSD_D_INNER))
    ssd_w_out = nrm((n_a, SSD_D_INNER, D_MODEL), SSD_D_INNER)
    nsa_w_in = nrm((n_b, D_MODEL, NSA_IN_DIM), D_MODEL)
    nsa_cmp_pos = small((n_b, 2, NSA_CMP_BLOCK, NSA_HEAD_DIM), 0.1)
    nsa_cmp_w1 = nrm((n_b, 2, NSA_CMP_BLOCK * NSA_HEAD_DIM, NSA_CMP_HIDDEN), NSA_CMP_BLOCK * NSA_HEAD_DIM)
    nsa_cmp_w2 = nrm((n_b, 2, NSA_CMP_HIDDEN, NSA_HEAD_DIM), NSA_CMP_HIDDEN)
    nsa_w_out = nrm((n_b, NSA_N_HEADS * NSA_HEAD_DIM, D_MODEL), NSA_N_HEADS * NSA_HEAD_DIM)
    sgu_w_in = nrm((n_c, D_MODEL, 2 * SGU_WIDTH), D_MODEL)
    sgu_b_in = small((n_c, 2 * SGU_WIDTH))
    sgu_ln_g = gain((n_c, SGU_WIDTH))
    sgu_w_spatial = nrm((n_c, SGU_GROUPS, SGU_CHUNK, SGU_CHUNK), SGU_CHUNK)
    sgu_b_spatial = 1.0 + small((n_c, SGU_GROUPS, SGU_CHUNK), 0.1)
    sgu_w_out = nrm((n_c, SGU_WIDTH, D_MODEL), SGU_WIDTH)
    pool_w_in = nrm((n_d, D_MODEL, D_MODEL), D_MODEL)
    pool_w_group = nrm((n_d, POOL_GROUPS, POOL_GROUP_DIM, POOL_GROUP_DIM), POOL_GROUP_DIM)
    pool_scale = 1.0 + small((n_d, POOL_GROUPS, POOL_GROUP_DIM), 0.1)
    pool_w_out = nrm((n_d, D_MODEL, D_MODEL), D_MODEL)
    xa_w_q = nrm((DEPTH, D_MODEL, XA_DIM), D_MODEL)
    xa_w_kv = nrm((DEPTH, D_MODEL, 2 * XA_DIM), D_MODEL)
    xa_w_o = nrm((DEPTH, XA_DIM, D_MODEL), XA_DIM)
    ffn_w_up = nrm((DEPTH, D_MODEL, 2 * FFN_HIDDEN), D_MODEL)
    ffn_conv_w = nrm((DEPTH, FFN_CONV, 2 * FFN_HIDDEN), FFN_CONV)
    ffn_conv_b = small((DEPTH, 2 * FFN_HIDDEN))
    ffn_w_down = nrm((DEPTH, FFN_HIDDEN, D_MODEL), FFN_HIDDEN)
    return {
        "x": x, "mem": mem,
        "norm_pre": norm_pre, "norm_post": norm_post, "norm_mem": norm_mem,
        "ssd_w_in": ssd_w_in, "ssd_conv_w": ssd_conv_w, "ssd_conv_b": ssd_conv_b,
        "ssd_dt_bias": ssd_dt_bias, "ssd_a_log": ssd_a_log, "ssd_d": ssd_d,
        "ssd_norm_g": ssd_norm_g, "ssd_w_out": ssd_w_out,
        "nsa_w_in": nsa_w_in, "nsa_cmp_pos": nsa_cmp_pos, "nsa_cmp_w1": nsa_cmp_w1,
        "nsa_cmp_w2": nsa_cmp_w2, "nsa_w_out": nsa_w_out,
        "sgu_w_in": sgu_w_in, "sgu_b_in": sgu_b_in, "sgu_ln_g": sgu_ln_g,
        "sgu_w_spatial": sgu_w_spatial, "sgu_b_spatial": sgu_b_spatial, "sgu_w_out": sgu_w_out,
        "pool_w_in": pool_w_in, "pool_w_group": pool_w_group, "pool_scale": pool_scale,
        "pool_w_out": pool_w_out,
        "xa_w_q": xa_w_q, "xa_w_kv": xa_w_kv, "xa_w_o": xa_w_o,
        "ffn_w_up": ffn_w_up, "ffn_conv_w": ffn_conv_w, "ffn_conv_b": ffn_conv_b,
        "ffn_w_down": ffn_w_down,
    }

def first_block(x, mem, norm_pre, norm_post, norm_mem,
              ssd_w_in, ssd_conv_w, ssd_conv_b, ssd_dt_bias, ssd_a_log, ssd_d, ssd_norm_g, ssd_w_out,
              nsa_w_in, nsa_cmp_pos, nsa_cmp_w1, nsa_cmp_w2, nsa_w_out,
              sgu_w_in, sgu_b_in, sgu_ln_g, sgu_w_spatial, sgu_b_spatial, sgu_w_out,
              pool_w_in, pool_w_group, pool_scale, pool_w_out,
              xa_w_q, xa_w_kv, xa_w_o,
              ffn_w_up, ffn_conv_w, ffn_conv_b, ffn_w_down):
    for i in range(DEPTH):
        kind, j = i % N_MIXERS, i // N_MIXERS
        h = _rmsnorm(x, norm_pre[i, 0])
        if kind == 0:
            m = _ssd_mixer(h, ssd_w_in[j], ssd_conv_w[j], ssd_conv_b[j], ssd_dt_bias[j],
                           ssd_a_log[j], ssd_d[j], ssd_norm_g[j], ssd_w_out[j])
        elif kind == 1:
            m = _nsa_mixer(h, nsa_w_in[j], nsa_cmp_pos[j], nsa_cmp_w1[j], nsa_cmp_w2[j], nsa_w_out[j])
        elif kind == 2:
            m = _sgu_mixer(h, sgu_w_in[j], sgu_b_in[j], sgu_ln_g[j], sgu_w_spatial[j],
                           sgu_b_spatial[j], sgu_w_out[j])
        else:
            m = _pool_mixer(h, pool_w_in[j], pool_w_group[j], pool_scale[j], pool_w_out[j])
        x = x + _rmsnorm(m, norm_post[i, 0])
        h = _rmsnorm(x, norm_pre[i, 1])
        a = _memory_cross_attention(h, _rmsnorm(mem, norm_mem[i]), xa_w_q[i], xa_w_kv[i], xa_w_o[i])
        x = x + _rmsnorm(a, norm_post[i, 1])
        h = _rmsnorm(x, norm_pre[i, 2])
        f = _conv_ffn(h, ffn_w_up[i], ffn_conv_w[i], ffn_conv_b[i], ffn_w_down[i])
        x = x + _rmsnorm(f, norm_post[i, 2])
    return x


HEAD_DIM = 128
N_HEADS_A = 8
N_HEADS_B = 8
MIX_WIDTH = (N_HEADS_A + N_HEADS_B) * HEAD_DIM
KV_RANK = 256
IDX_HEADS = 16
IDX_DIM = 64
TOPK_MAX = 256
N_BUCKETS = 32
MAX_DISTANCE = 128
D_FF = 5632
CONV_WIDTH = 3
Q_BLOCK = 128
EPS = 1e-6

COL_SIZES = (
    N_HEADS_A * HEAD_DIM,
    KV_RANK,
    IDX_HEADS * IDX_DIM,
    IDX_DIM,
    IDX_HEADS,
    N_HEADS_B * HEAD_DIM,
    N_HEADS_B * HEAD_DIM,
    N_HEADS_B * HEAD_DIM,
    N_HEADS_B,
)
D_IN = sum(COL_SIZES)


def rmsnorm(x, g):
    xf = x.astype(jnp.float32)
    y = xf * lax.rsqrt(jnp.mean(xf * xf, axis=-1, keepdims=True) + EPS)
    return (y * g.astype(jnp.float32)).astype(x.dtype)

def t5_bucket(n):
    max_exact = N_BUCKETS // 2
    nf = jnp.maximum(n, 1).astype(jnp.float32)
    large = max_exact + (jnp.log(nf / max_exact) / math.log(MAX_DISTANCE / max_exact)
                         * (N_BUCKETS - max_exact)).astype(jnp.int32)
    large = jnp.minimum(large, N_BUCKETS - 1)
    return jnp.where(n < max_exact, n, large)

def to_blocks(a):
    b, l = a.shape[0], a.shape[1]
    a = a.reshape((b, l // Q_BLOCK, Q_BLOCK) + a.shape[2:])
    return jnp.moveaxis(a, 1, 0)

def from_blocks(a):
    a = jnp.moveaxis(a, 0, 1)
    return a.reshape((a.shape[0], a.shape[1] * a.shape[2]) + a.shape[3:])

def dsa_mixer(q, c_kv, q_idx, k_idx, w_idx, w_uk, w_uv, t5_table):
    L = q.shape[1]
    nb = L // Q_BLOCK
    topk = min(TOPK_MAX, L // 4)
    key_pos = jnp.arange(L)
    q_lat = jnp.einsum('bthd,hdr->bthr', q, w_uk)

    def block(args):
        blk, ql, qi, wi = args
        t_pos = blk * Q_BLOCK + jnp.arange(Q_BLOCK)
        causal = key_pos[None, :] <= t_pos[:, None]
        dots = jnp.einsum('bthd,bsd->bths', qi, k_idx).astype(jnp.float32) * (IDX_DIM ** -0.5)
        score = jnp.einsum('bth,bths->bts', wi.astype(jnp.float32) * (IDX_HEADS ** -0.5),
                           jax.nn.relu(dots))
        score = jnp.where(causal[None], score, -jnp.inf)
        _, sel = lax.top_k(score, topk)
        c_sel = jax.vmap(lambda c, i: c[i])(c_kv, sel)
        dist = t_pos[None, :, None] - sel
        valid = dist >= 0
        bias = t5_table[t5_bucket(jnp.maximum(dist, 0))]
        logits = (jnp.einsum('bthr,btkr->bthk', ql, c_sel).astype(jnp.float32) * (HEAD_DIM ** -0.5)
                  + jnp.moveaxis(bias, -1, 2).astype(jnp.float32))
        logits = jnp.where(valid[:, :, None, :], logits, -jnp.inf)
        p = jax.nn.softmax(logits, axis=-1).astype(c_sel.dtype)
        return jnp.einsum('bthk,btkr->bthr', p, c_sel)

    o_lat = from_blocks(lax.map(block, (jnp.arange(nb), to_blocks(q_lat),
                                        to_blocks(q_idx), to_blocks(w_idx))))
    return jnp.einsum('bthr,hrd->bthd', o_lat, w_uv)

def fox_mixer(q, k, v, log_f):
    L = q.shape[1]
    nb = L // Q_BLOCK
    key_pos = jnp.arange(L)
    cum = jnp.cumsum(log_f.astype(jnp.float32), axis=1)
    cum_k = jnp.moveaxis(cum, 1, 2)

    def block(args):
        blk, qb, cq = args
        t_pos = blk * Q_BLOCK + jnp.arange(Q_BLOCK)
        causal = key_pos[None, :] <= t_pos[:, None]
        decay = jnp.moveaxis(cq, 1, 2)[..., None] - cum_k[:, :, None, :]
        logits = jnp.einsum('bthd,bshd->bhts', qb, k).astype(jnp.float32) * (HEAD_DIM ** -0.5) + decay
        logits = jnp.where(causal[None, None], logits, -jnp.inf)
        p = jax.nn.softmax(logits, axis=-1).astype(v.dtype)
        return jnp.einsum('bhts,bshd->bthd', p, v)

    return from_blocks(lax.map(block, (jnp.arange(nb), to_blocks(q), to_blocks(cum))))

def conv_ffn(h, w_up, conv_w, conv_b, w_down):
    L = h.shape[1]
    u = h @ w_up
    up = jnp.pad(u, ((0, 0), (CONV_WIDTH - 1, 0), (0, 0)))
    acc = conv_b
    for j in range(CONV_WIDTH):
        acc = acc + conv_w[j] * up[:, j:j + L]
    gate, val = jnp.split(acc, 2, axis=-1)
    return (jax.nn.silu(gate) * val) @ w_down

def second_inputs(seed: int = 0) -> dict:
    key = jax.random.key(seed)
    ks = jax.random.split(key, 15)
    f32 = jnp.float32
    n = lambda k, s: jax.random.normal(k, s, f32)
    return {
        'x': n(ks[0], (BATCH, SEQ, D_MODEL)),
        'w_in': n(ks[1], (DEPTH, D_MODEL, D_IN)) * D_MODEL ** -0.5,
        'kv_norm_g': 1.0 + 0.02 * n(ks[2], (DEPTH, KV_RANK)),
        'w_uk': n(ks[3], (DEPTH, N_HEADS_A, HEAD_DIM, KV_RANK)) * KV_RANK ** -0.5,
        'w_uv': n(ks[4], (DEPTH, N_HEADS_A, KV_RANK, HEAD_DIM)) * KV_RANK ** -0.5,
        't5_table': 0.5 * n(ks[5], (N_BUCKETS, N_HEADS_A)),
        'fgate_b': 3.0 + 0.1 * n(ks[6], (DEPTH, N_HEADS_B)),
        'w_o': n(ks[7], (DEPTH, MIX_WIDTH, D_MODEL)) * MIX_WIDTH ** -0.5,
        'norm1_g': 1.0 + 0.02 * n(ks[8], (DEPTH, D_MODEL)),
        'norm2_g': 1.0 + 0.02 * n(ks[9], (DEPTH, D_MODEL)),
        'w_up': n(ks[10], (DEPTH, D_MODEL, 2 * D_FF)) * D_MODEL ** -0.5,
        'conv_w': 0.5 * n(ks[11], (DEPTH, CONV_WIDTH, 2 * D_FF)),
        'conv_b': 0.02 * n(ks[12], (DEPTH, 2 * D_FF)),
        'w_down': n(ks[13], (DEPTH, D_FF, D_MODEL)) * D_FF ** -0.5,
        'final_g': 1.0 + 0.02 * n(ks[14], (D_MODEL,)),
    }

def second_block(x, w_in, kv_norm_g, w_uk, w_uv, t5_table, fgate_b, w_o, norm1_g, norm2_g,
              w_up, conv_w, conv_b, w_down, final_g):
    B, L, _ = x.shape
    split_points = [int(s) for s in np.cumsum(COL_SIZES)[:-1]]
    for l in range(DEPTH):
        h = rmsnorm(x, norm1_g[l])
        proj = h @ w_in[l]
        aq, akv, aiq, aik, aiw, bq, bk, bv, bf = jnp.split(proj, split_points, axis=-1)
        c_kv = rmsnorm(akv, kv_norm_g[l])
        o_a = dsa_mixer(aq.reshape(B, L, N_HEADS_A, HEAD_DIM), c_kv,
                        aiq.reshape(B, L, IDX_HEADS, IDX_DIM), aik, aiw,
                        w_uk[l], w_uv[l], t5_table)
        log_f = jax.nn.log_sigmoid(bf.astype(jnp.float32) + fgate_b[l].astype(jnp.float32))
        o_b = fox_mixer(bq.reshape(B, L, N_HEADS_B, HEAD_DIM),
                        bk.reshape(B, L, N_HEADS_B, HEAD_DIM),
                        bv.reshape(B, L, N_HEADS_B, HEAD_DIM), log_f)
        mix = jnp.concatenate([o_a.reshape(B, L, -1), o_b.reshape(B, L, -1)], axis=-1)
        x = x + mix @ w_o[l]
        x = x + conv_ffn(rmsnorm(x, norm2_g[l]), w_up[l], conv_w[l], conv_b[l], w_down[l])
    return rmsnorm(x, final_g)


def setup_inputs(seed=0):
    out = dict(first_inputs(seed))
    for name, value in second_inputs(seed + 1).items():
        if name != "x":
            out[name + "_2"] = value
    return out


def reference(
    x, mem, norm_pre, norm_post, norm_mem, ssd_w_in, ssd_conv_w, ssd_conv_b, ssd_dt_bias,
    ssd_a_log, ssd_d, ssd_norm_g, ssd_w_out, nsa_w_in, nsa_cmp_pos, nsa_cmp_w1, nsa_cmp_w2,
    nsa_w_out, sgu_w_in, sgu_b_in, sgu_ln_g, sgu_w_spatial, sgu_b_spatial, sgu_w_out, pool_w_in,
    pool_w_group, pool_scale, pool_w_out, xa_w_q, xa_w_kv, xa_w_o, ffn_w_up, ffn_conv_w,
    ffn_conv_b, ffn_w_down, w_in_2, kv_norm_g_2, w_uk_2, w_uv_2, t5_table_2, fgate_b_2, w_o_2,
    norm1_g_2, norm2_g_2, w_up_2, conv_w_2, conv_b_2, w_down_2, final_g_2,
):
    x = first_block(
        x, mem, norm_pre, norm_post, norm_mem, ssd_w_in, ssd_conv_w, ssd_conv_b, ssd_dt_bias,
        ssd_a_log, ssd_d, ssd_norm_g, ssd_w_out, nsa_w_in, nsa_cmp_pos, nsa_cmp_w1, nsa_cmp_w2,
        nsa_w_out, sgu_w_in, sgu_b_in, sgu_ln_g, sgu_w_spatial, sgu_b_spatial, sgu_w_out,
        pool_w_in, pool_w_group, pool_scale, pool_w_out, xa_w_q, xa_w_kv, xa_w_o, ffn_w_up,
        ffn_conv_w, ffn_conv_b, ffn_w_down,
    )
    return second_block(
        x, w_in_2, kv_norm_g_2, w_uk_2, w_uv_2, t5_table_2, fgate_b_2, w_o_2, norm1_g_2,
        norm2_g_2, w_up_2, conv_w_2, conv_b_2, w_down_2, final_g_2,
    )


_drawn_inputs = setup_inputs


def setup_inputs(seed=0):
    import zlib

    import numpy as np

    out = dict(_drawn_inputs(seed))
    spreads = {}
    factors = {'ffn_conv_b': 3.42,
     'kv_norm_g_2': 8.0,
     'fgate_b_2': 64.0,
     'norm1_g_2': 5.354,
     'norm2_g_2': 8.0,
     'conv_b_2': 8.0,
     'final_g_2': 7.958}
    for name, (base, spread) in spreads.items():
        noise = np.random.default_rng([zlib.crc32(name.encode()), seed]).standard_normal(out[name].shape)
        drawn = base * np.exp(spread * noise) if base else spread * noise
        out[name] = __import__('jax').numpy.asarray(drawn.astype(out[name].dtype))
    for name, factor in factors.items():
        out[name] = (out[name] * factor).astype(out[name].dtype)
    return out
```

```python
from contextlib import ExitStack

import numpy as np

import concourse.bass as bass
from concourse import mybir

F32 = mybir.dt.float32
F32R = mybir.dt.float32r
ALU = mybir.AluOpType
ACT = mybir.ActivationFunctionType
AX_X = mybir.AxisListType.X

P = 128
L = 256
TT = L // P
D = 2048
KC = D // P
BLK = 512
NB = D // BLK
EPS = 1e-6
NEG = -1e30
TAKEN = -3e38

GROUPS, HPG, HD, NST = 8, 8, 64, 128
HEADS = GROUPS * HPG
DI = HEADS * HD
XS_COL, B_COL, C_COL, DT_COL = DI, 2 * DI, 2 * DI + GROUPS * NST, 2 * DI + 2 * GROUPS * NST
CONV_CH = (DI + 2 * GROUPS * NST) // P
SSD_TAPS = 4
XH = 4
XW = XH * P
F = 5632
FC = F // P
FB = F // BLK
FFN_TAPS = 3
AH, BH, RANK, IH, ID = 8, 8, 256, 16, 64
TOPK = min(256, L // 4)
NBUCKET, MAXDIST = 32, 128
AKV = AH * P
AIQ = AKV + RANK
AIK = AIQ + IH * ID
AIW = AIK + ID
BQ = AIW + IH
BK = BQ + BH * P
BV = BK + BH * P
BF = BV + BH * P
ODD = RANK + ID + IH + BH
SCALE = float(P) ** -0.5

COLS = {}
_n = 0
for _name, _rows in (("norm_pre", 3 * KC), ("norm_mem", KC), ("ssd_conv_w", SSD_TAPS * CONV_CH),
                     ("ssd_conv_b", CONV_CH), ("ssd_norm_g", DI // P), ("ffn_conv_w", FFN_TAPS * 2 * FC),
                     ("ffn_conv_b", 2 * FC), ("norm1_g_2", KC), ("norm2_g_2", KC),
                     ("conv_w_2", FFN_TAPS * 2 * FC), ("conv_b_2", 2 * FC)):
    COLS[_name] = (_n, _rows)
    _n += _rows
NCOL = _n
NROWT = -(-NCOL // P)
N_ROW_LOADS = sum((r + n - 1) // P - r // P + 1 for r, n in COLS.values())

U_KV, U_DT, U_SSD = 0, 2, 3
U_WOUT = U_SSD + 3 * GROUPS
U_XQ = U_WOUT + DI // P // 4
U_XO = U_XQ + 1
U_UP1 = U_XO + 1
U_DN1 = U_UP1 + 2 * FB
U_IN2 = U_DN1 + FC // 4
U_ODD = U_IN2 + 4
U_B = U_ODD + 1
U_WO2 = U_B + 6
U_UP2 = U_WO2 + 4
U_DN2 = U_UP2 + 2 * FB
U_END = U_DN2 + FC // 4

E_KV, E_DT, E_SSD = 1, 3, 4
E_XQ = E_SSD + 3 * GROUPS
E_UP1 = E_XQ + 1
E_IN2 = E_UP1 + 2 * FB
E_ODD = E_IN2 + 4
E_B = E_ODD + 1
E_UP2 = E_B + 6

X_WOUT = 0
X_XO = X_WOUT + DI // P
X_DN1 = X_XO + XH
X_WO2 = X_DN1 + FC
X_DN2 = X_WO2 + KC

N_MEM, N_X, N_Y, N_P1, N_H1, N_P2, N_H2, N_P3, N_1, N_CKV, N_2, N_FIN = range(12)
TRANSPOSED = [N_MEM, N_X, N_H1, N_H2, N_1, N_2]

T_PLAN = [("params", (1, 1, 1, 0)), (N_MEM, (2,) * 4), ("kv", (1, 1, 0, 0)), (N_X, (2,) * 4),
          ("dt", (0, 0, 1, 1)), ("ssd", (4 * GROUPS, 4 * GROUPS, 2 * GROUPS, 2 * GROUPS)), (N_H1, (2,) * 4),
          ("xa", (3, 3, 2, 2)), (N_H2, (2,) * 4), ("up1", (FB,) * 4), (N_1, (2,) * 4), ("in2", (5, 5, 5, 4)),
          ("line", (0, 0, 0, 1)), ("qlat", (2,) * 4), ("idx", (4,) * 4), ("fox", (4,) * 4), ("dsa", (4,) * 4),
          (N_2, (2,) * 4), ("up2", (FB,) * 4), ("end", (0,) * 4)]
TB = {}
_at = [0] * 4
for _name, _uses in T_PLAN:
    TB[_name] = tuple(_at)
    _at = [a + u for a, u in zip(_at, _uses)]


IN2_UNITS = [(U_IN2, "aq", 0), (U_IN2 + 1, "aiq", 0), (U_IN2 + 2, "aq", 1), (U_IN2 + 3, "aiq", 1), (U_ODD, "odd", 0),
             (U_B, "bq", 0), (U_B + 1, "bk", 0), (U_B + 2, "bv", 0), (U_B + 3, "bq", 1), (U_B + 4, "bk", 1), (U_B + 5, "bv", 1)]
IN2_SLOT = {"aq": 0, "aiq": 1, "bq": 0, "bk": 1}
IN2_USE = {"aq": (0, 0), "aiq": (0, 0), "bq": (3, 3), "bk": (3, 2)}
IN2_TURN = {"aq": 0, "aiq": 0, "bq": 2, "bk": 2}


class Chain:

    def __init__(self, eng, sem):
        self.eng, self.sem, self.n, self.reg, self.per = eng, sem, 0, None, 0

    def __call__(self, ins):
        self.n += 1
        ins.then_inc(self.sem, 1)
        self.eng.wait_ge(self.sem, self.n if self.reg is None else self.reg * self.per + self.n)

    def enter(self, reg, per):
        self.reg, self.per, self.start = reg, per, self.n

    def leave(self, turns):
        assert self.n - self.start == self.per, (self.n - self.start, self.per)
        self.n = self.start + self.per * turns
        self.reg = None


def program(nc, I, out):
    with ExitStack() as ctx:
        def sb(name, shape, dt=F32):
            return ctx.enter_context(nc.sbuf_tensor(name, shape, dt))

        def sem(name):
            return ctx.enter_context(nc.semaphore(name))

        hT_at = -(-nc.sbuf_base // 32) * 32
        hT_hi = sb("hT_hi", [P, KC, L], F32R)
        hT_lo = sb("hT_lo", [P, KC, L], F32R)
        attn = nc.alloc_sbuf_tensor_at("attn", [P, 2 * KC * L], F32, offset=hT_at)
        raw = sb("raw", [P, 4, 4 * BLK])
        w_hi = sb("w_hi", [P, 4, 4 * BLK], F32R)
        w_lo = sb("w_lo", [P, 4, 4 * BLK], F32R)
        big = sb("big", [P, FC * L])
        x = sb("x", [P, TT * D])
        u = sb("u", [P, 4 * BLK])
        vb = sb("vb", [P, 4 * L])
        cols = sb("cols", [P, NCOL])
        ident = sb("ident", [P, P])
        triu = sb("triu", [P, P])
        ones = sb("ones", [P, P])
        small = sb("small", [P, 3 * HEADS])
        misc = sb("misc", [P, L])
        stat = sb("stat", [P, 48])

        bigc = big[:, :].rearrange("p (c t) -> p c t", t=L)
        xt = x[:, :].rearrange("p (a n) -> p a n", a=TT)
        u2 = u[:, :].rearrange("p (s a n) -> p s a n", s=2, a=TT)
        vbc = vb[:, :].rearrange("p (c t) -> p c t", t=L)
        xn_big = big[:, 0:TT * D].rearrange("p (a n) -> p a n", a=TT)
        tmp_big = big[:, TT * D:2 * TT * D].rearrange("p (a n) -> p a n", a=TT)
        bank2 = "p (c t) -> p c t"

        ssq = lambda n: stat[:, 2 * n:2 * n + 2]
        rstd = lambda n: stat[:, 24 + 2 * n:24 + 2 * n + 2]
        ssq_parts = sb("ssq_parts", [P, TT * NB])
        half = sb("half", [P, 2])
        mx = sb("mx", [P, 4])
        den = sb("den", [P, 4])
        rden = sb("rden", [P, 4])

        idle = sb("idle", [P, 13])
        rows = tmp_big[:, 0, 0:NROWT * P].rearrange("p (r f) -> p r f", f=P)

        ssd_m = x[:, 0:8 * L].rearrange("p (h t) -> p h t", t=L)
        xdt = x[:, 2048:3072].rearrange("p (a n) -> p a n", a=TT)
        yg = x[:, 3072:4096].rearrange("p (a n) -> p a n", a=TT)
        zs = big[:, 8192:9216].rearrange("p (a n) -> p a n", a=TT)
        xc = big[:, 9216:10240].rearrange(bank2, t=L)
        bc = big[:, 10240:10752].rearrange(bank2, t=L)
        bd = big[:, 10752:11264]
        u_xs = u2[:, 0]
        u_bc = u[:, 1024:1536].rearrange("p (a n) -> p a n", a=TT)
        states = u[:, 1536:2048]
        dt = vb[:, 0:128].rearrange("p (a h) -> p a h", a=TT)
        da = vb[:, 128:256].rearrange("p (a h) -> p a h", a=TT)
        acs = vb[:, 256:384].rearrange("p (a h) -> p a h", a=TT)
        dte = vb[:, 384:448]
        eacs = vb[:, 448:512]
        bm = vb[:, 512:640]
        cbm = vb[:, 640:896].rearrange("p (a t) -> p a t", a=TT)
        yssq = vb[:, 896:900].rearrange("p (k a) -> p k a", k=2)
        dt_bias, a_log, d_skip = (small[:, k * HEADS:(k + 1) * HEADS] for k in range(3))
        acsT = misc[0:HEADS, :]
        sp_tmp = [big[:, 4096 + 128 * k:4096 + 128 * (k + 1)] for k in range(8)]

        xa_kT = big[:, 4096:5120].rearrange(bank2, t=L)
        xa_v = big[:, 5120:6144].rearrange("p (a n) -> p a n", a=TT)
        xa_qT = big[:, 6144:7168].rearrange(bank2, t=L)
        xa_oT = big[:, 7168:8192].rearrange(bank2, t=L)
        prob = [u[:, 512 * k:512 * (k + 1)].rearrange("p (a s) -> p a s", a=TT) for k in range(2)]
        probT = [u[:, 1024 + 512 * k:1024 + 512 * (k + 1)].rearrange("p (a t) -> p a t", a=TT) for k in range(2)]

        aqT = big[:, 0:2048].rearrange(bank2, t=L)
        aiqT = big[:, 2048:4096].rearrange(bank2, t=L)
        bqT = big[:, 4096:6144].rearrange(bank2, t=L)
        bkT = big[:, 6144:8192].rearrange(bank2, t=L)
        bv = big[:, 8192:10240].rearrange("p (a n) -> p a n", a=TT)
        ckv = big[:, 10240:10752].rearrange("p (a r) -> p a r", a=TT)
        ckvT = big[:, 10752:11264].rearrange(bank2, t=L)
        w_uv = big[:, 0:2048].rearrange("p (h c d) -> p h c d", h=AH, c=2)
        w_uk = u[:, :].rearrange("p (h r) -> p h r", h=AH)
        qlT = attn[:, 0:4096].rearrange("p (h c t) -> p h c t", h=AH, c=2)
        skew = attn[:, 4096:7168].rearrange("p (h s) -> p h s", h=AH)
        score = attn[:, 7168:7680].rearrange("p (a s) -> p a s", a=TT)
        sel = attn[:, 7680:8192].rearrange("p (a s) -> p a s", a=TT)
        mixT = x[:, :].rearrange(bank2, t=L)
        odd = x[:, 0:2 * ODD].rearrange("p (a n) -> p a n", a=TT)
        aik2 = x[:, 768:1024].rearrange("p (a k n) -> p a k n", a=TT, k=2)
        onehot = x[0:NBUCKET, 1024:1536]
        line = x[0:AH, 1536:2048]
        kv_gain = x[:, 2048:2048 + RANK]
        table = x[0:NBUCKET, 2304:2304 + AH]
        fg_bias = x[:, 2320:2320 + BH]
        fox_tmp = [x[:, 2400 + 16 * k:2416 + 16 * k] for k in range(8)]
        lf = x[:, 2560:2576].rearrange("p (a h) -> p a h", a=TT)
        mask = vb[:, 0:512].rearrange("p (a s) -> p a s", a=TT)
        aikT = vb[:, 512:768]
        cum_row = vb[0:BH, 768:1024]
        anti = small[:, 0:P]
        iw = small[:, 128:160].rearrange("p (a h) -> p a h", a=TT)
        top8 = small[:, 160:176].rearrange("p (a k) -> p a k", a=TT)
        cumT = misc[0:BH, :]
        o_lat = attn[:, 7168:7680].rearrange(bank2, t=L)
        rl = [u[:, 512 * k:512 * (k + 1)].rearrange("p (a s) -> p a s", a=TT) for k in range(4)]

        PB = [ctx.enter_context(nc.psum_tensor(f"PB{k}", [P, BLK], F32)) for k in range(4)]
        T = [ctx.enter_context(nc.psum_tensor(f"T{k}", [P, BLK], F32)) for k in range(4)]
        T2 = [t[:, :].rearrange(bank2, t=L) for t in T]
        acc = [PB, T]

        kT_d = nc.dram_tensor("kT_d", (P, XH * L), F32, kind="Internal").ap()
        v_d = nc.dram_tensor("v_d", (P, TT * XW), F32, kind="Internal").ap()
        acsT_d = nc.dram_tensor("acsT_d", (HEADS, L), F32, kind="Internal").ap()
        x_d = nc.dram_tensor("x_d", (P, TT * D), F32, kind="Internal").ap()
        line_d = nc.dram_tensor("line_d", (AH, BLK), F32, kind="Internal").ap()

        raw_landed = [sem(f"raw_landed{j}") for j in range(4)]
        c_landed = [sem(f"c_landed{j}") for j in range(4)]
        odd_landed = [sem(f"odd_landed{j}") for j in range(4)]
        hi_ready, lo_ready = sem("hi_ready"), sem("lo_ready")
        quad_used = sem("quad_used")
        proj_evac = sem("proj_evac")
        tf = [sem(f"t{b}_full") for b in range(4)]
        te = [sem(f"t{b}_empty") for b in range(4)]
        xs_hi, xs_lo = sem("xs_hi"), sem("xs_lo")
        consts_ready, rows_landed, cols_ready = sem("consts_ready"), sem("rows_landed"), sem("cols_ready")
        x_landed, mem_landed, small_landed = sem("x_landed"), sem("mem_landed"), sem("small_landed")
        sq_done, ms_done, rstd_done = sem("sq_done"), sem("ms_done"), sem("rstd_done")
        xn_ready = sem("xn_ready")
        h_hi_done = sem("h_hi_done")
        kT_copied, kv_stored, kv_loaded = sem("kT_copied"), sem("kv_stored"), sem("kv_loaded")
        exp_asked, exp_done = sem("exp_asked"), sem("exp_done")
        da_ready, acsT_ready, acsT_stored = sem("da_ready"), sem("acsT_ready"), sem("acsT_stored")
        acs_landed, diff_made, diff_ready = sem("acs_landed"), sem("diff_made"), sem("diff_ready")
        decay_ready, m_ready = sem("decay_ready"), sem("m_ready")
        bc_tap, bc_ready, xs_tap, xc_ready = sem("bc_tap"), sem("bc_ready"), sem("xs_tap"), sem("xc_ready")
        bd_ready, yg_ready = sem("bd_ready"), sem("yg_ready")
        x_back, gain_landed, x_new, x_spilled = sem("x_back"), sem("gain_landed"), sem("x_new"), sem("x_spilled")
        gate_tap, val_tap, gate_act, ffn_mul = sem("gate_tap"), sem("val_tap"), sem("gate_act"), sem("ffn_mul")
        s_max, p_exp, p_ready = sem("s_max"), sem("p_exp"), sem("p_ready")
        pv_done, pv_taken = sem("pv_done"), sem("pv_taken")
        uv_done, uv_taken = sem("uv_done"), sem("uv_taken")
        m2_landed, m2_consts = sem("m2_landed"), sem("m2_consts")
        odd_ready, decay_sum_ready = sem("odd_ready"), sem("decay_sum_ready")
        line_ready, line_stored, skew_landed = sem("line_ready"), sem("line_stored"), sem("skew_landed")
        uk_landed, uv_landed, cum_row_ready = sem("uk_landed"), sem("uv_landed"), sem("cum_row_ready")
        relu_done, relu_used, sel_ready = sem("relu_done"), sem("relu_used"), sem("sel_ready")
        out_ready, out_stored = sem("out_ready"), sem("out_stored")
        act_own, dve_own, pool_own = sem("act_own"), sem("dve_own"), sem("pool_own")

        def quad(buf, j, n):
            return buf[:, j, :].rearrange("p (c n) -> p c n", c=4)[:, :, 0:n]

        def col(name, k):
            return cols[:, bass.ds(k + COLS[name][0], 1)]

        def landed(unit):
            return 16 * (unit + 1 - (unit > U_ODD))

        def chunk(a, k):
            return a[:, bass.ds(k, 1), :].rearrange("p c t -> p (c t)")

        def sq_count(n):
            return n + 1 - (n > N_Y)

        def t_idx(n):
            return TRANSPOSED.index(n)

        rows3 = lambda w: w.rearrange("(c p) n -> p c n", p=P)
        w_ssd, w_kv, w_q = rows3(I["ssd_w_in"][0]), rows3(I["xa_w_kv"][0]), rows3(I["xa_w_q"][0])
        w_up = {1: rows3(I["ffn_w_up"][0]), 2: rows3(I["w_up_2"][0])}
        w_in2 = rows3(I["w_in_2"][0])
        down_w = {"wout": rows3(I["ssd_w_out"][0]), "xo": rows3(I["xa_w_o"][0]), "dn1": rows3(I["ffn_w_down"][0]),
                  "wo2": rows3(I["w_o_2"][0]), "dn2": rows3(I["w_down_2"][0])}
        DOWN = {"wout": (U_WOUT, X_WOUT, DI // P // 4, bigc), "xo": (U_XO, X_XO, 1, xa_oT),
                "dn1": (U_DN1, X_DN1, FC // 4, bigc), "wo2": (U_WO2, X_WO2, KC // 4, mixT),
                "dn2": (U_DN2, X_DN2, FC // 4, bigc)}
        FFN = {1: (U_UP1, E_UP1, TB["up1"], "ffn_conv_w", "ffn_conv_b"),
               2: (U_UP2, E_UP2, TB["up2"], "conv_w_2", "conv_b_2")}
        tokens = lambda a: a.rearrange("(a p) n -> p a n", p=P)

        block = ctx.enter_context(nc.Block())

        @block.sync
        def _(sp):
            def load_up(q, w, c0, n, first=False):
                for j in range(4):
                    if not first:
                        sp.wait_ge(lo_ready, q - 3 + j)
                    sp.dma_start(quad(raw, j, n), w[:, 4 * j:4 * j + 4, bass.ds(c0, n)]).then_inc(raw_landed[j], 16)

            def load_down(name):
                unit, _, n, _ = DOWN[name]

                def rows(q, chunk):
                    for j in range(4):
                        sp.wait_ge(lo_ready, q - 3 + j)
                        sp.dma_start(raw[:, j, :], down_w[name][:, bass.ds(chunk + j, 1), :].rearrange("p c n -> p (c n)"))\
                            .then_inc(raw_landed[j], 16)

                if n == 1:
                    rows(4 * unit, 0)
                else:
                    with nc.sync.Fori(0, n) as i:
                        rows(i * 4 + 4 * unit, i * 4)

            def load_ffn(n):
                unit = FFN[n][0]
                with nc.sync.Fori(0, FB) as i:
                    load_up(i * 8 + 4 * unit, w_up[n], i * BLK, BLK)
                    load_up(i * 8 + 4 * (unit + 1), w_up[n], i * BLK + F, BLK)

            sp.dma_start(xn_big, tokens(I["mem"][0])).then_inc(mem_landed, 16)
            load_up(0, w_kv, 0, BLK, first=True)
            sp.dma_start(xt, tokens(I["x"][0])).then_inc(x_landed, 16)
            load_up(4, w_kv, XW, BLK)
            load_up(4 * U_DT, w_ssd, DT_COL, HEADS)
            with nc.sync.Fori(1, GROUPS + 1) as g1:
                q = g1 * 12 + (4 * U_SSD - 12)
                for j in range(4):
                    sp.wait_ge(lo_ready, q - 3 + j)
                    for k in range(2):
                        sp.dma_start(quad(raw, j, 2 * NST)[:, :, k * NST:(k + 1) * NST],
                                     w_ssd[:, 4 * j:4 * j + 4, bass.ds(g1 * NST + ((B_COL, C_COL)[k] - NST), NST)])\
                            .then_inc((raw_landed, c_landed)[k][j], 16)
                load_up(q + 4, w_ssd, g1 * BLK + (XS_COL - BLK), BLK)
                load_up(q + 8, w_ssd, g1 * BLK + (-BLK), BLK)
            load_down("wout")
            load_up(4 * U_XQ, w_q, 0, XW)
            load_down("xo")
            load_ffn(1)
            load_down("dn1")
            for k in range(2):
                load_up(4 * (U_IN2 + 2 * k), w_in2, k * BLK, BLK)
                load_up(4 * (U_IN2 + 2 * k + 1), w_in2, AIQ + k * BLK, BLK)
            for j in range(4):
                sp.wait_ge(lo_ready, 4 * U_ODD - 3 + j)
                for c0, n, at in ((AKV, RANK, 0), (AIK, ID + IH, RANK), (BF, BH, RANK + ID + IH)):
                    sp.dma_start(quad(raw, j, ODD)[:, :, at:at + n], w_in2[:, 4 * j:4 * j + 4, c0:c0 + n])\
                        .then_inc(odd_landed[j], 16)
            for k in range(2):
                for m, c0 in enumerate((BQ, BK, BV)):
                    load_up(4 * (U_B + 3 * k + m), w_in2, c0 + k * BLK, BLK)
            load_down("wo2")
            load_ffn(2)
            load_down("dn2")
            sp.wait_ge(out_ready, TT)
            sp.dma_start(tokens(out[0]), tmp_big).then_inc(out_stored, 16)
            sp.wait_ge(out_stored, 16)

        @block.gpsimd
        def _(pool):
            nc.gpsimd.memset(ident[:, :], 0.0).then_inc(pool_own, 1)
            nc.gpsimd.memset(ones[:, :], 1.0).then_inc(pool_own, 1)
            nc.gpsimd.memset(half[:, :], -0.5).then_inc(pool_own, 1)
            pool.wait_ge(pool_own, 3)
            nc.gpsimd.affine_select(out=ident[:, :], in_=ident[:, :], compare_op=ALU.not_equal, fill=1.0, base=0,
                                    pattern=[[-1, P]], channel_multiplier=1).then_inc(consts_ready, 1)
            nc.gpsimd.affine_select(out=triu[:, :], in_=ones[:, :], compare_op=ALU.is_ge, fill=0.0, base=0,
                                    pattern=[[1, P]], channel_multiplier=-1).then_inc(consts_ready, 1)

            for name, (r0, n) in COLS.items():
                a = I[name]
                flat = a.rearrange("a b (c f) -> (a b c) f", f=P) if len(a.shape) == 3 \
                    else a.rearrange("a (c f) -> (a c) f", f=P)
                r = r0
                while r < r0 + n:
                    k = min(r0 + n - r, P - r % P)
                    pool.dma_start(rows[r % P:r % P + k, r // P, :], flat[r - r0:r - r0 + k, :]).then_inc(rows_landed, 16)
                    r += k
            for dst, name in ((dt_bias, "ssd_dt_bias"), (a_log, "ssd_a_log"), (d_skip, "ssd_d")):
                pool.dma_start(dst, I[name][0].partition_broadcast(P)).then_inc(small_landed, 16)

            def inverse_root(n):
                pool.wait_ge(ms_done, n + 1)
                nc.gpsimd.tensor_tensor(rstd(n), ssq(n), half[:, :], ALU.pow).then_inc(rstd_done, 1)

            def load_gain(src):
                pool.dma_start(u[:, :], src.partition_broadcast(P)).then_inc(gain_landed, 16)

            inverse_root(N_MEM)
            pool.wait_ge(kT_copied, 1)
            pool.wait_ge(proj_evac, E_KV + 1)
            pool.dma_start(kT_d, vb[:, :]).then_inc(kv_stored, 16)
            pool.dma_start(v_d, u[:, 1024:2048]).then_inc(kv_stored, 16)
            inverse_root(N_X)
            pool.wait_ge(acsT_ready, 1)
            pool.dma_start(acsT_d, acsT).then_inc(acsT_stored, 16)
            pool.wait_ge(acsT_stored, 16)

            def exponents(g):
                pool.dma_start(ssd_m, bass.AP(acsT_d.tensor, g * (HPG * L), [[0, P], [L, HPG], [1, L]]))\
                    .then_inc(acs_landed, 16)
                pool.wait_ge(acs_landed, g * 16 + 16)
                for c in range(TT):
                    e = ssd_m[:, :, c * P:(c + 1) * P]
                    at_s = acs[:, c, bass.ds(g * HPG, HPG)].unsqueeze(2).broadcast_to([P, HPG, P])
                    ins = nc.gpsimd.tensor_tensor(e, e, at_s, ALU.subtract)
                ins.then_inc(diff_made, 1)
                pool.wait_ge(diff_made, g + 1)
                nc.gpsimd.tensor_tensor(idle[:, 0:1], half[:, 0:1], half[:, 1:2], ALU.add)
                nc.gpsimd.tensor_scalar(x[:, 0:2048], x[:, 0:2048], 0.0, None, ALU.min).then_inc(diff_ready, 1)

            exponents(0)
            with nc.gpsimd.Fori(0, GROUPS - 1) as i:
                pool.wait_ge(tf[3], i * 2 + (TB["ssd"][3] + 1))
                nc.gpsimd.tensor_tensor(idle[:, 0:1], half[:, 0:1], half[:, 1:2], ALU.add)
                exponents(i + 1)

            inverse_root(N_Y)
            pool.wait_ge(te[3], TB["ssd"][3] + 2 * GROUPS)
            pool.dma_start(xt, tokens(I["x"][0])).then_inc(x_back, 16)
            load_gain(I["norm_post"][0, 0])
            inverse_root(N_P1)
            inverse_root(N_H1)
            pool.wait_ge(kv_stored, 32)
            pool.wait_ge(x_new, TT)
            pool.dma_start(big[:, 4096:5120], kT_d).then_inc(kv_loaded, 16)
            pool.dma_start(big[:, 5120:6144], v_d).then_inc(kv_loaded, 16)
            pool.wait_ge(pv_done, XH)
            load_gain(I["norm_post"][0, 1])
            inverse_root(N_P2)
            inverse_root(N_H2)
            pool.wait_ge(tf[3], TB["up1"][3] + FB)
            load_gain(I["norm_post"][0, 2])
            inverse_root(N_P3)
            pool.wait_ge(x_new, 3 * TT)
            pool.dma_start(x_d, x[:, :]).then_inc(x_spilled, 16)
            inverse_root(N_1)
            pool.wait_ge(x_spilled, 16)
            pool.wait_ge(xn_ready, t_idx(N_1) + 1)
            for dst, src in ((onehot, I["bucket_onehot"]), (table, I["t5_table_2"]),
                             (kv_gain, I["kv_norm_g_2"][0].partition_broadcast(P)),
                             (fg_bias, I["fgate_b_2"][0].partition_broadcast(P))):
                pool.dma_start(dst, src).then_inc(m2_landed, 16)
            nc.gpsimd.memset(anti, 0.0).then_inc(pool_own, 1)
            nc.gpsimd.memset(vb[:, 0:512], 0.0).then_inc(pool_own, 1)
            pool.wait_ge(pool_own, 5)
            nc.gpsimd.affine_select(out=anti, in_=anti, compare_op=ALU.not_equal, fill=1.0, base=-(P - 1),
                                    pattern=[[1, P]], channel_multiplier=1).then_inc(m2_consts, 1)
            nc.gpsimd.affine_select(out=mask, in_=mask, compare_op=ALU.is_ge, fill=NEG, base=0,
                                    pattern=[[P, TT], [-1, L]], channel_multiplier=1).then_inc(m2_consts, 1)
            inverse_root(N_CKV)
            pool.wait_ge(line_ready, 1)
            pool.dma_start(line_d, line).then_inc(line_stored, 16)
            pool.wait_ge(te[2], TB["in2"][2] + 5)
            pool.wait_ge(te[3], TB["in2"][3] + 4)
            pool.wait_ge(te[1], TB["in2"][1] + 5)
            pool.dma_start(w_uk, I["w_uk_2"][0].rearrange("h d r -> d h r")).then_inc(uk_landed, 16)
            pool.wait_ge(line_stored, 16)
            pool.wait_ge(quad_used, 4 * U_WO2)
            pool.dma_start(skew, bass.AP(line_d.tensor, 0, [[1, P], [BLK, AH], [1, L + P]])).then_inc(skew_landed, 16)
            for b in range(4):
                pool.wait_ge(tf[b], TB["qlat"][b] + 2)
            pool.dma_start(w_uv, I["w_uv_2"][0].rearrange("h (c p) d -> p h c d", p=P)).then_inc(uv_landed, 16)
            pool.wait_ge(decay_sum_ready, 1)
            for h in range(BH):
                if h:
                    b = (h - 1) % 2
                    pool.wait_ge(tf[b], TB["fox"][b] + (h - 1) // 2 + 1)
                nc.gpsimd.tensor_scalar(cum_row, cumT, ident[0:BH, h:h + 1], None, ALU.mult).then_inc(cum_row_ready, 1)
            pool.wait_ge(uv_done, AH)
            pool.dma_start(xn_big, x_d.rearrange("p (a n) -> p a n", a=TT)).then_inc(x_back, 16)
            inverse_root(N_2)
            pool.wait_ge(tf[3], TB["up2"][3] + FB)
            load_gain(I["final_g_2"])
            inverse_root(N_FIN)

        @block.scalar
        def _(act):
            def hi(q, land, j, n=4 * BLK, land_sem=None, first=False):
                act.wait_ge(land_sem or raw_landed[j], land)
                if not first:
                    act.wait_ge(quad_used, q - 3 + j)
                dst, src = (w_hi[:, j, :], raw[:, j, :]) if n == 4 * BLK else (quad(w_hi, j, n), quad(raw, j, n))
                nc.scalar.activation(dst, src, ACT.Copy).then_inc(hi_ready, 1)

            def hi_unit(unit, n=4 * BLK, js=range(4), first=False):
                for j in js:
                    hi(4 * unit, landed(unit), j, n, None, first)

            def hi_bc(g, j):
                act.wait_ge(c_landed[j], g * 16 + 16)
                hi(g * 12 + 4 * U_SSD, g * 48 + landed(U_SSD), j, 2 * NST)

            def evac(q, pair, dst, n=BLK, func=ACT.Copy, scale=1.0):
                act.wait_ge(quad_used, q + 4)
                for tt in range(TT):
                    ins = nc.scalar.activation(dst[:, tt, 0:n], PB[2 * pair + tt][:, 0:n], func, scale=scale)
                ins.then_inc(proj_evac, 1)

            def square(n, src, scratch):
                for tt in range(TT):
                    ins = nc.scalar.activation(scratch(tt), src[:, tt, :], ACT.Square, accum_out=ssq(n)[:, tt:tt + 1])
                ins.then_inc(sq_done, 1)

            def normalise(n, src, dst, gain, k0, next_unit):
                act.wait_ge(sq_done, sq_count(n))
                act.wait_ge(rstd_done, n + 1)
                for tt in range(TT):
                    ins = nc.scalar.activation(dst[:, tt, :], src[:, tt, :], ACT.Copy, scale=rstd(n)[:, tt:tt + 1])
                ins.then_inc(xn_ready, 1)
                act.wait_ge(quad_used, 4 * next_unit)
                for m in range(KC // 2):
                    act.wait_ge(tf[m % 4], TB[n][m % 4] + m // 4 + 1)
                    for c in range(2):
                        k = 2 * m + c
                        ins = nc.scalar.activation(hT_hi[:, k, :], T2[m % 4][:, c, :], ACT.Copy, scale=col(gain, k0 + k))
                    ins.then_inc(h_hi_done, 1)

            def down(name, ready):
                unit, _, n, src = DOWN[name]
                act.wait_ge(quad_used, 4 * unit)
                for j in range(4):
                    ready(j)
                    nc.scalar.activation(hT_hi[:, j, :], src[:, j, :], ACT.Copy).then_inc(xs_hi, 1)
                if n > 1:
                    with nc.scalar.Fori(0, n - 1) as i:
                        for j in range(4):
                            hi(i * 4 + 4 * (unit + 1), i * 16 + landed(unit + 1), j)
                            nc.scalar.activation(hT_hi[:, j, :], chunk(src, i * 4 + (4 + j)), ACT.Copy).then_inc(xs_hi, 1)

            def square_parts(last_unit):
                act.wait_ge(quad_used, 4 * last_unit + 4)
                for tt in range(TT):
                    for nb in range(NB):
                        k = tt * NB + nb
                        ins = nc.scalar.activation(big[:, k * BLK:(k + 1) * BLK], acc[tt][nb][:, :], ACT.Square,
                                                   accum_out=ssq_parts[:, k:k + 1])
                ins.then_inc(sq_done, 1)

            def after_down(unit, n, k, parts=True, scratch=xn_big):
                hi_unit(unit, js=(0, 1, 2))
                if parts:
                    square_parts(unit - 1)
                act.wait_ge(x_new, TT * k)
                square(n, xt, lambda tt: scratch[:, tt, :])
                hi_unit(unit, js=(3,))

            hi_unit(0, first=True)
            act.wait_ge(mem_landed, 16)
            square(N_MEM, xn_big, lambda tt: (u[:, :], tmp_big[:, 1, :])[tt])
            act.wait_ge(cols_ready, 1)
            normalise(N_MEM, xn_big, xn_big, "norm_mem", 0, 0)
            hi_unit(1)
            evac(0, 0, u2[:, 0])
            hi_unit(U_DT, HEADS)
            act.wait_ge(x_landed, 16)
            square(N_X, xt, lambda tt: xn_big[:, tt, :])
            evac(4, 1, u2[:, 1])
            normalise(N_X, xt, xn_big, "norm_pre", 0, U_DT)
            for j in range(4):
                hi_bc(0, j)
            evac(4 * U_DT, 0, sp_tmp[0].rearrange("p (a h) -> p a h", a=TT), HEADS)
            act.wait_ge(small_landed, 48)
            nc.scalar.activation(a_log, a_log, ACT.Exp).then_inc(exp_done, 1)
            act.wait_ge(exp_asked, 1)
            nc.scalar.activation(sp_tmp[2], sp_tmp[2], ACT.Exp).then_inc(exp_done, 1)
            tb = TB["ssd"]

            def decays(g):
                act.wait_ge(diff_ready, g + 1)
                nc.scalar.activation(x[:, 0:2048], x[:, 0:2048], ACT.Exp).then_inc(decay_ready, 1)

            def states_out(uses):
                act.wait_ge(tf[0], uses)
                nc.scalar.activation(states, T[0][:, :], ACT.Copy).then_inc(te[0], 1)

            def y_out(g, after):
                for b in range(2):
                    act.wait_ge(tf[2 + b], after * 2 + tb[2 + b])
                    for c in range(2):
                        k = g * 4 + (2 * b + c)
                        ins = nc.scalar.activation(chunk(bigc, k), T2[2 + b][:, c, :], ACT.Copy, scale=col("ssd_norm_g", k))
                    ins.then_inc(te[2 + b], 1)

            def group(g, prev, nxt):
                q = g * 12 + 4 * U_SSD
                land = lambda k: g * 48 + landed(U_SSD + k)

                def hi_next(j):
                    if nxt:
                        hi_bc(g + 1, j)
                    else:
                        hi(4 * U_WOUT, landed(U_WOUT), j)

                for j in range(4):
                    hi(q + 4, land(1), j)
                evac(q, 0, u_bc, 2 * NST)
                if prev:
                    states_out(g * 4 + tb[0])
                else:
                    act.wait_ge(exp_asked, 2)
                    nc.scalar.activation(dte, dte, ACT.Exp).then_inc(exp_done, 1)
                    nc.scalar.activation(eacs, acs[:, 1, :], ACT.Exp).then_inc(exp_done, 1)
                for j in range(2):
                    hi(q + 8, land(2), j)
                act.wait_ge(tf[0], g * 4 + (tb[0] + 1))
                if prev:
                    act.wait_ge(tf[1], g * 4 + tb[1])
                for k in range(2):
                    c = g + (32 + 8 * k)
                    ins = nc.scalar.activation(bc[:, k, :], T2[0][:, k, :], ACT.Identity, bias=col("ssd_conv_b", c),
                                               scale=col("ssd_conv_w", c + (SSD_TAPS - 1) * CONV_CH))
                ins.then_inc(bc_tap, 1)
                hi(q + 8, land(2), 2)
                act.wait_ge(te[0], g * 4 + (tb[0] + 1))
                nc.scalar.activation(big[:, 10240:10752], big[:, 10240:10752], ACT.Silu).then_inc(bc_ready, 1)
                if prev:
                    y_out(g - 1, g)
                hi(q + 8, land(2), 3)
                evac(q + 4, 1, u_xs)
                hi_next(0)
                decays(g)
                hi_next(1)
                for b in range(2):
                    act.wait_ge(tf[b], g * 4 + (tb[b] + 2))
                for k in range(4):
                    c = g * 4 + k
                    ins = nc.scalar.activation(xc[:, k, :], T2[k // 2][:, k % 2, :], ACT.Identity, bias=col("ssd_conv_b", c),
                                               scale=col("ssd_conv_w", c + (SSD_TAPS - 1) * CONV_CH))
                ins.then_inc(xs_tap, 1)
                hi_next(2)
                act.wait_ge(te[1], g * 4 + (tb[1] + 2))
                nc.scalar.activation(big[:, 9216:10240], big[:, 9216:10240], ACT.Silu).then_inc(xc_ready, 1)
                hi_next(3)
                evac(q + 8, 0, zs, BLK, ACT.Silu)

            act.wait_ge(kv_stored, 32)
            group(0, False, True)
            with nc.scalar.Fori(0, GROUPS - 2) as i:
                group(i + 1, True, True)
            group(GROUPS - 1, True, False)
            states_out(GROUPS * 4 + tb[0])
            y_out(GROUPS - 1, GROUPS)
            down("wout", lambda j: act.wait_ge(te[3], tb[3] + 2 * GROUPS))
            after_down(U_XQ, N_H1, 1)
            normalise(N_H1, xt, xn_big, "norm_pre", KC, U_XQ)

            hi_unit(U_XO)
            evac(4 * U_XQ, 0, u2[:, 0], XW, ACT.Copy, SCALE)

            def exps(k, src, then):
                par = k % 2
                for tt in range(TT):
                    ins = nc.scalar.activation(prob[par][:, tt, :], src(tt), ACT.Exp,
                                               bias=mx[:, 2 * par + tt:2 * par + tt + 1],
                                               accum_out=den[:, 2 * par + tt:2 * par + tt + 1])
                ins.then_inc(then, 1)

            def prob_out(h, name, pv0):
                b = 2 + h % 2
                act.wait_ge(tf[b], TB[name][b] + h // 2 + 1)
                if h >= 2:
                    act.wait_ge(pv_done, pv0 + h - 1)
                nc.scalar.activation(probT[h % 2], T2[b], ACT.Copy).then_inc(te[b], 1)

            for h in range(XH + 1):
                if h < XH:
                    act.wait_ge(s_max, h + 1)
                    if h < 2:
                        act.wait_ge(tf[1], TB["xa"][1] + 1)
                    else:
                        act.wait_ge(tf[2 + h % 2], TB["xa"][2 + h % 2] + h // 2)
                    exps(h, lambda tt: T2[h % 2][:, tt, :], te[h % 2])
                if h >= 1:
                    prob_out(h - 1, "xa", 0)
            down("xo", lambda j: act.wait_ge(pv_taken, j + 1))
            after_down(U_UP1, N_H2, 2)
            normalise(N_H2, xt, xn_big, "norm_pre", 2 * KC, U_UP1)

            def ffn(n, down_name):
                unit, _, tb, cw, cb = FFN[n]
                m0 = (n - 1) * FB

                def gate_conv(i):
                    for b in range(2):
                        act.wait_ge(tf[b], i + (tb[b] + 1))
                    for k in range(4):
                        c = i * 4 + k
                        ins = nc.scalar.activation(chunk(bigc, c), T2[k // 2][:, k % 2, :], ACT.Identity, bias=col(cb, c),
                                                   scale=col(cw, c + (FFN_TAPS - 1) * 2 * FC))
                    ins.then_inc(gate_tap, 1)

                def gate_silu(i):
                    for b in range(2):
                        act.wait_ge(te[b], i + (tb[b] + 1))
                    g = big[:, bass.ds(i * (4 * L), 4 * L)]
                    nc.scalar.activation(g, g, ACT.Silu).then_inc(gate_act, 1)

                def val_conv(i, first):
                    for b in range(2, 4):
                        act.wait_ge(tf[b], i + (tb[b] + 1))
                    if not first:
                        act.wait_ge(ffn_mul, i + m0)
                    for k in range(4):
                        c = i * 4 + (k + FC)
                        ins = nc.scalar.activation(vbc[:, k, :], T2[2 + k // 2][:, k % 2, :], ACT.Identity, bias=col(cb, c),
                                                   scale=col(cw, c + (FFN_TAPS - 1) * 2 * FC))
                    ins.then_inc(val_tap, 1)

                def pair(i, prev, val_first=False):
                    q, land = i * 8 + 4 * unit, i * 32 + landed(unit)
                    for j in range(2):
                        hi(q + 4, land + 16, j)
                    if prev:
                        val_conv(i - 1, val_first)
                    for j in range(2, 4):
                        hi(q + 4, land + 16, j)
                    evac(q, 0, u2[:, 0])
                    for j in range(2):
                        hi(q + 8, land + 32, j)
                    gate_conv(i)
                    hi(q + 8, land + 32, 2)
                    gate_silu(i)
                    hi(q + 8, land + 32, 3)
                    evac(q + 4, 1, u2[:, 1])

                pair(0, False)
                pair(1, True, True)
                with nc.scalar.Fori(0, FB - 2) as i:
                    pair(i + 2, True)
                val_conv(FB - 1, False)
                down(down_name, lambda j: act.wait_ge(ffn_mul, m0 + 1))

            ffn(1, "dn1")
            after_down(U_IN2, N_1, 3)
            normalise(N_1, xt, xn_big, "norm1_g_2", 0, U_IN2)

            units = IN2_UNITS
            for k, (unit, kind, half_) in enumerate(units):
                if k + 1 < len(units) and units[k + 1][0] == U_ODD:
                    for j in range(4):
                        hi(4 * U_ODD, 48, j, ODD, odd_landed[j])
                else:
                    hi_unit(unit + 1)
                pr = k % 2
                if kind in IN2_SLOT:
                    s, turn = IN2_SLOT[kind], IN2_TURN[kind] + half_
                    if turn:
                        act.wait_ge(tf[2 * s + 1], TB["in2"][2 * s + 1] + IN2_USE[kind][1] + half_)
                    evac(4 * unit, pr, u2[:, s])
                elif kind == "odd":
                    act.wait_ge(m2_landed, 64)
                    evac(4 * unit, pr, odd, ODD)
                    act.wait_ge(proj_evac, E_ODD)
                    for tt in range(TT):
                        ins = nc.scalar.activation(x[:, 3072 + RANK * tt:3072 + RANK * (tt + 1)], odd[:, tt, 0:RANK], ACT.Square,
                                                   accum_out=ssq(N_CKV)[:, tt:tt + 1])
                    ins.then_inc(sq_done, 1)
                    act.wait_ge(exp_asked, 3)
                    nc.scalar.activation(fox_tmp[2], fox_tmp[2], ACT.Exp).then_inc(exp_done, 1)
                else:
                    evac(4 * unit, pr, bv[:, :, half_ * BLK:(half_ + 1) * BLK])

            for h in range(AH):
                b = h % 4
                act.wait_ge(tf[b], TB["qlat"][b] + h // 4 + 1)
                nc.scalar.activation(qlT[:, h], T2[b], ACT.Copy).then_inc(te[b], 1)
            for n in range(IH):
                b = n % 4
                act.wait_ge(tf[b], TB["idx"][b] + n // 4 + 1)
                if n >= 4:
                    act.wait_ge(relu_used, n - 3)
                nc.scalar.activation(rl[b], T2[b], ACT.Relu, scale=float(ID) ** -0.5).then_inc(te[b], 1)
            for name, k0 in (("fox", 0), ("dsa", BH)):
                for h in range(AH + 1):
                    if h < AH:
                        act.wait_ge(s_max, XH + k0 + h + 1)
                        exps(k0 + h, lambda tt: prob[h % 2][:, tt, :], p_exp)
                    if h >= 1:
                        prob_out(h - 1, name, XH + k0)
            down("wo2", lambda j: act.wait_ge(uv_taken, AH))
            after_down(U_UP2, N_2, 4, False, tmp_big)
            normalise(N_2, xt, xn_big, "norm2_g_2", 0, U_UP2)
            ffn(2, "dn2")
            act.wait_ge(x_new, 5 * TT)
            square(N_FIN, xt, lambda tt: xn_big[:, tt, :])

        @block.tensor
        def _(pe):
            def bank_free(b, uses):
                if not isinstance(uses, int) or uses:
                    pe.wait_ge(te[b], uses)

            def up(q, pair, n, evac_before, after=None):
                for j in range(4):
                    if j == 0 and evac_before is not None:
                        pe.wait_ge(proj_evac, evac_before)
                    pe.wait_ge(lo_ready, q + j + 1)
                    wh, wl = quad(w_hi, j, n), quad(w_lo, j, n)
                    for c in range(4):
                        k = 4 * j + c
                        for tt in range(TT):
                            o = PB[2 * pair + tt][:, 0:n]
                            h, l = (t[:, k, tt * P:(tt + 1) * P] for t in (hT_hi, hT_lo))
                            nc.tensor.matmul(o, h, wh[:, c, :], start=(k == 0), stop=False)
                            nc.tensor.matmul(o, h, wl[:, c, :], start=False, stop=False)
                            ins = nc.tensor.matmul(o, l, wh[:, c, :], start=False, stop=(k == KC - 1))
                    ins.then_inc(quad_used, 1)
                    if after and j in after:
                        after[j]()

            def down(name, ready):
                unit, xi, n, _ = DOWN[name]
                ready()

                def rows(q, xq, first, last):
                    for j in range(4):
                        pe.wait_ge(xs_lo, xq + j + 1)
                        pe.wait_ge(lo_ready, q + j + 1)
                        for tt in range(TT):
                            h, l = (t[:, j, tt * P:(tt + 1) * P] for t in (hT_hi, hT_lo))
                            for a, w in ((h, w_hi), (h, w_lo), (l, w_hi)):
                                for nb in range(NB):
                                    ins = nc.tensor.matmul(acc[tt][nb][:, :], a, w[:, j, nb * BLK:(nb + 1) * BLK],
                                                           start=(first and j == 0 and a is h and w is w_hi),
                                                           stop=(last and j == 3 and a is l))
                        ins.then_inc(quad_used, 1)

                if n == 1:
                    rows(4 * unit, xi, True, True)
                else:
                    rows(4 * unit, xi, True, False)
                    with nc.tensor.Fori(0, n - 2) as i:
                        rows(i * 4 + 4 * (unit + 1), i * 4 + (xi + 4), False, False)
                    rows(4 * (unit + n - 1), xi + 4 * (n - 1), False, True)

            def banks_free(phase):
                for b in range(4):
                    bank_free(b, TB[phase][b])

            def norm_transposes(n, src):
                pe.wait_ge(xn_ready, t_idx(n) + 1)
                for m in range(KC // 2):
                    b = m % 4
                    bank_free(b, TB[n][b] + m // 4)
                    for c in range(2):
                        for tt in range(TT):
                            ins = nc.tensor.transpose(T2[b][:, c, tt * P:(tt + 1) * P],
                                                      src[:, tt, (2 * m + c) * P:(2 * m + c + 1) * P], ident[:, :])
                    ins.then_inc(tf[b], 1)
                for b in range(4):
                    pe.wait_ge(te[b], TB[n][b] + 2)

            def turn_block(b0, uses, stage):
                for b in range(2):
                    bank_free(b0 + b, uses[b])
                    for c in range(2):
                        for tt in range(TT):
                            ins = nc.tensor.transpose(T2[b0 + b][:, c, tt * P:(tt + 1) * P],
                                                      stage[:, tt, (2 * b + c) * P:(2 * b + c + 1) * P], ident[:, :])
                    ins.then_inc(tf[b0 + b], 1)

            pe.wait_ge(consts_ready, 2)
            pe.wait_ge(rows_landed, 16 * N_ROW_LOADS)
            for r in range(NROWT):
                k = min(P, NCOL - r * P)
                ins = nc.tensor.transpose(T[r // 4][:, (r % 4) * P:(r % 4) * P + k], rows[0:k, r, :], ident[0:k, 0:k])
                if r % 4 == 3 or r == NROWT - 1:
                    ins.then_inc(tf[r // 4], 1)
            norm_transposes(N_MEM, xn_big)

            def turn_keys():
                pe.wait_ge(proj_evac, E_KV)
                turn_block(0, TB["kv"], u2[:, 0])

            up(0, 0, BLK, None)
            up(4, 1, BLK, None, {1: turn_keys})
            norm_transposes(N_X, xn_big)
            up(4 * U_DT, 0, HEADS, E_KV)
            tb = TB["ssd"]

            def cumulative_sums():
                pe.wait_ge(da_ready, 1)
                bank_free(2, TB["dt"][2])
                for c in range(TT):
                    nc.tensor.matmul(T[2][:, c * HEADS:(c + 1) * HEADS], triu[:, :], da[:, c, :], start=True, stop=True)
                nc.tensor.matmul(T[2][:, TT * HEADS:(TT + 1) * HEADS], ones[:, :], da[:, 0, :], start=True, stop=True)\
                    .then_inc(tf[2], 1)
                bank_free(3, TB["dt"][3])
                for c in range(TT):
                    ins = nc.tensor.matmul(T[3][0:HEADS, c * P:(c + 1) * P], da[:, c, :], triu[:, :], start=True, stop=True)
                ins.then_inc(tf[3], 1)

            def turn_bc(g):
                pe.wait_ge(proj_evac, g * 3 + E_SSD)
                bank_free(0, g * 4 + tb[0])
                for k in range(2):
                    for tt in range(TT):
                        ins = nc.tensor.transpose(T2[0][:, k, tt * P:(tt + 1) * P], u_bc[:, tt, k * NST:(k + 1) * NST], ident[:, :])
                ins.then_inc(tf[0], 1)

            def cb_products(g):
                pe.wait_ge(bc_ready, g + 1)
                bank_free(1, g * 4 + tb[1])
                for c in range(TT):
                    nc.tensor.matmul(T[1][:, c * P:(c + 1) * P], bc[:, 0, c * P:(c + 1) * P], bc[:, 1, c * P:(c + 1) * P],
                                     start=True, stop=True)
                nc.tensor.transpose(T[1][:, TT * P:(TT + 1) * P], bc[:, 0, 0:P], ident[:, :]).then_inc(tf[1], 1)

            def turn_xs(g):
                pe.wait_ge(proj_evac, g * 3 + (E_SSD + 1))
                turn_block(0, [g * 4 + (tb[b] + 1) for b in range(2)], u_xs)

            def back_xs(g):
                pe.wait_ge(xc_ready, g + 1)
                for tt in range(TT):
                    bank_free(tt, g * 4 + (tb[tt] + 2))
                    for k in range(4):
                        ins = nc.tensor.transpose(T[tt][:, k * P:(k + 1) * P], xc[:, k, tt * P:(tt + 1) * P], ident[:, :])
                    ins.then_inc(tf[tt], 1)

            def states_and_diagonal(g):
                pe.wait_ge(bd_ready, g + 1)
                bank_free(0, g * 4 + (tb[0] + 3))
                nc.tensor.matmul(T[0][:, :], bm, bd, start=True, stop=True).then_inc(tf[0], 1)
                pe.wait_ge(m_ready, g + 1)
                for c in range(TT):
                    bank_free(2 + c, g * 2 + tb[2 + c])
                    for h in range(HPG):
                        ins = nc.tensor.matmul(T[2 + c][:, h * HD:(h + 1) * HD], ssd_m[:, h, c * P:(c + 1) * P],
                                               xdt[:, c, h * HD:(h + 1) * HD], start=True, stop=True)
                    ins.then_inc(tf[2 + c], 1)

            def from_states(g):
                pe.wait_ge(te[0], g * 4 + (tb[0] + 4))
                bank_free(1, g * 4 + (tb[1] + 3))
                nc.tensor.matmul(T[1][:, :], bc[:, 1, P:2 * P], states, start=True, stop=True).then_inc(tf[1], 1)

            def turn_y(g):
                pe.wait_ge(yg_ready, g + 1)
                turn_block(2, [g * 2 + (tb[2 + b] + 1) for b in range(2)], yg)

            def group(g, prev):
                q = g * 12 + 4 * U_SSD
                late = (lambda f: lambda: f(g - 1)) if prev else (lambda f: lambda: None)
                up(q, 0, 2 * NST, g * 3 + (E_SSD - 1), {1: late(back_xs), 3: late(states_and_diagonal)})
                if not prev:
                    cumulative_sums()
                up(q + 4, 1, BLK, g * 3 + (E_SSD - 2), {0: late(from_states), 1: lambda: turn_bc(g), 2: late(turn_y)})
                up(q + 8, 0, BLK, g * 3 + E_SSD, {0: lambda: cb_products(g), 1: lambda: turn_xs(g)})

            group(0, False)
            with nc.tensor.Fori(0, GROUPS - 1) as i:
                group(i + 1, True)
            last = GROUPS - 1
            back_xs(last)
            states_and_diagonal(last)
            from_states(last)
            turn_y(last)

            def after_ssd():
                pe.wait_ge(proj_evac, E_SSD + 3 * GROUPS - 1)
                banks_free(N_H1)

            down("wout", after_ssd)
            norm_transposes(N_H1, xn_big)
            up(4 * U_XQ, 0, XW, None)
            pe.wait_ge(proj_evac, E_XQ)
            turn_block(0, TB["xa"], u2[:, 0])
            pe.wait_ge(kv_loaded, 32)

            def turn_probs(h, name, k):
                b = 2 + h % 2
                pe.wait_ge(p_ready, k + 1)
                bank_free(b, TB[name][b] + h // 2)
                for s in range(2):
                    for tt in range(TT):
                        ins = nc.tensor.transpose(T2[b][:, s, tt * P:(tt + 1) * P], prob[h % 2][:, tt, s * P:(s + 1) * P], ident[:, :])
                ins.then_inc(tf[b], 1)

            def weighted(h, name, k, vals, parts=1):
                pe.wait_ge(te[2 + h % 2], TB[name][2 + h % 2] + h // 2 + 1)
                if h >= 2:
                    pe.wait_ge(pv_taken, k - 1)
                for r in range(parts):
                    for s in range(2):
                        ins = nc.tensor.matmul(PB[h % 2][:, r * L:(r + 1) * L], vals(s, r), probT[h % 2][:, s, :],
                                               start=(s == 0), stop=(s == 1))
                ins.then_inc(pv_done, 1)

            for b in range(2):
                pe.wait_ge(te[b], TB["xa"][b] + 1)
            for h in range(XH + 2):
                if h < XH:
                    b = h % 2
                    bank_free(b, TB["xa"][b] + 1 + h // 2)
                    for tt in range(TT):
                        ins = nc.tensor.matmul(T2[b][:, tt, :], xa_qT[:, h, tt * P:(tt + 1) * P], xa_kT[:, h, :], start=True, stop=True)
                    ins.then_inc(tf[b], 1)
                if 1 <= h <= XH:
                    turn_probs(h - 1, "xa", h - 1)
                if h >= 2:
                    weighted(h - 2, "xa", h - 2, lambda s, r: xa_v[:, s, (h - 2) * P:(h - 1) * P])

            def after_xa():
                pe.wait_ge(pv_taken, XH)
                banks_free(N_H2)

            down("xo", after_xa)
            norm_transposes(N_H2, xn_big)

            def ffn(n, down_name, done):
                unit, e0, tb, _, _ = FFN[n]

                def turn(i, val):
                    pe.wait_ge(proj_evac, i * 2 + (e0 + val))
                    turn_block(2 * val, [i + tb[2 * val + b] for b in range(2)], u2[:, val])

                def pair(i, first):
                    q = i * 8 + 4 * unit
                    up(q, 0, BLK, None if first else i * 2 + (e0 - 2), None if first else {1: lambda: turn(i - 1, 1)})
                    up(q + 4, 1, BLK, None if first else i * 2 + (e0 - 1), {1: lambda: turn(i, 0)})

                pair(0, True)
                with nc.tensor.Fori(0, FB - 1) as i:
                    pair(i + 1, False)
                turn(FB - 1, 1)

                def after_up():
                    pe.wait_ge(proj_evac, e0 + 2 * FB - 1)
                    banks_free(done)

                down(down_name, after_up)

            ffn(1, "dn1", N_1)
            norm_transposes(N_1, xn_big)

            units = IN2_UNITS

            def turn_unit(k):
                unit, kind, half_ = units[k]
                pe.wait_ge(proj_evac, E_IN2 + k)
                s = IN2_SLOT[kind]
                turn_block(2 * s, [TB["in2"][2 * s + b] + IN2_USE[kind][b] + half_ for b in range(2)], u2[:, s])

            def turn_odd():
                pe.wait_ge(odd_ready, 1)
                bank_free(0, TB["in2"][0] + 2)
                for r in range(2):
                    for tt in range(TT):
                        ins = nc.tensor.transpose(T2[0][:, r, tt * P:(tt + 1) * P], ckv[:, tt, r * P:(r + 1) * P], ident[:, :])
                ins.then_inc(tf[0], 1)
                bank_free(1, TB["in2"][1] + 2)
                for tt in range(TT):
                    ins = nc.tensor.transpose(T[1][:, tt * P:(tt + 1) * P], aik2[:, tt].rearrange("p k n -> p (k n)"), ident[:, :])
                ins.then_inc(tf[1], 1)
                bank_free(2, TB["in2"][2] + 2)
                c = T[2][0:BH, :]
                nc.tensor.matmul(c[:, 0:P], lf[:, 0, :], triu[:, :], start=True, stop=True)
                nc.tensor.matmul(c[:, P:L], lf[:, 0, :], ones[:, :], start=True, stop=False)
                nc.tensor.matmul(c[:, P:L], lf[:, 1, :], triu[:, :], start=False, stop=True).then_inc(tf[2], 1)

            for k, (unit, kind, half_) in enumerate(units):
                after = {}
                if k and units[k - 1][1] in IN2_SLOT:
                    after[1] = lambda k=k: turn_unit(k - 1)
                if k and units[k - 1][1] == "odd":
                    after[3] = turn_odd
                up(4 * unit, k % 2, ODD if kind == "odd" else BLK, E_IN2 + k - 2 if k >= 2 else None, after)
            pe.wait_ge(m2_landed, 64)
            bank_free(3, TB["line"][3])
            nc.tensor.matmul(T[3][0:AH, :], table, onehot, start=True, stop=True).then_inc(tf[3], 1)
            pe.wait_ge(uk_landed, 16)
            pe.wait_ge(te[0], TB["in2"][0] + 5)
            for h in range(AH):
                b = h % 4
                bank_free(b, TB["qlat"][b] + h // 4)
                for r in range(2):
                    ins = nc.tensor.matmul(T2[b][:, r, :], w_uk[:, h, r * P:(r + 1) * P], aqT[:, h, :], start=True, stop=True)
                ins.then_inc(tf[b], 1)
            for n in range(IH):
                b = n % 4
                bank_free(b, TB["idx"][b] + n // 4)
                half_ = slice(n % 2 * ID, n % 2 * ID + ID)
                for tt in range(TT):
                    ins = nc.tensor.matmul(T2[b][:, tt, :], aiqT[half_, n // 2, tt * P:(tt + 1) * P], aikT[half_, :], start=True, stop=True)
                ins.then_inc(tf[b], 1)
            pe.wait_ge(proj_evac, E_IN2 + len(units) - 1)
            for h in range(BH + 2):
                if h < BH:
                    b = h % 2
                    bank_free(b, TB["fox"][b] + h // 2)
                    pe.wait_ge(cum_row_ready, h + 1)
                    for tt in range(TT):
                        nc.tensor.matmul(T2[b][:, tt, :], bqT[:, h, tt * P:(tt + 1) * P], bkT[:, h, :], start=True, stop=False)
                        ins = nc.tensor.matmul(T2[b][:, tt, :], ones[0:BH, :], cum_row, start=False, stop=True)
                    ins.then_inc(tf[b], 1)
                if 1 <= h <= BH:
                    turn_probs(h - 1, "fox", XH + h - 1)
                if h >= 2:
                    weighted(h - 2, "fox", XH + h - 2, lambda s, r: bv[:, s, (h - 2) * P:(h - 1) * P])
            pe.wait_ge(uv_landed, 16)
            pe.wait_ge(skew_landed, 16)
            pe.wait_ge(m2_consts, 2)
            pe.wait_ge(pv_taken, XH + BH)
            for h in range(AH + 3):
                if h < AH:
                    b = h % 2
                    bank_free(b, TB["dsa"][b] + h // 2)
                    for tt in range(TT):
                        for r in range(2):
                            nc.tensor.matmul(T2[b][:, tt, :], qlT[:, h, r, tt * P:(tt + 1) * P], ckvT[:, r, :], start=(r == 0), stop=False)
                        ins = nc.tensor.matmul(T2[b][:, tt, :], anti, skew[:, h, (1 - tt) * P:(1 - tt) * P + L], start=False, stop=True)
                    ins.then_inc(tf[b], 1)
                if 1 <= h <= AH:
                    turn_probs(h - 1, "dsa", XH + BH + h - 1)
                if 2 <= h <= AH + 1:
                    weighted(h - 2, "dsa", XH + BH + h - 2, lambda s, r: ckv[:, s, r * P:(r + 1) * P], 2)
                if h >= 3:
                    g = h - 3
                    pe.wait_ge(pv_taken, XH + BH + g + 1)
                    if g >= 2:
                        pe.wait_ge(uv_taken, g - 1)
                    for r in range(2):
                        ins = nc.tensor.matmul(PB[2 + g % 2][:, 0:L], w_uv[:, g, r, :], o_lat[:, r, :], start=(r == 0), stop=(r == 1))
                    ins.then_inc(uv_done, 1)

            def after_mix():
                pe.wait_ge(uv_taken, AH)
                banks_free(N_2)

            down("wo2", after_mix)
            norm_transposes(N_2, xn_big)
            ffn(2, "dn2", "end")

        @block.vector
        def _(dve):
            own = Chain(dve, dve_own)
            V = nc.vector
            marks = iter(range(1, idle.shape[1]))

            def signal(semaphore):
                k = next(marks)
                V.memset(idle[:, k:k + 1], 0.0).then_inc(semaphore, 1)

            def lo(q, j, n=4 * BLK):
                dve.wait_ge(hi_ready, q + j + 1)
                dst, src, h = (w_lo[:, j, :], raw[:, j, :], w_hi[:, j, :]) if n == 4 * BLK else \
                    (quad(w_lo, j, n), quad(raw, j, n), quad(w_hi, j, n))
                V.tensor_tensor(dst, src, h.bitcast(F32), ALU.subtract).then_inc(lo_ready, 1)

            def lo_unit(unit, n=4 * BLK, js=range(4)):
                for j in js:
                    lo(4 * unit, j, n)

            def mean(n, width):
                dve.wait_ge(sq_done, sq_count(n))
                V.tensor_scalar(ssq(n), ssq(n), 1.0 / width, EPS, ALU.mult, ALU.add).then_inc(ms_done, 1)

            def h_lo(n, gain, k0):
                for m in range(KC // 2):
                    dve.wait_ge(h_hi_done, 8 * t_idx(n) + m + 1)
                    for c in range(2):
                        k = 2 * m + c
                        ins = V.scalar_tensor_tensor(hT_lo[:, k, :], T2[m % 4][:, c, :], col(gain, k0 + k),
                                                     hT_hi[:, k, :].bitcast(F32), ALU.mult, ALU.subtract)
                    ins.then_inc(te[m % 4], 1)

            def down(name):
                unit, xi, n, src = DOWN[name]
                for j in range(4):
                    dve.wait_ge(xs_hi, xi + j + 1)
                    V.tensor_tensor(hT_lo[:, j, :], src[:, j, :], hT_hi[:, j, :].bitcast(F32), ALU.subtract).then_inc(xs_lo, 1)
                if n > 1:
                    with V.Fori(0, n - 1) as i:
                        for j in range(4):
                            lo(i * 4 + 4 * (unit + 1), j)
                            dve.wait_ge(xs_hi, i * 4 + (xi + 4 + j + 1))
                            V.tensor_tensor(hT_lo[:, j, :], chunk(src, i * 4 + (4 + j)), hT_hi[:, j, :].bitcast(F32), ALU.subtract)\
                                .then_inc(xs_lo, 1)

            def post_norm(n, unit, k, scale=None):
                lo_unit(unit, js=(0, 1, 2))
                dve.wait_ge(sq_done, sq_count(n))
                own(V.tensor_reduce(ssq(n), ssq_parts[:, :].rearrange("p (a k) -> p a k", a=TT), AX_X, ALU.add))
                if scale is not None:
                    own(V.tensor_tensor(ssq(n), ssq(n), scale, ALU.mult))
                    own(V.tensor_tensor(ssq(n), ssq(n), scale, ALU.mult))
                V.tensor_scalar(ssq(n), ssq(n), 1.0 / D, EPS, ALU.mult, ALU.add).then_inc(ms_done, 1)
                dve.wait_ge(rstd_done, n + 1)
                if scale is not None:
                    own(V.tensor_tensor(rstd(n), rstd(n), scale, ALU.mult))
                dve.wait_ge(gain_landed, 16 * k)
                for tt in range(TT):
                    for nb in range(NB):
                        s = slice(nb * BLK, (nb + 1) * BLK)
                        ins = V.scalar_tensor_tensor(tmp_big[:, tt, s], acc[tt][nb][:, :], rstd(n)[:, tt:tt + 1], u[:, s],
                                                     ALU.mult, ALU.mult)
                    own(ins)
                    V.tensor_tensor(xt[:, tt, :], xt[:, tt, :], tmp_big[:, tt, :], ALU.add).then_inc(x_new, 1)

            def softplus(tmp, ask):
                terms = 7
                own(V.tensor_scalar(tmp[1], tmp[0], 0.0, None, ALU.max))
                V.scalar_tensor_tensor(tmp[2], tmp[0], -1.0, tmp[0], ALU.mult, ALU.min).then_inc(exp_asked, 1)
                dve.wait_ge(exp_done, ask)
                own(V.tensor_scalar(tmp[3], tmp[2], 2.0, None, ALU.add))
                own(V.reciprocal(tmp[4], tmp[3]))
                own(V.tensor_tensor(tmp[5], tmp[2], tmp[4], ALU.mult))
                own(V.tensor_tensor(tmp[6], tmp[5], tmp[5], ALU.mult))
                own(V.tensor_scalar(tmp[7], tmp[6], 1.0 / (2 * terms + 1), None, ALU.mult))
                for k in range(terms - 1, 0, -1):
                    own(V.scalar_tensor_tensor(tmp[7], tmp[7], 1.0 / (2 * k + 1), tmp[6], ALU.add, ALU.mult))
                own(V.scalar_tensor_tensor(tmp[7], tmp[7], 1.0, tmp[5], ALU.add, ALU.mult))
                own(V.scalar_tensor_tensor(tmp[0], tmp[7], 2.0, tmp[1], ALU.mult, ALU.add))

            def tap(dst, src, shift, w):
                return V.scalar_tensor_tensor(dst[:, shift:L], src[:, 0:L - shift], w, dst[:, shift:L], ALU.mult, ALU.add)

            lo_unit(0)
            for b in range(3):
                dve.wait_ge(tf[b], 1)
                n = min(BLK, NCOL - b * BLK)
                ins = V.tensor_copy(cols[:, b * BLK:b * BLK + n], T[b][:, 0:n])
                if b < 2:
                    ins.then_inc(te[b], 1)
                else:
                    ins.then_inc(te[b], 1)
            dve.wait_ge(te[2], 1)
            signal(cols_ready)
            mean(N_MEM, D)
            h_lo(N_MEM, "norm_mem", 0)
            lo_unit(1)
            for b in range(2):
                dve.wait_ge(tf[b], TB["kv"][b] + 1)
                own(V.tensor_copy(vbc[:, 2 * b:2 * b + 2, :], T2[b]))
                signal(te[b])
            signal(kT_copied)
            lo_unit(U_DT, HEADS)
            mean(N_X, D)
            h_lo(N_X, "norm_pre", 0)
            for j in range(4):
                lo(4 * U_SSD, j, 2 * NST)

            dve.wait_ge(proj_evac, E_DT)
            dve.wait_ge(small_landed, 48)
            dve.wait_ge(kv_stored, 32)
            own(V.memset(yssq[:, 0, :], 0.0))
            t0 = sp_tmp[0].rearrange("p (a h) -> p a h", a=TT)
            own(V.tensor_tensor(t0, t0, dt_bias.unsqueeze(1).broadcast_to([P, TT, HEADS]), ALU.add))
            softplus(sp_tmp, 2)
            own(V.tensor_copy(vb[:, 0:128], sp_tmp[0]))
            V.scalar_tensor_tensor(da, dt, -1.0, a_log.unsqueeze(1).broadcast_to([P, TT, HEADS]), ALU.mult, ALU.mult)\
                .then_inc(da_ready, 1)

            def sums():
                dve.wait_ge(tf[2], TB["dt"][2] + 1)
                own(V.tensor_copy(vb[:, 256:384], T[2][:, 0:128]))
                own(V.tensor_tensor(dte, T[2][:, 128:192], acs[:, 0, :], ALU.subtract))
                signal(te[2])
                signal(exp_asked)
                dve.wait_ge(tf[3], TB["dt"][3] + 1)
                own(V.tensor_copy(acsT, T[3][0:HEADS, 0:L]))
                signal(te[3])
                signal(acsT_ready)
                dve.wait_ge(exp_done, 4)

            tb = TB["ssd"]

            def by_head(a, g, n=HPG):
                return a[:, bass.ds(g * HPG, HPG)].unsqueeze(2).broadcast_to([P, HPG, HD])

            heads = lambda a: a.rearrange("p (h d) -> p h d", d=HD)

            def bc_taps(g):
                dve.wait_ge(bc_tap, g + 1)
                for t in range(SSD_TAPS - 2, -1, -1):
                    for k in range(2):
                        ins = tap(bc[:, k, :], T2[0][:, k, :], SSD_TAPS - 1 - t, col("ssd_conv_w", g + (32 + 8 * k + t * CONV_CH)))
                    if t:
                        own(ins)
                ins.then_inc(te[0], 1)

            def xs_taps(g):
                dve.wait_ge(xs_tap, g + 1)
                for t in range(SSD_TAPS - 2, -1, -1):
                    for k in range(4):
                        ins = tap(xc[:, k, :], T2[k // 2][:, k % 2, :], SSD_TAPS - 1 - t, col("ssd_conv_w", g * 4 + (k + t * CONV_CH)))
                        if t == 0 and k % 2:
                            ins.then_inc(te[k // 2], 1)
                    if t:
                        own(ins)

            def cb_out(g):
                dve.wait_ge(tf[1], g * 4 + (tb[1] + 1))
                V.tensor_tensor(cbm, T[1][:, 0:2 * P].rearrange("p (a t) -> p a t", a=TT),
                                triu[:, :].unsqueeze(1).broadcast_to([P, TT, P]), ALU.mult)
                V.tensor_copy(bm, T[1][:, 2 * P:3 * P]).then_inc(te[1], 1)

            def decayed(g):
                dve.wait_ge(te[1], g * 4 + (tb[1] + 1))
                dve.wait_ge(decay_ready, g + 1)
                for c in range(TT):
                    m = ssd_m[:, :, c * P:(c + 1) * P]
                    ins = V.tensor_tensor(m, m, cbm[:, c, :].unsqueeze(1).broadcast_to([P, HPG, P]), ALU.mult)
                ins.then_inc(m_ready, 1)

            def xs_back(g, first):
                for tt in range(TT):
                    dve.wait_ge(tf[tt], g * 4 + (tb[tt] + 3))
                    if not first:
                        dve.wait_ge(tf[2 + tt], g * 2 + tb[2 + tt])
                for tt in range(TT):
                    V.tensor_tensor(heads(xdt[:, tt, :]), heads(T[tt][:, :]), by_head(dt[:, tt, :], g), ALU.mult)
                    ins = V.tensor_tensor(heads(yg[:, tt, :]), heads(T[tt][:, :]), by_head(d_skip, g), ALU.mult)
                    ins.then_inc(te[tt], 1)
                dve.wait_ge(te[1], g * 4 + (tb[1] + 3))
                V.tensor_tensor(heads(bd), heads(xdt[:, 0, :]), by_head(dte, g), ALU.mult).then_inc(bd_ready, 1)

            def gather(g):
                dve.wait_ge(tf[1], g * 4 + (tb[1] + 4))
                V.tensor_tensor(heads(bd), heads(T[1][:, :]), by_head(eacs, g), ALU.mult).then_inc(te[1], 1)
                dve.wait_ge(te[1], g * 4 + (tb[1] + 4))
                own(V.tensor_tensor(bd, bd, yg[:, 1, :], ALU.add))
                for c in range(TT):
                    dve.wait_ge(tf[2 + c], g * 2 + (tb[2 + c] + 1))
                    V.tensor_tensor(yg[:, c, :], T[2 + c][:, :], (yg[:, 0, :], bd)[c], ALU.add).then_inc(te[2 + c], 1)
                dve.wait_ge(proj_evac, g * 3 + (E_SSD + 2))
                for c in range(TT):
                    dve.wait_ge(te[2 + c], g * 2 + (tb[2 + c] + 1))
                V.tensor_tensor(yg, yg, zs, ALU.mult).then_inc(yg_ready, 1)
                dve.wait_ge(yg_ready, g + 1)
                for c in range(TT):
                    own(V.tensor_tensor_reduce(bd, yg[:, c, :], yg[:, c, :], 1.0, 0.0, ALU.mult, ALU.add,
                                               accum_out=yssq[:, 1, c:c + 1]))
                own(V.tensor_tensor(yssq[:, 0, :], yssq[:, 0, :], yssq[:, 1, :], ALU.add))

            def group(g, prev, nxt, first=False):
                q = g * 12 + 4 * U_SSD

                def lo_next(j):
                    if nxt:
                        lo(q + 12, j, 2 * NST)
                    else:
                        lo(4 * U_WOUT, j)

                for j in range(4):
                    lo(q + 4, j)
                    if j == 1 and prev:
                        xs_back(g - 1, first)
                if not prev:
                    sums()
                lo(q + 8, 0)
                if prev:
                    gather(g - 1)
                lo(q + 8, 1)
                bc_taps(g)
                lo(q + 8, 2)
                lo(q + 8, 3)
                lo_next(0)
                cb_out(g)
                lo_next(1)
                xs_taps(g)
                lo_next(2)
                decayed(g)
                lo_next(3)

            group(0, False, True)
            group(1, True, True, True)
            with V.Fori(0, GROUPS - 3) as i:
                own.enter(i, 8)
                group(i + 2, True, True)
            own.leave(GROUPS - 3)
            group(GROUPS - 1, True, False)
            xs_back(GROUPS - 1, False)
            gather(GROUPS - 1)
            V.tensor_scalar(ssq(N_Y), yssq[:, 0, :], 1.0 / DI, EPS, ALU.mult, ALU.add).then_inc(ms_done, 1)
            down("wout")
            dve.wait_ge(rstd_done, N_Y + 1)
            dve.wait_ge(x_back, 16)
            post_norm(N_P1, U_XQ, 1, rstd(N_Y))
            lo_unit(U_XQ, js=(3,))
            mean(N_H1, D)
            h_lo(N_H1, "norm_pre", KC)

            lo_unit(U_XO)
            for b in range(2):
                dve.wait_ge(tf[b], TB["xa"][b] + 1)
                V.tensor_copy(xa_qT[:, 2 * b:2 * b + 2, :], T2[b]).then_inc(te[b], 1)

            def scale_probs(k):
                par = k % 2
                own(V.reciprocal(rden[:, 2 * par:2 * par + 2], den[:, 2 * par:2 * par + 2]))
                for tt in range(TT):
                    ins = V.tensor_scalar(prob[par][:, tt, :], prob[par][:, tt, :], rden[:, 2 * par + tt:2 * par + tt + 1], None, ALU.mult)
                ins.then_inc(p_ready, 1)

            for h in range(XH + 2):
                if h < XH:
                    b = h % 2
                    dve.wait_ge(tf[b], TB["xa"][b] + 1 + h // 2 + 1)
                    V.tensor_reduce(mx[:, 2 * b:2 * b + 2], T2[b], AX_X, ALU.max, negate=True).then_inc(s_max, 1)
                if 1 <= h <= XH:
                    b = (h - 1) % 2
                    dve.wait_ge(te[b], TB["xa"][b] + 1 + (h - 1) // 2 + 1)
                    scale_probs(h - 1)
                if h >= 2:
                    dve.wait_ge(pv_done, h - 1)
                    V.tensor_copy(xa_oT[:, h - 2, :], PB[h % 2][:, 0:L]).then_inc(pv_taken, 1)
            down("xo")
            post_norm(N_P2, U_UP1, 2)
            lo_unit(U_UP1, js=(3,))
            mean(N_H2, D)
            h_lo(N_H2, "norm_pre", 2 * KC)

            def ffn(n, down_name):
                unit, _, tb, cw, cb = FFN[n]
                m0 = (n - 1) * FB

                def gate_taps(i):
                    dve.wait_ge(gate_tap, i + (m0 + 1))
                    for t in range(FFN_TAPS - 2, -1, -1):
                        for k in range(4):
                            c = i * 4 + k
                            ins = tap(chunk(bigc, c), T2[k // 2][:, k % 2, :], FFN_TAPS - 1 - t, col(cw, c + t * 2 * FC))
                            if t == 0 and k % 2:
                                ins.then_inc(te[k // 2], 1)
                        if t:
                            own(ins)

                def val_taps(i):
                    dve.wait_ge(val_tap, i + (m0 + 1))
                    for t in range(FFN_TAPS - 2, -1, -1):
                        for k in range(4):
                            ins = tap(vbc[:, k, :], T2[2 + k // 2][:, k % 2, :], FFN_TAPS - 1 - t, col(cw, i * 4 + (k + FC + t * 2 * FC)))
                            if t == 0 and k % 2:
                                ins.then_inc(te[2 + k // 2], 1)
                        if t:
                            own(ins)
                    dve.wait_ge(te[3], i + (tb[3] + 1))
                    dve.wait_ge(gate_act, i + (m0 + 1))
                    g = big[:, bass.ds(i * (4 * L), 4 * L)]
                    V.tensor_tensor(g, g, vb[:, :], ALU.mult).then_inc(ffn_mul, 1)

                def pair(i, prev):
                    q = i * 8 + 4 * unit
                    for j in range(4):
                        lo(q + 4, j)
                        if j == 1 and prev:
                            val_taps(i - 1)
                    for j in range(4):
                        lo(q + 8, j)
                        if j == 1:
                            gate_taps(i)

                pair(0, False)
                with V.Fori(0, FB - 1) as i:
                    own.enter(i, 2)
                    pair(i + 1, True)
                own.leave(FB - 1)
                val_taps(FB - 1)
                dve.wait_ge(ffn_mul, m0 + FB)
                down(down_name)

            ffn(1, "dn1")
            post_norm(N_P3, U_IN2, 3)
            lo_unit(U_IN2, js=(3,))
            mean(N_1, D)
            h_lo(N_1, "norm1_g_2", 0)

            units = IN2_UNITS
            dest = {"aq": aqT, "aiq": aiqT, "bq": bqT, "bk": bkT}
            factor = {"aq": SCALE, "bq": SCALE}

            def unit_out(k):
                unit, kind, half_ = units[k]
                s = IN2_SLOT[kind]
                for b in range(2):
                    t = 2 * s + b
                    dve.wait_ge(tf[t], TB["in2"][t] + IN2_USE[kind][b] + half_ + 1)
                    c = 4 * half_ + 2 * b
                    V.tensor_scalar(dest[kind][:, c:c + 2, :], T2[t], factor.get(kind, 1.0), None, ALU.mult).then_inc(te[t], 1)

            def odd_in():
                dve.wait_ge(proj_evac, E_ODD)
                for tt in range(TT):
                    for k in range(2):
                        V.tensor_copy(aik2[:, tt, k, :], odd[:, tt, RANK:RANK + ID])
                V.tensor_scalar(iw, odd[:, :, RANK + ID:RANK + ID + IH], float(IH) ** -0.5, None, ALU.mult)
                f0 = fox_tmp[0].rearrange("p (a h) -> p a h", a=TT)
                own(V.scalar_tensor_tensor(f0, odd[:, :, RANK + ID + IH:ODD], -1.0,
                                           fg_bias.unsqueeze(1).broadcast_to([P, TT, BH]), ALU.mult, ALU.subtract))
                softplus(fox_tmp, 5)
                own(V.tensor_copy(x[:, 2560:2576], fox_tmp[0]))
                mean(N_CKV, RANK)
                dve.wait_ge(rstd_done, N_CKV + 1)
                for tt in range(TT):
                    ins = V.scalar_tensor_tensor(ckv[:, tt, :], odd[:, tt, 0:RANK], rstd(N_CKV)[:, tt:tt + 1], kv_gain, ALU.mult, ALU.mult)
                ins.then_inc(odd_ready, 1)

            def odd_out():
                dve.wait_ge(tf[0], TB["in2"][0] + 3)
                V.tensor_copy(ckvT, T2[0]).then_inc(te[0], 1)
                dve.wait_ge(tf[1], TB["in2"][1] + 3)
                V.tensor_copy(aikT, T[1][:, 0:L]).then_inc(te[1], 1)
                dve.wait_ge(tf[2], TB["in2"][2] + 3)
                own(V.tensor_copy(cumT, T[2][0:BH, 0:L]))
                signal(te[2])
                signal(decay_sum_ready)

            dve.wait_ge(m2_landed, 64)
            for k, (unit, kind, half_) in enumerate(units):
                nxt = ODD if unit + 1 == U_ODD else 4 * BLK
                for j in range(4):
                    lo(4 * (unit + 1), j, nxt)
                    if j == 1 and k and units[k - 1][1] in IN2_SLOT:
                        unit_out(k - 1)
                if kind == "odd":
                    odd_in()
                if k and units[k - 1][1] == "odd":
                    odd_out()
            dve.wait_ge(tf[3], TB["line"][3] + 1)
            own(V.tensor_copy(line, T[3][0:AH, :]))
            signal(te[3])
            signal(line_ready)

            for n in range(IH):
                dve.wait_ge(te[n % 4], TB["idx"][n % 4] + n // 4 + 1)
                if n:
                    dve.wait_ge(relu_used, n)
                for tt in range(TT):
                    w = iw[:, tt, n:n + 1]
                    if n == 0:
                        ins = V.tensor_scalar(score[:, tt, :], rl[0][:, tt, :], w, None, ALU.mult)
                    else:
                        ins = V.scalar_tensor_tensor(score[:, tt, :], rl[n % 4][:, tt, :], w, score[:, tt, :], ALU.mult, ALU.add)
                ins.then_inc(relu_used, 1)
            dve.wait_ge(relu_used, IH)
            dve.wait_ge(m2_consts, 2)
            own(V.tensor_tensor(sel, score, mask, ALU.add))

            def top_round(r):
                src = sel if r == 0 else score
                for tt in range(TT):
                    ins = V.max(top8[:, tt, :], src[:, tt, :])
                own(ins)
                for tt in range(TT):
                    ins = V.match_replace(score[:, tt, :], top8[:, tt, :], src[:, tt, :], TAKEN)
                own(ins)

            def attention(name, k0, bias, extra, end):
                for h in range(BH + 2):
                    if h < BH:
                        b = h % 2
                        dve.wait_ge(tf[b], TB[name][b] + h // 2 + 1)
                        if h >= 2:
                            dve.wait_ge(tf[2 + b], TB[name][2 + b] + h // 2)
                        for tt in range(TT):
                            ins = V.tensor_tensor_reduce(prob[b][:, tt, :], T2[b][:, tt, :], bias[:, tt, :], 1.0, TAKEN, ALU.add, ALU.max,
                                                         accum_out=mx[:, 2 * b + tt:2 * b + tt + 1])
                        ins.then_inc(te[b], 1)
                        dve.wait_ge(te[b], TB[name][b] + h // 2 + 1)
                        V.tensor_scalar(mx[:, 2 * b:2 * b + 2], mx[:, 2 * b:2 * b + 2], -1.0, None, ALU.mult).then_inc(s_max, 1)
                        extra(h)
                    if 1 <= h <= BH:
                        dve.wait_ge(p_exp, k0 + h)
                        scale_probs(h - 1)
                    if h >= 2:
                        end(h - 2)

            def fox_end(h):
                dve.wait_ge(pv_done, XH + h + 1)
                V.tensor_copy(mixT[:, AH + h, :], PB[h % 2][:, 0:L]).then_inc(pv_taken, 1)

            attention("fox", 0, mask, top_round, fox_end)
            assert TOPK == 8 * BH
            own(V.tensor_scalar(sel, score, TAKEN, -1.0, ALU.is_equal, ALU.add))
            own(V.scalar_tensor_tensor(sel, sel, -NEG, mask, ALU.mult, ALU.add))

            def mix_out(g):
                dve.wait_ge(uv_done, g + 1)
                V.tensor_copy(mixT[:, g, :], PB[2 + g % 2][:, 0:L]).then_inc(uv_taken, 1)

            def dsa_end(h):
                dve.wait_ge(pv_done, XH + BH + h + 1)
                if h:
                    mix_out(h - 1)
                V.tensor_copy(o_lat, PB[h % 2][:, :].rearrange(bank2, t=L)).then_inc(pv_taken, 1)

            attention("dsa", BH, sel, lambda h: None, dsa_end)
            mix_out(AH - 1)
            down("wo2")
            def add_residual(unit, src):
                dve.wait_ge(quad_used, 4 * unit)
                for tt in range(TT):
                    for nb in range(NB):
                        s = slice(nb * BLK, (nb + 1) * BLK)
                        ins = V.tensor_tensor(xt[:, tt, s], acc[tt][nb][:, :], src[:, tt, s], ALU.add)
                    ins.then_inc(x_new, 1)

            lo_unit(U_UP2, js=(0, 1, 2))
            dve.wait_ge(x_back, 32)
            add_residual(U_UP2, xn_big)
            lo_unit(U_UP2, js=(3,))
            mean(N_2, D)
            h_lo(N_2, "norm2_g_2", 0)
            ffn(2, "dn2")
            add_residual(U_END, xt)
            mean(N_FIN, D)
            dve.wait_ge(rstd_done, N_FIN + 1)
            dve.wait_ge(gain_landed, 64)
            for tt in range(TT):
                V.scalar_tensor_tensor(tmp_big[:, tt, :], xt[:, tt, :], rstd(N_FIN)[:, tt:tt + 1], u[:, :], ALU.mult, ALU.mult)\
                    .then_inc(out_ready, 1)


_INS = ["x", "mem", "norm_pre", "norm_post", "norm_mem", "ssd_w_in", "ssd_conv_w", "ssd_conv_b", "ssd_dt_bias",
        "ssd_a_log", "ssd_d", "ssd_norm_g", "ssd_w_out", "xa_w_q", "xa_w_kv", "xa_w_o", "ffn_w_up", "ffn_conv_w",
        "ffn_conv_b", "ffn_w_down", "w_in_2", "kv_norm_g_2", "w_uk_2", "w_uv_2", "t5_table_2", "fgate_b_2", "w_o_2",
        "norm1_g_2", "norm2_g_2", "w_up_2", "conv_w_2", "conv_b_2", "w_down_2", "final_g_2"]


def _bucket_onehot():
    d = np.maximum(L - 1 - np.arange(BLK), 0)
    exact = NBUCKET // 2
    far = exact + (np.log(np.maximum(d, 1) / exact) / np.log(MAXDIST / exact) * (NBUCKET - exact)).astype(np.int32)
    bucket = np.where(d < exact, d, np.minimum(far, NBUCKET - 1))
    return (bucket[None, :] == np.arange(NBUCKET)[:, None]).astype(np.float32)


def kernel(**inputs):
    import concourse.bacc as _bacc
    from concourse.bass_utils import run_bass_kernel_spmd as _run

    nc = _bacc.Bacc("TRN2", target_bir_lowering=False, num_devices=1)
    arrays, aps = {}, {}
    for name in _INS + ["bucket_onehot"]:
        a = _bucket_onehot() if name == "bucket_onehot" else np.ascontiguousarray(inputs[name])
        arrays[f"in_{name}_dram"] = a
        aps[name] = nc.dram_tensor(f"in_{name}_dram", a.shape, mybir.dt.from_np(a.dtype), kind="ExternalInput").ap()
    out = nc.dram_tensor("out_0_dram", (1, L, D), F32, kind="ExternalOutput").ap()
    program(nc, aps, out)
    r = _run(nc, [arrays], core_ids=[0])
    return r.results[0]["out_0_dram"]
```

```python
from contextlib import ExitStack

import numpy as np

import concourse.bass as bass
from concourse import mybir

F32 = mybir.dt.float32
F32R = mybir.dt.float32r
ALU = mybir.AluOpType
ACT = mybir.ActivationFunctionType
AX_X = mybir.AxisListType.X

P = 128
L = 256
TT = L // P
D = 2048
KC = D // P
BLK = 512
NB = D // BLK
EPS = 1e-6
NEG = -1e30
TAKEN = -3e38

GROUPS, HPG, HD, NST = 8, 8, 64, 128
HEADS = GROUPS * HPG
DI = HEADS * HD
XS_COL, B_COL, C_COL, DT_COL = DI, 2 * DI, 2 * DI + GROUPS * NST, 2 * DI + 2 * GROUPS * NST
CONV_CH = (DI + 2 * GROUPS * NST) // P
SSD_TAPS = 4
XH = 4
XW = XH * P
F = 5632
FC = F // P
FB = F // BLK
FFN_TAPS = 3
AH, BH, RANK, IH, ID = 8, 8, 256, 16, 64
TOPK = min(256, L // 4)
NBUCKET, MAXDIST = 32, 128
AKV = AH * P
AIQ = AKV + RANK
AIK = AIQ + IH * ID
AIW = AIK + ID
BQ = AIW + IH
BK = BQ + BH * P
BV = BK + BH * P
BF = BV + BH * P
ODD = RANK + ID + IH + BH
SCALE = float(P) ** -0.5

COLS = {}
_n = 0
for _name, _rows in (("norm_pre", 3 * KC), ("norm_mem", KC), ("ssd_conv_w", SSD_TAPS * CONV_CH),
                     ("ssd_conv_b", CONV_CH), ("ssd_norm_g", DI // P), ("ffn_conv_w", FFN_TAPS * 2 * FC),
                     ("ffn_conv_b", 2 * FC), ("norm1_g_2", KC), ("norm2_g_2", KC),
                     ("conv_w_2", FFN_TAPS * 2 * FC), ("conv_b_2", 2 * FC)):
    COLS[_name] = (_n, _rows)
    _n += _rows
NCOL = _n
NROWT = -(-NCOL // P)
N_ROW_LOADS = sum((r + n - 1) // P - r // P + 1 for r, n in COLS.values())

U_KV, U_DT, U_SSD = 0, 2, 3
U_WOUT = U_SSD + 3 * GROUPS
U_XQ = U_WOUT + DI // P // 4
U_XO = U_XQ + 1
U_UP1 = U_XO + 1
U_DN1 = U_UP1 + 2 * FB
U_IN2 = U_DN1 + FC // 4
U_ODD = U_IN2 + 4
U_B = U_ODD + 1
U_WO2 = U_B + 6
U_UP2 = U_WO2 + 4
U_DN2 = U_UP2 + 2 * FB
U_END = U_DN2 + FC // 4

E_KV, E_DT, E_SSD = 1, 3, 4
E_XQ = E_SSD + 3 * GROUPS
E_UP1 = E_XQ + 1
E_IN2 = E_UP1 + 2 * FB
E_ODD = E_IN2 + 4
E_B = E_ODD + 1
E_UP2 = E_B + 6

X_WOUT = 0
X_XO = X_WOUT + DI // P
X_DN1 = X_XO + XH
X_WO2 = X_DN1 + FC
X_DN2 = X_WO2 + KC

N_MEM, N_X, N_Y, N_P1, N_H1, N_P2, N_H2, N_P3, N_1, N_CKV, N_2, N_FIN = range(12)
TRANSPOSED = [N_MEM, N_X, N_H1, N_H2, N_1, N_2]
POST = [N_P1, N_P2, N_P3]


def nth(n, tt):
    if n in POST:
        return 2 * n + 2 * tt + 1
    if n - 1 in POST:
        return 2 * (n - 1) + 2 * tt + 2
    return 2 * n + tt + 1


T_PLAN = [("params", (1, 1, 1, 0)), (N_MEM, (2,) * 4), ("kv", (1, 1, 0, 0)), (N_X, (2,) * 4),
          ("dt", (0, 0, 1, 1)), ("ssd", (4 * GROUPS, 4 * GROUPS, 2 * GROUPS, 2 * GROUPS)), (N_H1, (2,) * 4),
          ("xa", (3, 3, 2, 2)), (N_H2, (2,) * 4), ("up1", (FB,) * 4), (N_1, (2,) * 4), ("in2", (5, 5, 5, 4)),
          ("line", (0, 0, 0, 1)), ("qlat", (2,) * 4), ("idx", (4,) * 4), ("fox", (4,) * 4), ("dsa", (4,) * 4),
          (N_2, (2,) * 4), ("up2", (FB,) * 4), ("end", (0,) * 4)]
TB = {}
_at = [0] * 4
for _name, _uses in T_PLAN:
    TB[_name] = tuple(_at)
    _at = [a + u for a, u in zip(_at, _uses)]


IN2_UNITS = [(U_IN2, "aq", 0), (U_IN2 + 1, "aiq", 0), (U_IN2 + 2, "aq", 1), (U_IN2 + 3, "aiq", 1), (U_ODD, "odd", 0),
             (U_B, "bq", 0), (U_B + 1, "bk", 0), (U_B + 2, "bv", 0), (U_B + 3, "bq", 1), (U_B + 4, "bk", 1), (U_B + 5, "bv", 1)]
IN2_SLOT = {"aq": 0, "aiq": 1, "bq": 0, "bk": 1}
IN2_USE = {"aq": (0, 0), "aiq": (0, 0), "bq": (3, 3), "bk": (3, 2)}
IN2_TURN = {"aq": 0, "aiq": 0, "bq": 2, "bk": 2}


class Chain:

    def __init__(self, eng, sem):
        self.eng, self.sem, self.n, self.reg, self.per = eng, sem, 0, None, 0

    def __call__(self, ins):
        self.n += 1
        ins.then_inc(self.sem, 1)
        self.eng.wait_ge(self.sem, self.n if self.reg is None else self.reg * self.per + self.n)

    def enter(self, reg, per):
        self.reg, self.per, self.start = reg, per, self.n

    def leave(self, turns):
        assert self.n - self.start == self.per, (self.n - self.start, self.per)
        self.n = self.start + self.per * turns
        self.reg = None


def program(nc, I, out):
    with ExitStack() as ctx:
        def sb(name, shape, dt=F32):
            return ctx.enter_context(nc.sbuf_tensor(name, shape, dt))

        def sem(name):
            return ctx.enter_context(nc.semaphore(name))

        hT_at = -(-nc.sbuf_base // 32) * 32
        hT_hi = sb("hT_hi", [P, KC, L], F32R)
        hT_lo = sb("hT_lo", [P, KC, L], F32R)
        attn = nc.alloc_sbuf_tensor_at("attn", [P, 2 * KC * L], F32, offset=hT_at)
        raw = sb("raw", [P, 4, 4 * BLK])
        w_hi = sb("w_hi", [P, 4, 4 * BLK], F32R)
        w_lo = sb("w_lo", [P, 4, 4 * BLK], F32R)
        big = sb("big", [P, FC * L])
        x = sb("x", [P, TT * D])
        u = sb("u", [P, 4 * BLK])
        vb = sb("vb", [P, 4 * L])
        cols = sb("cols", [P, NCOL])
        ident = sb("ident", [P, P])
        triu = sb("triu", [P, P])
        ones = sb("ones", [P, P])
        small = sb("small", [P, 3 * HEADS])
        misc = sb("misc", [P, L])
        diag = misc[:, :].rearrange("p (a t) -> p a t", a=TT)
        stat = sb("stat", [P, 48])

        bigc = big[:, :].rearrange("p (c t) -> p c t", t=L)
        xt = x[:, :].rearrange("p (a n) -> p a n", a=TT)
        u2 = u[:, :].rearrange("p (s a n) -> p s a n", s=2, a=TT)
        vbc = vb[:, :].rearrange("p (c t) -> p c t", t=L)
        xn_big = big[:, 0:TT * D].rearrange("p (a n) -> p a n", a=TT)
        tmp_big = big[:, TT * D:2 * TT * D].rearrange("p (a n) -> p a n", a=TT)
        bank2 = "p (c t) -> p c t"

        ssq = lambda n: stat[:, 2 * n:2 * n + 2]
        rstd = lambda n: stat[:, 24 + 2 * n:24 + 2 * n + 2]
        ssq_parts = sb("ssq_parts", [P, TT * NB])
        half = sb("half", [P, 2])
        mx = sb("mx", [P, 4])
        den = sb("den", [P, 4])
        rden = sb("rden", [P, 4])

        idle = sb("idle", [P, 13])
        rows = tmp_big[:, 0, 0:NROWT * P].rearrange("p (r f) -> p r f", f=P)

        ssd_m = x[:, 0:8 * L].rearrange("p (h t) -> p h t", t=L)
        xdt = x[:, 2048:3072].rearrange("p (a n) -> p a n", a=TT)
        yg = x[:, 3072:4096].rearrange("p (a n) -> p a n", a=TT)
        zs = big[:, 8192:9216].rearrange("p (a n) -> p a n", a=TT)
        xc = big[:, 9216:10240].rearrange(bank2, t=L)
        bc = big[:, 10240:10752].rearrange(bank2, t=L)
        bd = big[:, 10752:11264]
        u_xs = u2[:, 0]
        u_bc = u[:, 1024:1536].rearrange("p (a n) -> p a n", a=TT)
        states = u[:, 1536:2048]
        dt = vb[:, 0:128].rearrange("p (a h) -> p a h", a=TT)
        da = vb[:, 128:256].rearrange("p (a h) -> p a h", a=TT)
        acs = vb[:, 256:384].rearrange("p (a h) -> p a h", a=TT)
        dte = vb[:, 384:448]
        eacs = vb[:, 448:512]
        bm = vb[:, 512:640]
        cbm = vb[:, 640:896].rearrange("p (a t) -> p a t", a=TT)
        yssq = vb[:, 896:900].rearrange("p (k a) -> p k a", k=2)
        dt_bias, a_log, d_skip = (small[:, k * HEADS:(k + 1) * HEADS] for k in range(3))
        acsT = misc[0:HEADS, :]
        sp_tmp = [big[:, 4096 + 128 * k:4096 + 128 * (k + 1)] for k in range(8)]

        xa_kT = big[:, 4096:5120].rearrange(bank2, t=L)
        xa_v = big[:, 5120:6144].rearrange("p (a n) -> p a n", a=TT)
        xa_qT = big[:, 6144:7168].rearrange(bank2, t=L)
        xa_oT = big[:, 7168:8192].rearrange(bank2, t=L)
        prob = [u[:, 512 * k:512 * (k + 1)].rearrange("p (a s) -> p a s", a=TT) for k in range(2)]
        probT = [u[:, 1024 + 512 * k:1024 + 512 * (k + 1)].rearrange("p (a t) -> p a t", a=TT) for k in range(2)]

        aqT = big[:, 0:2048].rearrange(bank2, t=L)
        aiqT = big[:, 2048:4096].rearrange(bank2, t=L)
        bqT = big[:, 4096:6144].rearrange(bank2, t=L)
        bkT = big[:, 6144:8192].rearrange(bank2, t=L)
        bv = big[:, 8192:10240].rearrange("p (a n) -> p a n", a=TT)
        ckv = big[:, 10240:10752].rearrange("p (a r) -> p a r", a=TT)
        ckvT = big[:, 10752:11264].rearrange(bank2, t=L)
        w_uv = big[:, 0:2048].rearrange("p (h c d) -> p h c d", h=AH, c=2)
        w_uk = u[:, :].rearrange("p (h r) -> p h r", h=AH)
        qlT = attn[:, 0:4096].rearrange("p (h c t) -> p h c t", h=AH, c=2)
        skew = attn[:, 4096:7168].rearrange("p (h s) -> p h s", h=AH)
        score = attn[:, 7168:7680].rearrange("p (a s) -> p a s", a=TT)
        sel = attn[:, 7680:8192].rearrange("p (a s) -> p a s", a=TT)
        mixT = x[:, :].rearrange(bank2, t=L)
        odd = x[:, 0:2 * ODD].rearrange("p (a n) -> p a n", a=TT)
        aik2 = x[:, 768:1024].rearrange("p (a k n) -> p a k n", a=TT, k=2)
        onehot = x[0:NBUCKET, 1024:1536]
        line = x[0:AH, 1536:2048]
        kv_gain = x[:, 2048:2048 + RANK]
        table = x[0:NBUCKET, 2304:2304 + AH]
        fg_bias = x[:, 2320:2320 + BH]
        fox_tmp = [x[:, 2400 + 16 * k:2416 + 16 * k] for k in range(8)]
        lf = x[:, 2560:2576].rearrange("p (a h) -> p a h", a=TT)
        mask = vb[:, 0:512].rearrange("p (a s) -> p a s", a=TT)
        aikT = vb[:, 512:768]
        cum_row = vb[0:BH, 768:1024]
        anti = small[:, 0:P]
        iw = small[:, 128:160].rearrange("p (a h) -> p a h", a=TT)
        top8 = small[:, 160:176].rearrange("p (a k) -> p a k", a=TT)
        cumT = misc[0:BH, :]
        o_lat = attn[:, 7168:7680].rearrange(bank2, t=L)
        rl = [u[:, 512 * k:512 * (k + 1)].rearrange("p (a s) -> p a s", a=TT) for k in range(4)]

        PB = [ctx.enter_context(nc.psum_tensor(f"PB{k}", [P, BLK], F32)) for k in range(4)]
        T = [ctx.enter_context(nc.psum_tensor(f"T{k}", [P, BLK], F32)) for k in range(4)]
        T2 = [t[:, :].rearrange(bank2, t=L) for t in T]
        acc = [T, PB]

        kT_d = nc.dram_tensor("kT_d", (P, XH * L), F32, kind="Internal").ap()
        v_d = nc.dram_tensor("v_d", (P, TT * XW), F32, kind="Internal").ap()
        acsT_d = nc.dram_tensor("acsT_d", (HEADS, L), F32, kind="Internal").ap()
        x_d = nc.dram_tensor("x_d", (P, TT * D), F32, kind="Internal").ap()
        line_d = nc.dram_tensor("line_d", (AH, BLK), F32, kind="Internal").ap()

        raw_landed = [sem(f"raw_landed{j}") for j in range(4)]
        c_landed = [sem(f"c_landed{j}") for j in range(4)]
        odd_landed = [sem(f"odd_landed{j}") for j in range(4)]
        hi_ready, lo_ready = sem("hi_ready"), sem("lo_ready")
        quad_used = sem("quad_used")
        proj_evac = sem("proj_evac")
        tf = [sem(f"t{b}_full") for b in range(4)]
        te = [sem(f"t{b}_empty") for b in range(4)]
        xs_hi, xs_lo = sem("xs_hi"), sem("xs_lo")
        consts_ready, rows_landed, cols_ready = sem("consts_ready"), sem("rows_landed"), sem("cols_ready")
        x_landed = [sem(f"x_landed{tt}") for tt in range(TT)]
        mem_landed = [sem(f"mem_landed{tt}") for tt in range(TT)]
        small_landed = sem("small_landed")
        sq_done, ms_done, rstd_done = sem("sq_done"), sem("ms_done"), sem("rstd_done")
        diag_ready = sem("diag_ready")
        tile0_done = sem("tile0_done")
        h_hi_done = sem("h_hi_done")
        kT_copied, kv_stored, kv_loaded = sem("kT_copied"), sem("kv_stored"), sem("kv_loaded")
        exp_asked, exp_done = sem("exp_asked"), sem("exp_done")
        da_ready, acsT_ready, acsT_stored = sem("da_ready"), sem("acsT_ready"), sem("acsT_stored")
        acs_landed, diff_made, diff_ready = sem("acs_landed"), sem("diff_made"), sem("diff_ready")
        decay_ready, m_ready = sem("decay_ready"), sem("m_ready")
        bc_tap, bc_ready, xs_tap, xc_ready = sem("bc_tap"), sem("bc_ready"), sem("xs_tap"), sem("xc_ready")
        bd_ready, yg_ready = sem("bd_ready"), sem("yg_ready")
        x_back, gain_landed, x_new, x_spilled = sem("x_back"), sem("gain_landed"), sem("x_new"), sem("x_spilled")
        gate_tap, val_tap, gate_act, ffn_mul = sem("gate_tap"), sem("val_tap"), sem("gate_act"), sem("ffn_mul")
        s_max, p_exp, p_ready = sem("s_max"), sem("p_exp"), sem("p_ready")
        pv_done, pv_taken = sem("pv_done"), sem("pv_taken")
        uv_done, uv_taken = sem("uv_done"), sem("uv_taken")
        m2_landed, m2_consts = sem("m2_landed"), sem("m2_consts")
        odd_ready, decay_sum_ready = sem("odd_ready"), sem("decay_sum_ready")
        line_ready, line_stored, skew_landed = sem("line_ready"), sem("line_stored"), sem("skew_landed")
        uk_landed, uv_landed, cum_row_ready = sem("uk_landed"), sem("uv_landed"), sem("cum_row_ready")
        relu_done, relu_used, sel_ready = sem("relu_done"), sem("relu_used"), sem("sel_ready")
        out_ready, out_stored = sem("out_ready"), sem("out_stored")
        act_own, dve_own, pool_own = sem("act_own"), sem("dve_own"), sem("pool_own")

        def quad(buf, j, n):
            return buf[:, j, :].rearrange("p (c n) -> p c n", c=4)[:, :, 0:n]

        def col(name, k):
            return cols[:, bass.ds(k + COLS[name][0], 1)]

        def landed(unit):
            return 16 * (unit + 1 - (unit > U_ODD))

        def chunk(a, k):
            return a[:, bass.ds(k, 1), :].rearrange("p c t -> p (c t)")

        def sq_count(n, tt):
            return nth(n, tt) - TT * (n > N_Y)

        def t_idx(n):
            return TRANSPOSED.index(n)

        rows3 = lambda w: w.rearrange("(c p) n -> p c n", p=P)
        w_ssd, w_kv, w_q = rows3(I["ssd_w_in"][0]), rows3(I["xa_w_kv"][0]), rows3(I["xa_w_q"][0])
        w_up = {1: rows3(I["ffn_w_up"][0]), 2: rows3(I["w_up_2"][0])}
        w_in2 = rows3(I["w_in_2"][0])
        down_w = {"wout": rows3(I["ssd_w_out"][0]), "xo": rows3(I["xa_w_o"][0]), "dn1": rows3(I["ffn_w_down"][0]),
                  "wo2": rows3(I["w_o_2"][0]), "dn2": rows3(I["w_down_2"][0])}
        DOWN = {"wout": (U_WOUT, X_WOUT, DI // P // 4, bigc), "xo": (U_XO, X_XO, 1, xa_oT),
                "dn1": (U_DN1, X_DN1, FC // 4, bigc), "wo2": (U_WO2, X_WO2, KC // 4, mixT),
                "dn2": (U_DN2, X_DN2, FC // 4, bigc)}
        FFN = {1: (U_UP1, E_UP1, TB["up1"], "ffn_conv_w", "ffn_conv_b"),
               2: (U_UP2, E_UP2, TB["up2"], "conv_w_2", "conv_b_2")}
        tokens = lambda a: a.rearrange("(a p) n -> p a n", p=P)

        block = ctx.enter_context(nc.Block())

        @block.sync
        def _(sp):
            def load_up(q, w, c0, n, first=False):
                for j in range(4):
                    if not first:
                        sp.wait_ge(lo_ready, q - 3 + j)
                    sp.dma_start(quad(raw, j, n), w[:, 4 * j:4 * j + 4, bass.ds(c0, n)]).then_inc(raw_landed[j], 16)

            def load_down(name):
                unit, _, n, _ = DOWN[name]

                def rows(q, chunk):
                    for j in range(4):
                        sp.wait_ge(lo_ready, q - 3 + j)
                        sp.dma_start(raw[:, j, :], down_w[name][:, bass.ds(chunk + j, 1), :].rearrange("p c n -> p (c n)"))\
                            .then_inc(raw_landed[j], 16)

                if n == 1:
                    rows(4 * unit, 0)
                else:
                    with nc.sync.Fori(0, n) as i:
                        rows(i * 4 + 4 * unit, i * 4)

            def load_ffn(n):
                unit = FFN[n][0]
                with nc.sync.Fori(0, FB) as i:
                    load_up(i * 8 + 4 * unit, w_up[n], i * BLK, BLK)
                    load_up(i * 8 + 4 * (unit + 1), w_up[n], i * BLK + F, BLK)

            for tt in range(TT):
                sp.dma_start(xn_big[:, tt, :], I["mem"][0, tt * P:(tt + 1) * P, :]).then_inc(mem_landed[tt], 16)
            for name, (r0, n) in COLS.items():
                a = I[name]
                flat = a.rearrange("a b (c f) -> (a b c) f", f=P) if len(a.shape) == 3 \
                    else a.rearrange("a (c f) -> (a c) f", f=P)
                r = r0
                while r < r0 + n:
                    k = min(r0 + n - r, P - r % P)
                    sp.dma_start(rows[r % P:r % P + k, r // P, :], flat[r - r0:r - r0 + k, :]).then_inc(rows_landed, 16)
                    r += k
            load_up(0, w_kv, 0, BLK, first=True)
            for tt in range(TT):
                sp.dma_start(xt[:, tt, :], I["x"][0, tt * P:(tt + 1) * P, :]).then_inc(x_landed[tt], 16)
            load_up(4, w_kv, XW, BLK)
            load_up(4 * U_DT, w_ssd, DT_COL, HEADS)
            with nc.sync.Fori(1, GROUPS + 1) as g1:
                q = g1 * 12 + (4 * U_SSD - 12)
                for j in range(4):
                    sp.wait_ge(lo_ready, q - 3 + j)
                    for k in range(2):
                        sp.dma_start(quad(raw, j, 2 * NST)[:, :, k * NST:(k + 1) * NST],
                                     w_ssd[:, 4 * j:4 * j + 4, bass.ds(g1 * NST + ((B_COL, C_COL)[k] - NST), NST)])\
                            .then_inc((raw_landed, c_landed)[k][j], 16)
                load_up(q + 4, w_ssd, g1 * BLK + (XS_COL - BLK), BLK)
                load_up(q + 8, w_ssd, g1 * BLK + (-BLK), BLK)
            load_down("wout")
            load_up(4 * U_XQ, w_q, 0, XW)
            load_down("xo")
            load_ffn(1)
            load_down("dn1")
            for k in range(2):
                load_up(4 * (U_IN2 + 2 * k), w_in2, k * BLK, BLK)
                load_up(4 * (U_IN2 + 2 * k + 1), w_in2, AIQ + k * BLK, BLK)
            for j in range(4):
                sp.wait_ge(lo_ready, 4 * U_ODD - 3 + j)
                for c0, n, at in ((AKV, RANK, 0), (AIK, ID + IH, RANK), (BF, BH, RANK + ID + IH)):
                    sp.dma_start(quad(raw, j, ODD)[:, :, at:at + n], w_in2[:, 4 * j:4 * j + 4, c0:c0 + n])\
                        .then_inc(odd_landed[j], 16)
            for k in range(2):
                for m, c0 in enumerate((BQ, BK, BV)):
                    load_up(4 * (U_B + 3 * k + m), w_in2, c0 + k * BLK, BLK)
            load_down("wo2")
            load_ffn(2)
            load_down("dn2")
            for tt in range(TT):
                sp.wait_ge(out_ready, tt + 1)
                sp.dma_start(out[0, tt * P:(tt + 1) * P, :], tmp_big[:, tt, :]).then_inc(out_stored, 16)
            sp.wait_ge(out_stored, 16 * TT)

        @block.gpsimd
        def _(pool):
            nc.gpsimd.memset(ident[:, :], 0.0).then_inc(pool_own, 1)
            nc.gpsimd.memset(ones[:, :], 1.0).then_inc(pool_own, 1)
            nc.gpsimd.memset(half[:, :], -0.5).then_inc(pool_own, 1)
            pool.wait_ge(pool_own, 3)
            nc.gpsimd.affine_select(out=ident[:, :], in_=ident[:, :], compare_op=ALU.not_equal, fill=1.0, base=0,
                                    pattern=[[-1, P]], channel_multiplier=1).then_inc(consts_ready, 1)
            nc.gpsimd.affine_select(out=triu[:, :], in_=ones[:, :], compare_op=ALU.is_ge, fill=0.0, base=0,
                                    pattern=[[1, P]], channel_multiplier=-1).then_inc(consts_ready, 1)

            for dst, name in ((dt_bias, "ssd_dt_bias"), (a_log, "ssd_a_log"), (d_skip, "ssd_d")):
                pool.dma_start(dst, I[name][0].partition_broadcast(P)).then_inc(small_landed, 16)

            def inverse_root(n, tiles=range(TT)):
                for tt in tiles:
                    r = rstd(n)[:, tt:tt + 1]
                    pool.wait_ge(ms_done, nth(n, tt))
                    nc.gpsimd.tensor_tensor(r, ssq(n)[:, tt:tt + 1], half[:, 0:1], ALU.pow).then_inc(rstd_done, 1)
                    if n in TRANSPOSED:
                        pool.wait_ge(rstd_done, nth(n, tt))
                        nc.gpsimd.tensor_tensor(diag[:, tt, :], ident[:, :], r.broadcast_to([P, P]), ALU.mult)\
                            .then_inc(diag_ready, 1)

            def inverse_roots(post, n):
                for tt in range(TT):
                    inverse_root(post, (tt,))
                    inverse_root(n, (tt,))

            def load_gain(src):
                pool.dma_start(u[:, :], src.partition_broadcast(P)).then_inc(gain_landed, 16)

            inverse_root(N_MEM)
            inverse_root(N_X)
            pool.wait_ge(kT_copied, 1)
            pool.wait_ge(proj_evac, E_KV + 1)
            pool.dma_start(kT_d, vb[:, :]).then_inc(kv_stored, 16)
            pool.dma_start(v_d, u[:, 1024:2048]).then_inc(kv_stored, 16)
            pool.wait_ge(acsT_ready, 1)
            pool.dma_start(acsT_d, acsT).then_inc(acsT_stored, 16)
            pool.wait_ge(acsT_stored, 16)

            def exponents(g):
                pool.dma_start(ssd_m, bass.AP(acsT_d.tensor, g * (HPG * L), [[0, P], [L, HPG], [1, L]]))\
                    .then_inc(acs_landed, 16)
                pool.wait_ge(acs_landed, g * 16 + 16)
                for c in range(TT):
                    e = ssd_m[:, :, c * P:(c + 1) * P]
                    at_s = acs[:, c, bass.ds(g * HPG, HPG)].unsqueeze(2).broadcast_to([P, HPG, P])
                    ins = nc.gpsimd.tensor_tensor(e, e, at_s, ALU.subtract)
                ins.then_inc(diff_made, 1)
                pool.wait_ge(diff_made, g + 1)
                nc.gpsimd.tensor_tensor(idle[:, 0:1], half[:, 0:1], half[:, 1:2], ALU.add)
                nc.gpsimd.tensor_scalar(x[:, 0:2048], x[:, 0:2048], 0.0, None, ALU.min).then_inc(diff_ready, 1)

            exponents(0)
            with nc.gpsimd.Fori(0, GROUPS - 1) as i:
                pool.wait_ge(tf[3], i * 2 + (TB["ssd"][3] + 1))
                nc.gpsimd.tensor_tensor(idle[:, 0:1], half[:, 0:1], half[:, 1:2], ALU.add)
                exponents(i + 1)

            inverse_root(N_Y)
            pool.wait_ge(te[3], TB["ssd"][3] + 2 * GROUPS)
            pool.dma_start(xt, tokens(I["x"][0])).then_inc(x_back, 16)
            load_gain(I["norm_post"][0, 0])
            inverse_roots(N_P1, N_H1)
            pool.wait_ge(kv_stored, 32)
            pool.wait_ge(x_new, TT * NB)
            pool.dma_start(big[:, 4096:5120], kT_d).then_inc(kv_loaded, 16)
            pool.dma_start(big[:, 5120:6144], v_d).then_inc(kv_loaded, 16)
            pool.wait_ge(pv_done, XH)
            load_gain(I["norm_post"][0, 1])
            inverse_roots(N_P2, N_H2)
            pool.wait_ge(tf[3], TB["up1"][3] + FB)
            load_gain(I["norm_post"][0, 2])
            inverse_roots(N_P3, N_1)
            pool.wait_ge(x_new, 3 * TT * NB)
            pool.dma_start(x_d, x[:, :]).then_inc(x_spilled, 16)
            pool.wait_ge(x_spilled, 16)
            for b in range(4):
                pool.wait_ge(tf[b], TB[N_1][b] + 2)
            for dst, src in ((onehot, I["bucket_onehot"]), (table, I["t5_table_2"]),
                             (kv_gain, I["kv_norm_g_2"][0].partition_broadcast(P)),
                             (fg_bias, I["fgate_b_2"][0].partition_broadcast(P))):
                pool.dma_start(dst, src).then_inc(m2_landed, 16)
            nc.gpsimd.memset(anti, 0.0).then_inc(pool_own, 1)
            nc.gpsimd.memset(vb[:, 0:512], 0.0).then_inc(pool_own, 1)
            pool.wait_ge(pool_own, 5)
            nc.gpsimd.affine_select(out=anti, in_=anti, compare_op=ALU.not_equal, fill=1.0, base=-(P - 1),
                                    pattern=[[1, P]], channel_multiplier=1).then_inc(m2_consts, 1)
            nc.gpsimd.affine_select(out=mask, in_=mask, compare_op=ALU.is_ge, fill=NEG, base=0,
                                    pattern=[[P, TT], [-1, L]], channel_multiplier=1).then_inc(m2_consts, 1)
            inverse_root(N_CKV)
            pool.wait_ge(line_ready, 1)
            pool.dma_start(line_d, line).then_inc(line_stored, 16)
            pool.wait_ge(te[2], TB["in2"][2] + 5)
            pool.wait_ge(te[3], TB["in2"][3] + 4)
            pool.wait_ge(te[1], TB["in2"][1] + 5)
            pool.dma_start(w_uk, I["w_uk_2"][0].rearrange("h d r -> d h r")).then_inc(uk_landed, 16)
            pool.wait_ge(line_stored, 16)
            pool.wait_ge(quad_used, 4 * U_WO2)
            pool.dma_start(skew, bass.AP(line_d.tensor, 0, [[1, P], [BLK, AH], [1, L + P]])).then_inc(skew_landed, 16)
            for b in range(4):
                pool.wait_ge(tf[b], TB["qlat"][b] + 2)
            pool.dma_start(w_uv, I["w_uv_2"][0].rearrange("h (c p) d -> p h c d", p=P)).then_inc(uv_landed, 16)
            pool.wait_ge(decay_sum_ready, 1)
            for h in range(BH):
                if h:
                    b = (h - 1) % 2
                    pool.wait_ge(tf[b], TB["fox"][b] + (h - 1) // 2 + 1)
                nc.gpsimd.tensor_scalar(cum_row, cumT, ident[0:BH, h:h + 1], None, ALU.mult).then_inc(cum_row_ready, 1)
            pool.wait_ge(uv_done, AH)
            pool.dma_start(xn_big, x_d.rearrange("p (a n) -> p a n", a=TT)).then_inc(x_back, 16)
            inverse_root(N_2)
            pool.wait_ge(tf[3], TB["up2"][3] + FB)
            load_gain(I["final_g_2"])
            inverse_root(N_FIN)

        @block.scalar
        def _(act):
            def hi(q, land, j, n=4 * BLK, land_sem=None, first=False):
                act.wait_ge(land_sem or raw_landed[j], land)
                if not first:
                    act.wait_ge(quad_used, q - 3 + j)
                dst, src = (w_hi[:, j, :], raw[:, j, :]) if n == 4 * BLK else (quad(w_hi, j, n), quad(raw, j, n))
                nc.scalar.activation(dst, src, ACT.Copy).then_inc(hi_ready, 1)

            def hi_unit(unit, n=4 * BLK, js=range(4), first=False):
                for j in js:
                    hi(4 * unit, landed(unit), j, n, None, first)

            def hi_bc(g, j):
                act.wait_ge(c_landed[j], g * 16 + 16)
                hi(g * 12 + 4 * U_SSD, g * 48 + landed(U_SSD), j, 2 * NST)

            def evac(q, pair, dst, n=BLK, func=ACT.Copy, scale=1.0):
                act.wait_ge(quad_used, q + 4)
                for tt in range(TT):
                    ins = nc.scalar.activation(dst[:, tt, 0:n], PB[2 * pair + tt][:, 0:n], func, scale=scale)
                ins.then_inc(proj_evac, 1)

            def square(n, tt, src, scratch):
                nc.scalar.activation(scratch, src, ACT.Square, accum_out=ssq(n)[:, tt:tt + 1]).then_inc(sq_done, 1)

            def h_hi(n, tt, gain, k0, quads=None):
                for b in range(4):
                    if quads is not None:
                        act.wait_ge(quad_used, quads + b)
                    act.wait_ge(tf[b], TB[n][b] + tt + 1)
                    for c in range(4):
                        k = 4 * b + c
                        ins = nc.scalar.activation(hT_hi[:, k, tt * P:(tt + 1) * P], T[b][:, c * P:(c + 1) * P], ACT.Copy,
                                                   scale=col(gain, k0 + k))
                    ins.then_inc(h_hi_done, 1)

            def down_first(name, ready):
                unit, _, _, src = DOWN[name]
                act.wait_ge(quad_used, 4 * unit)
                for j in range(4):
                    ready(j)
                    nc.scalar.activation(hT_hi[:, j, :], src[:, j, :], ACT.Copy).then_inc(xs_hi, 1)

            def down_rest(name):
                unit, _, n, src = DOWN[name]
                with nc.scalar.Fori(0, n - 1) as i:
                    for j in range(4):
                        hi(i * 4 + 4 * (unit + 1), i * 16 + landed(unit + 1), j)
                        nc.scalar.activation(hT_hi[:, j, :], chunk(src, i * 4 + (4 + j)), ACT.Copy).then_inc(xs_hi, 1)

            def square_bank(n, tt, nb, src, scratch):
                k = tt * NB + nb
                ins = nc.scalar.activation(scratch[:, tt, nb * BLK:(nb + 1) * BLK], src, ACT.Square, accum_out=ssq_parts[:, k:k + 1])
                if nb == NB - 1:
                    ins.then_inc(sq_done, 1)

            def square_sums(post, k, unit, tt):
                if tt == 0:
                    act.wait_ge(tile0_done, k)
                else:
                    act.wait_ge(quad_used, 4 * unit)
                for nb in range(NB):
                    square_bank(post, tt, nb, acc[tt][nb][:, :], xn_big)

            def square_residual(n, k, tt, scratch):
                for nb in range(NB):
                    act.wait_ge(x_new, ((k - 1) * TT + tt) * NB + nb + 1)
                    square_bank(n, tt, nb, xt[:, tt, nb * BLK:(nb + 1) * BLK], scratch)

            def after_down(unit, post, n, k, gain, k0, scratch=xn_big):
                if post is not None:
                    square_sums(post, k, unit, 0)
                hi_unit(unit, js=(0, 1))
                square_residual(n, k, 0, scratch)
                if post is not None:
                    square_sums(post, k, unit, 1)
                act.wait_ge(quad_used, 4 * unit)
                h_hi(n, 0, gain, k0)
                square_residual(n, k, 1, scratch)
                h_hi(n, 1, gain, k0)
                hi_unit(unit, js=(2, 3))

            for tt in range(TT):
                act.wait_ge(mem_landed[tt], 16)
                square(N_MEM, tt, xn_big[:, tt, :], (u[:, :], tmp_big[:, 1, :])[tt])
            hi_unit(0, js=(0, 1), first=True)
            act.wait_ge(cols_ready, 1)
            for tt in range(TT):
                h_hi(N_MEM, tt, "norm_mem", 0)
            hi_unit(0, js=(2, 3), first=True)
            for tt in range(TT):
                act.wait_ge(x_landed[tt], 16)
                square(N_X, tt, xt[:, tt, :], xn_big[:, tt, :])
            hi_unit(1)
            evac(0, 0, u2[:, 0])
            hi_unit(U_DT, HEADS)
            h_hi(N_X, 0, "norm_pre", 0, 4 * U_DT - 3)
            evac(4, 1, u2[:, 1])
            h_hi(N_X, 1, "norm_pre", 0)
            for j in range(4):
                hi_bc(0, j)
            evac(4 * U_DT, 0, sp_tmp[0].rearrange("p (a h) -> p a h", a=TT), HEADS)
            act.wait_ge(small_landed, 48)
            nc.scalar.activation(a_log, a_log, ACT.Exp).then_inc(exp_done, 1)
            act.wait_ge(exp_asked, 1)
            nc.scalar.activation(sp_tmp[2], sp_tmp[2], ACT.Exp).then_inc(exp_done, 1)
            tb = TB["ssd"]

            def decays(g):
                act.wait_ge(diff_ready, g + 1)
                nc.scalar.activation(x[:, 0:2048], x[:, 0:2048], ACT.Exp).then_inc(decay_ready, 1)

            def states_out(uses):
                act.wait_ge(tf[0], uses)
                nc.scalar.activation(states, T[0][:, :], ACT.Copy).then_inc(te[0], 1)

            def y_out(g, after):
                for b in range(2):
                    act.wait_ge(tf[2 + b], after * 2 + tb[2 + b])
                    for c in range(2):
                        k = g * 4 + (2 * b + c)
                        ins = nc.scalar.activation(chunk(bigc, k), T2[2 + b][:, c, :], ACT.Copy, scale=col("ssd_norm_g", k))
                    ins.then_inc(te[2 + b], 1)

            def group(g, prev, nxt):
                q = g * 12 + 4 * U_SSD
                land = lambda k: g * 48 + landed(U_SSD + k)

                def hi_next(j):
                    if nxt:
                        hi_bc(g + 1, j)
                    else:
                        hi(4 * U_WOUT, landed(U_WOUT), j)

                for j in range(4):
                    hi(q + 4, land(1), j)
                evac(q, 0, u_bc, 2 * NST)
                if prev:
                    states_out(g * 4 + tb[0])
                else:
                    act.wait_ge(exp_asked, 2)
                    nc.scalar.activation(dte, dte, ACT.Exp).then_inc(exp_done, 1)
                    nc.scalar.activation(eacs, acs[:, 1, :], ACT.Exp).then_inc(exp_done, 1)
                for j in range(2):
                    hi(q + 8, land(2), j)
                act.wait_ge(tf[0], g * 4 + (tb[0] + 1))
                if prev:
                    act.wait_ge(tf[1], g * 4 + tb[1])
                for k in range(2):
                    c = g + (32 + 8 * k)
                    ins = nc.scalar.activation(bc[:, k, :], T2[0][:, k, :], ACT.Identity, bias=col("ssd_conv_b", c),
                                               scale=col("ssd_conv_w", c + (SSD_TAPS - 1) * CONV_CH))
                ins.then_inc(bc_tap, 1)
                hi(q + 8, land(2), 2)
                act.wait_ge(te[0], g * 4 + (tb[0] + 1))
                nc.scalar.activation(big[:, 10240:10752], big[:, 10240:10752], ACT.Silu).then_inc(bc_ready, 1)
                if prev:
                    y_out(g - 1, g)
                hi(q + 8, land(2), 3)
                evac(q + 4, 1, u_xs)
                hi_next(0)
                decays(g)
                hi_next(1)
                for b in range(2):
                    act.wait_ge(tf[b], g * 4 + (tb[b] + 2))
                for k in range(4):
                    c = g * 4 + k
                    ins = nc.scalar.activation(xc[:, k, :], T2[k // 2][:, k % 2, :], ACT.Identity, bias=col("ssd_conv_b", c),
                                               scale=col("ssd_conv_w", c + (SSD_TAPS - 1) * CONV_CH))
                ins.then_inc(xs_tap, 1)
                hi_next(2)
                act.wait_ge(te[1], g * 4 + (tb[1] + 2))
                nc.scalar.activation(big[:, 9216:10240], big[:, 9216:10240], ACT.Silu).then_inc(xc_ready, 1)
                hi_next(3)
                evac(q + 8, 0, zs, BLK, ACT.Silu)

            act.wait_ge(kv_stored, 32)
            group(0, False, True)
            with nc.scalar.Fori(0, GROUPS - 2) as i:
                group(i + 1, True, True)
            group(GROUPS - 1, True, False)
            states_out(GROUPS * 4 + tb[0])
            y_out(GROUPS - 1, GROUPS)
            down_first("wout", lambda j: act.wait_ge(te[3], tb[3] + 2 * GROUPS))
            down_rest("wout")
            after_down(U_XQ, N_P1, N_H1, 1, "norm_pre", KC)

            hi_unit(U_XO)
            evac(4 * U_XQ, 0, u2[:, 0], XW, ACT.Copy, SCALE)

            def exps(k, src, then):
                par = k % 2
                for tt in range(TT):
                    ins = nc.scalar.activation(prob[par][:, tt, :], src(tt), ACT.Exp,
                                               bias=mx[:, 2 * par + tt:2 * par + tt + 1],
                                               accum_out=den[:, 2 * par + tt:2 * par + tt + 1])
                ins.then_inc(then, 1)

            def prob_out(h, name, pv0):
                b = 2 + h % 2
                act.wait_ge(tf[b], TB[name][b] + h // 2 + 1)
                if h >= 2:
                    act.wait_ge(pv_done, pv0 + h - 1)
                nc.scalar.activation(probT[h % 2], T2[b], ACT.Copy).then_inc(te[b], 1)

            for h in range(XH + 1):
                if h < XH:
                    act.wait_ge(s_max, h + 1)
                    if h < 2:
                        act.wait_ge(tf[1], TB["xa"][1] + 1)
                    else:
                        act.wait_ge(tf[2 + h % 2], TB["xa"][2 + h % 2] + h // 2)
                    exps(h, lambda tt: T2[h % 2][:, tt, :], te[h % 2])
                if h >= 1:
                    prob_out(h - 1, "xa", 0)
            down_first("xo", lambda j: act.wait_ge(pv_taken, j + 1))
            after_down(U_UP1, N_P2, N_H2, 2, "norm_pre", 2 * KC)

            def ffn(n, down_name):
                unit, _, tb, cw, cb = FFN[n]
                m0 = (n - 1) * FB

                def gate_conv(i):
                    for b in range(2):
                        act.wait_ge(tf[b], i + (tb[b] + 1))
                    for k in range(4):
                        c = i * 4 + k
                        ins = nc.scalar.activation(chunk(bigc, c), T2[k // 2][:, k % 2, :], ACT.Identity, bias=col(cb, c),
                                                   scale=col(cw, c + (FFN_TAPS - 1) * 2 * FC))
                    ins.then_inc(gate_tap, 1)

                def gate_silu(i):
                    for b in range(2):
                        act.wait_ge(te[b], i + (tb[b] + 1))
                    g = big[:, bass.ds(i * (4 * L), 4 * L)]
                    nc.scalar.activation(g, g, ACT.Silu).then_inc(gate_act, 1)

                def val_conv(i, first):
                    for b in range(2, 4):
                        act.wait_ge(tf[b], i + (tb[b] + 1))
                    if not first:
                        act.wait_ge(ffn_mul, i + m0)
                    for k in range(4):
                        c = i * 4 + (k + FC)
                        ins = nc.scalar.activation(vbc[:, k, :], T2[2 + k // 2][:, k % 2, :], ACT.Identity, bias=col(cb, c),
                                                   scale=col(cw, c + (FFN_TAPS - 1) * 2 * FC))
                    ins.then_inc(val_tap, 1)

                def pair(i, prev, val_first=False):
                    q, land = i * 8 + 4 * unit, i * 32 + landed(unit)
                    for j in range(2):
                        hi(q + 4, land + 16, j)
                    if prev:
                        val_conv(i - 1, val_first)
                    for j in range(2, 4):
                        hi(q + 4, land + 16, j)
                    evac(q, 0, u2[:, 0])
                    for j in range(2):
                        hi(q + 8, land + 32, j)
                    gate_conv(i)
                    hi(q + 8, land + 32, 2)
                    gate_silu(i)
                    hi(q + 8, land + 32, 3)
                    evac(q + 4, 1, u2[:, 1])

                pair(0, False)
                pair(1, True, True)
                with nc.scalar.Fori(0, FB - 2) as i:
                    pair(i + 2, True)
                down_first(down_name, lambda j: act.wait_ge(ffn_mul, m0 + 1))
                val_conv(FB - 1, False)
                act.wait_ge(ffn_mul, m0 + FB)
                down_rest(down_name)

            ffn(1, "dn1")
            after_down(U_IN2, N_P3, N_1, 3, "norm1_g_2", 0)

            units = IN2_UNITS
            for k, (unit, kind, half_) in enumerate(units):
                if k + 1 < len(units) and units[k + 1][0] == U_ODD:
                    for j in range(4):
                        hi(4 * U_ODD, 48, j, ODD, odd_landed[j])
                else:
                    hi_unit(unit + 1)
                pr = k % 2
                if kind in IN2_SLOT:
                    s, turn = IN2_SLOT[kind], IN2_TURN[kind] + half_
                    if turn:
                        act.wait_ge(tf[2 * s + 1], TB["in2"][2 * s + 1] + IN2_USE[kind][1] + half_)
                    evac(4 * unit, pr, u2[:, s])
                elif kind == "odd":
                    act.wait_ge(m2_landed, 64)
                    evac(4 * unit, pr, odd, ODD)
                    act.wait_ge(proj_evac, E_ODD)
                    for tt in range(TT):
                        square(N_CKV, tt, odd[:, tt, 0:RANK], x[:, 3072 + RANK * tt:3072 + RANK * (tt + 1)])
                    act.wait_ge(exp_asked, 3)
                    nc.scalar.activation(fox_tmp[2], fox_tmp[2], ACT.Exp).then_inc(exp_done, 1)
                else:
                    evac(4 * unit, pr, bv[:, :, half_ * BLK:(half_ + 1) * BLK])

            for h in range(AH):
                b = h % 4
                act.wait_ge(tf[b], TB["qlat"][b] + h // 4 + 1)
                nc.scalar.activation(qlT[:, h], T2[b], ACT.Copy).then_inc(te[b], 1)
            for n in range(IH):
                b = n % 4
                act.wait_ge(tf[b], TB["idx"][b] + n // 4 + 1)
                if n >= 4:
                    act.wait_ge(relu_used, n - 3)
                nc.scalar.activation(rl[b], T2[b], ACT.Relu, scale=float(ID) ** -0.5).then_inc(te[b], 1)
            for name, k0 in (("fox", 0), ("dsa", BH)):
                for h in range(AH + 1):
                    if h < AH:
                        act.wait_ge(s_max, XH + k0 + h + 1)
                        exps(k0 + h, lambda tt: prob[h % 2][:, tt, :], p_exp)
                    if h >= 1:
                        prob_out(h - 1, name, XH + k0)
            down_first("wo2", lambda j: act.wait_ge(uv_taken, AH))
            down_rest("wo2")
            after_down(U_UP2, None, N_2, 4, "norm2_g_2", 0, tmp_big)
            ffn(2, "dn2")
            for tt in range(TT):
                square_residual(N_FIN, 5, tt, xn_big)

        @block.tensor
        def _(pe):
            def bank_free(b, uses):
                if not isinstance(uses, int) or uses:
                    pe.wait_ge(te[b], uses)

            def up(q, pair, n, evac_before, after=None, norm=None):
                for j in range(4):
                    if norm is not None:
                        pe.wait_ge(te[j], TB[norm][j] + 2)
                    if j == 0 and evac_before is not None:
                        pe.wait_ge(proj_evac, evac_before)
                    pe.wait_ge(lo_ready, q + j + 1)
                    wh, wl = quad(w_hi, j, n), quad(w_lo, j, n)
                    for c in range(4):
                        k = 4 * j + c
                        for tt in range(TT):
                            o = PB[2 * pair + tt][:, 0:n]
                            h, l = (t[:, k, tt * P:(tt + 1) * P] for t in (hT_hi, hT_lo))
                            nc.tensor.matmul(o, h, wh[:, c, :], start=(k == 0), stop=False)
                            nc.tensor.matmul(o, h, wl[:, c, :], start=False, stop=False)
                            ins = nc.tensor.matmul(o, l, wh[:, c, :], start=False, stop=(k == KC - 1))
                    ins.then_inc(quad_used, 1)
                    if after and j in after:
                        after[j]()

            def down(name, free, k):
                unit, xi, n, _ = DOWN[name]

                def tile(j, tt, first, last):
                    h, l = (t[:, j, tt * P:(tt + 1) * P] for t in (hT_hi, hT_lo))
                    for a, w in ((h, w_hi), (h, w_lo), (l, w_hi)):
                        for nb in range(NB):
                            ins = nc.tensor.matmul(acc[tt][nb][:, :], a, w[:, j, nb * BLK:(nb + 1) * BLK],
                                                   start=(first and j == 0 and a is h and w is w_hi),
                                                   stop=(last and j == 3 and a is l))
                    return ins

                def operands(q, xq, j):
                    pe.wait_ge(xs_lo, xq + j + 1)
                    pe.wait_ge(lo_ready, q + j + 1)

                def by_tile(q, xq, tiles, first, last):
                    for m, tt in enumerate(tiles):
                        if first:
                            free[tt]()
                        for j in range(4):
                            if m == 0:
                                operands(q, xq, j)
                            ins = tile(j, tt, first, last)
                            if m == 1:
                                ins.then_inc(quad_used, 1)
                        if last and m == 0:
                            ins.then_inc(tile0_done, 1)

                if n == 1:
                    by_tile(4 * unit, xi, (0, 1), True, True)
                else:
                    by_tile(4 * unit, xi, (1, 0), True, False)
                    with nc.tensor.Fori(0, n - 2) as i:
                        for j in range(4):
                            operands(i * 4 + 4 * (unit + 1), i * 4 + (xi + 4), j)
                            tile(j, 0, False, False)
                            tile(j, 1, False, False).then_inc(quad_used, 1)
                    by_tile(4 * (unit + n - 1), xi + 4 * (n - 1), (0, 1), False, True)

            def banks_free(phase):
                for b in range(4):
                    bank_free(b, TB[phase][b])

            def norm_transposes(n, src, tiles=range(TT)):
                for tt in tiles:
                    pe.wait_ge(diag_ready, TT * t_idx(n) + tt + 1)
                    for b in range(4):
                        bank_free(b, TB[n][b] + tt)
                        for c in range(4):
                            k = 4 * b + c
                            ins = nc.tensor.matmul(T[b][:, c * P:(c + 1) * P], src[:, tt, k * P:(k + 1) * P], diag[:, tt, :],
                                                   start=True, stop=True)
                        ins.then_inc(tf[b], 1)

            def turn_block(b0, uses, stage):
                for b in range(2):
                    bank_free(b0 + b, uses[b])
                    for c in range(2):
                        for tt in range(TT):
                            ins = nc.tensor.transpose(T2[b0 + b][:, c, tt * P:(tt + 1) * P],
                                                      stage[:, tt, (2 * b + c) * P:(2 * b + c + 1) * P], ident[:, :])
                    ins.then_inc(tf[b0 + b], 1)

            pe.wait_ge(consts_ready, 2)
            pe.wait_ge(rows_landed, 16 * N_ROW_LOADS)
            for r in range(NROWT):
                k = min(P, NCOL - r * P)
                ins = nc.tensor.transpose(T[r // 4][:, (r % 4) * P:(r % 4) * P + k], rows[0:k, r, :], ident[0:k, 0:k])
                if r % 4 == 3 or r == NROWT - 1:
                    ins.then_inc(tf[r // 4], 1)
            norm_transposes(N_MEM, xn_big)

            def turn_keys():
                pe.wait_ge(proj_evac, E_KV)
                turn_block(0, TB["kv"], u2[:, 0])

            up(0, 0, BLK, None, norm=N_MEM)
            up(4, 1, BLK, None, {1: turn_keys, 2: lambda: norm_transposes(N_X, xt, (0,))})
            norm_transposes(N_X, xt, (1,))
            up(4 * U_DT, 0, HEADS, E_KV, norm=N_X)
            tb = TB["ssd"]

            def cumulative_sums():
                pe.wait_ge(da_ready, 1)
                bank_free(2, TB["dt"][2])
                for c in range(TT):
                    nc.tensor.matmul(T[2][:, c * HEADS:(c + 1) * HEADS], triu[:, :], da[:, c, :], start=True, stop=True)
                nc.tensor.matmul(T[2][:, TT * HEADS:(TT + 1) * HEADS], ones[:, :], da[:, 0, :], start=True, stop=True)\
                    .then_inc(tf[2], 1)
                bank_free(3, TB["dt"][3])
                for c in range(TT):
                    ins = nc.tensor.matmul(T[3][0:HEADS, c * P:(c + 1) * P], da[:, c, :], triu[:, :], start=True, stop=True)
                ins.then_inc(tf[3], 1)

            def turn_bc(g):
                pe.wait_ge(proj_evac, g * 3 + E_SSD)
                bank_free(0, g * 4 + tb[0])
                for k in range(2):
                    for tt in range(TT):
                        ins = nc.tensor.transpose(T2[0][:, k, tt * P:(tt + 1) * P], u_bc[:, tt, k * NST:(k + 1) * NST], ident[:, :])
                ins.then_inc(tf[0], 1)

            def cb_products(g):
                pe.wait_ge(bc_ready, g + 1)
                bank_free(1, g * 4 + tb[1])
                for c in range(TT):
                    nc.tensor.matmul(T[1][:, c * P:(c + 1) * P], bc[:, 0, c * P:(c + 1) * P], bc[:, 1, c * P:(c + 1) * P],
                                     start=True, stop=True)
                nc.tensor.transpose(T[1][:, TT * P:(TT + 1) * P], bc[:, 0, 0:P], ident[:, :]).then_inc(tf[1], 1)

            def turn_xs(g):
                pe.wait_ge(proj_evac, g * 3 + (E_SSD + 1))
                turn_block(0, [g * 4 + (tb[b] + 1) for b in range(2)], u_xs)

            def back_xs(g):
                pe.wait_ge(xc_ready, g + 1)
                for tt in range(TT):
                    bank_free(tt, g * 4 + (tb[tt] + 2))
                    for k in range(4):
                        ins = nc.tensor.transpose(T[tt][:, k * P:(k + 1) * P], xc[:, k, tt * P:(tt + 1) * P], ident[:, :])
                    ins.then_inc(tf[tt], 1)

            def states_and_diagonal(g):
                pe.wait_ge(bd_ready, g + 1)
                bank_free(0, g * 4 + (tb[0] + 3))
                nc.tensor.matmul(T[0][:, :], bm, bd, start=True, stop=True).then_inc(tf[0], 1)
                pe.wait_ge(m_ready, g + 1)
                for c in range(TT):
                    bank_free(2 + c, g * 2 + tb[2 + c])
                    for h in range(HPG):
                        ins = nc.tensor.matmul(T[2 + c][:, h * HD:(h + 1) * HD], ssd_m[:, h, c * P:(c + 1) * P],
                                               xdt[:, c, h * HD:(h + 1) * HD], start=True, stop=True)
                    ins.then_inc(tf[2 + c], 1)

            def from_states(g):
                pe.wait_ge(te[0], g * 4 + (tb[0] + 4))
                bank_free(1, g * 4 + (tb[1] + 3))
                nc.tensor.matmul(T[1][:, :], bc[:, 1, P:2 * P], states, start=True, stop=True).then_inc(tf[1], 1)

            def turn_y(g):
                pe.wait_ge(yg_ready, g + 1)
                turn_block(2, [g * 2 + (tb[2 + b] + 1) for b in range(2)], yg)

            def group(g, prev):
                q = g * 12 + 4 * U_SSD
                late = (lambda f: lambda: f(g - 1)) if prev else (lambda f: lambda: None)
                up(q, 0, 2 * NST, g * 3 + (E_SSD - 1), {1: late(back_xs), 3: late(states_and_diagonal)})
                if not prev:
                    cumulative_sums()
                up(q + 4, 1, BLK, g * 3 + (E_SSD - 2), {0: late(from_states), 1: lambda: turn_bc(g), 2: late(turn_y)})
                up(q + 8, 0, BLK, g * 3 + E_SSD, {0: lambda: cb_products(g), 1: lambda: turn_xs(g)})

            group(0, False)
            with nc.tensor.Fori(0, GROUPS - 1) as i:
                group(i + 1, True)
            last = GROUPS - 1
            back_xs(last)
            states_and_diagonal(last)
            from_states(last)
            turn_y(last)

            down("wout", [lambda: banks_free(N_H1), lambda: pe.wait_ge(proj_evac, E_SSD + 3 * GROUPS - 1)], 1)
            norm_transposes(N_H1, xt)
            up(4 * U_XQ, 0, XW, None, norm=N_H1)
            pe.wait_ge(proj_evac, E_XQ)
            turn_block(0, TB["xa"], u2[:, 0])
            pe.wait_ge(kv_loaded, 32)

            def turn_probs(h, name, k):
                b = 2 + h % 2
                pe.wait_ge(p_ready, k + 1)
                bank_free(b, TB[name][b] + h // 2)
                for s in range(2):
                    for tt in range(TT):
                        ins = nc.tensor.transpose(T2[b][:, s, tt * P:(tt + 1) * P], prob[h % 2][:, tt, s * P:(s + 1) * P], ident[:, :])
                ins.then_inc(tf[b], 1)

            def weighted(h, name, k, vals, parts=1):
                pe.wait_ge(te[2 + h % 2], TB[name][2 + h % 2] + h // 2 + 1)
                if h >= 2:
                    pe.wait_ge(pv_taken, k - 1)
                for r in range(parts):
                    for s in range(2):
                        ins = nc.tensor.matmul(PB[h % 2][:, r * L:(r + 1) * L], vals(s, r), probT[h % 2][:, s, :],
                                               start=(s == 0), stop=(s == 1))
                ins.then_inc(pv_done, 1)

            for b in range(2):
                pe.wait_ge(te[b], TB["xa"][b] + 1)
            for h in range(XH + 2):
                if h < XH:
                    b = h % 2
                    bank_free(b, TB["xa"][b] + 1 + h // 2)
                    for tt in range(TT):
                        ins = nc.tensor.matmul(T2[b][:, tt, :], xa_qT[:, h, tt * P:(tt + 1) * P], xa_kT[:, h, :], start=True, stop=True)
                    ins.then_inc(tf[b], 1)
                if 1 <= h <= XH:
                    turn_probs(h - 1, "xa", h - 1)
                if h >= 2:
                    weighted(h - 2, "xa", h - 2, lambda s, r: xa_v[:, s, (h - 2) * P:(h - 1) * P])

            down("xo", [lambda: banks_free(N_H2), lambda: pe.wait_ge(pv_taken, XH)], 2)
            norm_transposes(N_H2, xt)

            def ffn(n, norm, down_name, done, down_k):
                unit, e0, tb, _, _ = FFN[n]

                def turn(i, val):
                    pe.wait_ge(proj_evac, i * 2 + (e0 + val))
                    turn_block(2 * val, [i + tb[2 * val + b] for b in range(2)], u2[:, val])

                def pair(i, first):
                    q = i * 8 + 4 * unit
                    up(q, 0, BLK, None if first else i * 2 + (e0 - 2), None if first else {1: lambda: turn(i - 1, 1)},
                       norm if first else None)
                    up(q + 4, 1, BLK, None if first else i * 2 + (e0 - 1), {1: lambda: turn(i, 0)})

                pair(0, True)
                with nc.tensor.Fori(0, FB - 1) as i:
                    pair(i + 1, False)
                turn(FB - 1, 1)

                down(down_name, [lambda: banks_free(done), lambda: pe.wait_ge(proj_evac, e0 + 2 * FB - 1)], down_k)

            ffn(1, N_H2, "dn1", N_1, 3)
            norm_transposes(N_1, xt)

            units = IN2_UNITS

            def turn_unit(k):
                unit, kind, half_ = units[k]
                pe.wait_ge(proj_evac, E_IN2 + k)
                s = IN2_SLOT[kind]
                turn_block(2 * s, [TB["in2"][2 * s + b] + IN2_USE[kind][b] + half_ for b in range(2)], u2[:, s])

            def turn_odd():
                pe.wait_ge(odd_ready, 1)
                bank_free(0, TB["in2"][0] + 2)
                for r in range(2):
                    for tt in range(TT):
                        ins = nc.tensor.transpose(T2[0][:, r, tt * P:(tt + 1) * P], ckv[:, tt, r * P:(r + 1) * P], ident[:, :])
                ins.then_inc(tf[0], 1)
                bank_free(1, TB["in2"][1] + 2)
                for tt in range(TT):
                    ins = nc.tensor.transpose(T[1][:, tt * P:(tt + 1) * P], aik2[:, tt].rearrange("p k n -> p (k n)"), ident[:, :])
                ins.then_inc(tf[1], 1)
                bank_free(2, TB["in2"][2] + 2)
                c = T[2][0:BH, :]
                nc.tensor.matmul(c[:, 0:P], lf[:, 0, :], triu[:, :], start=True, stop=True)
                nc.tensor.matmul(c[:, P:L], lf[:, 0, :], ones[:, :], start=True, stop=False)
                nc.tensor.matmul(c[:, P:L], lf[:, 1, :], triu[:, :], start=False, stop=True).then_inc(tf[2], 1)

            for k, (unit, kind, half_) in enumerate(units):
                after = {}
                if k and units[k - 1][1] in IN2_SLOT:
                    after[1] = lambda k=k: turn_unit(k - 1)
                if k and units[k - 1][1] == "odd":
                    after[3] = turn_odd
                up(4 * unit, k % 2, ODD if kind == "odd" else BLK, E_IN2 + k - 2 if k >= 2 else None, after,
                   N_1 if k == 0 else None)
            pe.wait_ge(m2_landed, 64)
            bank_free(3, TB["line"][3])
            nc.tensor.matmul(T[3][0:AH, :], table, onehot, start=True, stop=True).then_inc(tf[3], 1)
            pe.wait_ge(uk_landed, 16)
            pe.wait_ge(te[0], TB["in2"][0] + 5)
            for h in range(AH):
                b = h % 4
                bank_free(b, TB["qlat"][b] + h // 4)
                for r in range(2):
                    ins = nc.tensor.matmul(T2[b][:, r, :], w_uk[:, h, r * P:(r + 1) * P], aqT[:, h, :], start=True, stop=True)
                ins.then_inc(tf[b], 1)
            for n in range(IH):
                b = n % 4
                bank_free(b, TB["idx"][b] + n // 4)
                half_ = slice(n % 2 * ID, n % 2 * ID + ID)
                for tt in range(TT):
                    ins = nc.tensor.matmul(T2[b][:, tt, :], aiqT[half_, n // 2, tt * P:(tt + 1) * P], aikT[half_, :], start=True, stop=True)
                ins.then_inc(tf[b], 1)
            pe.wait_ge(proj_evac, E_IN2 + len(units) - 1)
            for h in range(BH + 2):
                if h < BH:
                    b = h % 2
                    bank_free(b, TB["fox"][b] + h // 2)
                    pe.wait_ge(cum_row_ready, h + 1)
                    for tt in range(TT):
                        nc.tensor.matmul(T2[b][:, tt, :], bqT[:, h, tt * P:(tt + 1) * P], bkT[:, h, :], start=True, stop=False)
                        ins = nc.tensor.matmul(T2[b][:, tt, :], ones[0:BH, :], cum_row, start=False, stop=True)
                    ins.then_inc(tf[b], 1)
                if 1 <= h <= BH:
                    turn_probs(h - 1, "fox", XH + h - 1)
                if h >= 2:
                    weighted(h - 2, "fox", XH + h - 2, lambda s, r: bv[:, s, (h - 2) * P:(h - 1) * P])
            pe.wait_ge(uv_landed, 16)
            pe.wait_ge(skew_landed, 16)
            pe.wait_ge(m2_consts, 2)
            pe.wait_ge(pv_taken, XH + BH)
            for h in range(AH + 3):
                if h < AH:
                    b = h % 2
                    bank_free(b, TB["dsa"][b] + h // 2)
                    for tt in range(TT):
                        for r in range(2):
                            nc.tensor.matmul(T2[b][:, tt, :], qlT[:, h, r, tt * P:(tt + 1) * P], ckvT[:, r, :], start=(r == 0), stop=False)
                        ins = nc.tensor.matmul(T2[b][:, tt, :], anti, skew[:, h, (1 - tt) * P:(1 - tt) * P + L], start=False, stop=True)
                    ins.then_inc(tf[b], 1)
                if 1 <= h <= AH:
                    turn_probs(h - 1, "dsa", XH + BH + h - 1)
                if 2 <= h <= AH + 1:
                    weighted(h - 2, "dsa", XH + BH + h - 2, lambda s, r: ckv[:, s, r * P:(r + 1) * P], 2)
                if h >= 3:
                    g = h - 3
                    pe.wait_ge(pv_taken, XH + BH + g + 1)
                    if g >= 2:
                        pe.wait_ge(uv_taken, g - 1)
                    for r in range(2):
                        ins = nc.tensor.matmul(PB[2 + g % 2][:, 0:L], w_uv[:, g, r, :], o_lat[:, r, :], start=(r == 0), stop=(r == 1))
                    ins.then_inc(uv_done, 1)

            down("wo2", [lambda: banks_free(N_2), lambda: pe.wait_ge(uv_taken, AH)], 4)
            norm_transposes(N_2, xt)
            ffn(2, N_2, "dn2", "end", 5)

        @block.vector
        def _(dve):
            own = Chain(dve, dve_own)
            V = nc.vector
            marks = iter(range(1, idle.shape[1]))

            def signal(semaphore):
                k = next(marks)
                V.memset(idle[:, k:k + 1], 0.0).then_inc(semaphore, 1)

            def lo(q, j, n=4 * BLK):
                dve.wait_ge(hi_ready, q + j + 1)
                dst, src, h = (w_lo[:, j, :], raw[:, j, :], w_hi[:, j, :]) if n == 4 * BLK else \
                    (quad(w_lo, j, n), quad(raw, j, n), quad(w_hi, j, n))
                V.tensor_tensor(dst, src, h.bitcast(F32), ALU.subtract).then_inc(lo_ready, 1)

            def lo_unit(unit, n=4 * BLK, js=range(4)):
                for j in js:
                    lo(4 * unit, j, n)

            def mean(n, tt, width):
                s = ssq(n)[:, tt:tt + 1]
                V.tensor_scalar(s, s, 1.0 / width, EPS, ALU.mult, ALU.add).then_inc(ms_done, 1)

            def means(n, width):
                for tt in range(TT):
                    dve.wait_ge(sq_done, sq_count(n, tt))
                    mean(n, tt, width)

            def bank_sums(n, tt):
                dve.wait_ge(sq_done, sq_count(n, tt))
                own(V.tensor_reduce(ssq(n)[:, tt:tt + 1], ssq_parts[:, tt * NB:(tt + 1) * NB], AX_X, ALU.add))

            def h_lo(n, tt, gain, k0):
                for b in range(4):
                    dve.wait_ge(h_hi_done, 8 * t_idx(n) + 4 * tt + b + 1)
                    for c in range(4):
                        k = 4 * b + c
                        s = slice(tt * P, (tt + 1) * P)
                        ins = V.scalar_tensor_tensor(hT_lo[:, k, s], T[b][:, c * P:(c + 1) * P], col(gain, k0 + k),
                                                     hT_hi[:, k, s].bitcast(F32), ALU.mult, ALU.subtract)
                    ins.then_inc(te[b], 1)

            def down_first(name):
                _, xi, _, src = DOWN[name]
                for j in range(4):
                    dve.wait_ge(xs_hi, xi + j + 1)
                    V.tensor_tensor(hT_lo[:, j, :], src[:, j, :], hT_hi[:, j, :].bitcast(F32), ALU.subtract).then_inc(xs_lo, 1)

            def down_rest(name):
                unit, xi, n, src = DOWN[name]
                with V.Fori(0, n - 1) as i:
                    for j in range(4):
                        lo(i * 4 + 4 * (unit + 1), j)
                        dve.wait_ge(xs_hi, i * 4 + (xi + 4 + j + 1))
                        V.tensor_tensor(hT_lo[:, j, :], chunk(src, i * 4 + (4 + j)), hT_hi[:, j, :].bitcast(F32), ALU.subtract)\
                            .then_inc(xs_lo, 1)

            def branch_added(post, tt, k, scale):
                s1, r1 = ssq(post)[:, tt:tt + 1], rstd(post)[:, tt:tt + 1]
                bank_sums(post, tt)
                if scale is not None:
                    own(V.tensor_tensor(s1, s1, scale[:, tt:tt + 1], ALU.mult))
                    own(V.tensor_tensor(s1, s1, scale[:, tt:tt + 1], ALU.mult))
                mean(post, tt, D)
                dve.wait_ge(rstd_done, nth(post, tt))
                if scale is not None:
                    own(V.tensor_tensor(r1, r1, scale[:, tt:tt + 1], ALU.mult))
                dve.wait_ge(gain_landed, 16 * k)
                for nb in range(NB):
                    s = slice(nb * BLK, (nb + 1) * BLK)
                    own(V.scalar_tensor_tensor(tmp_big[:, tt, s], acc[tt][nb][:, :], r1, u[:, s], ALU.mult, ALU.mult))
                    V.tensor_tensor(xt[:, tt, s], xt[:, tt, s], tmp_big[:, tt, s], ALU.add).then_inc(x_new, 1)

            def product_added(tt, k, unit, src):
                if tt == 0:
                    dve.wait_ge(tile0_done, k)
                else:
                    dve.wait_ge(quad_used, 4 * unit)
                for nb in range(NB):
                    s = slice(nb * BLK, (nb + 1) * BLK)
                    V.tensor_tensor(xt[:, tt, s], acc[tt][nb][:, :], src[:, tt, s], ALU.add).then_inc(x_new, 1)

            def after_down(unit, add, n, gain, k0):
                for tt in range(TT):
                    add(tt)
                    bank_sums(n, tt)
                    mean(n, tt, D)
                    if tt == 0:
                        lo_unit(unit, js=(0, 1))
                for tt in range(TT):
                    h_lo(n, tt, gain, k0)
                lo_unit(unit, js=(2, 3))

            def softplus(tmp, ask):
                terms = 7
                own(V.tensor_scalar(tmp[1], tmp[0], 0.0, None, ALU.max))
                V.scalar_tensor_tensor(tmp[2], tmp[0], -1.0, tmp[0], ALU.mult, ALU.min).then_inc(exp_asked, 1)
                dve.wait_ge(exp_done, ask)
                own(V.tensor_scalar(tmp[3], tmp[2], 2.0, None, ALU.add))
                own(V.reciprocal(tmp[4], tmp[3]))
                own(V.tensor_tensor(tmp[5], tmp[2], tmp[4], ALU.mult))
                own(V.tensor_tensor(tmp[6], tmp[5], tmp[5], ALU.mult))
                own(V.tensor_scalar(tmp[7], tmp[6], 1.0 / (2 * terms + 1), None, ALU.mult))
                for k in range(terms - 1, 0, -1):
                    own(V.scalar_tensor_tensor(tmp[7], tmp[7], 1.0 / (2 * k + 1), tmp[6], ALU.add, ALU.mult))
                own(V.scalar_tensor_tensor(tmp[7], tmp[7], 1.0, tmp[5], ALU.add, ALU.mult))
                own(V.scalar_tensor_tensor(tmp[0], tmp[7], 2.0, tmp[1], ALU.mult, ALU.add))

            def tap(dst, src, shift, w):
                return V.scalar_tensor_tensor(dst[:, shift:L], src[:, 0:L - shift], w, dst[:, shift:L], ALU.mult, ALU.add)

            for b in range(3):
                dve.wait_ge(tf[b], 1)
                n = min(BLK, NCOL - b * BLK)
                V.tensor_copy(cols[:, b * BLK:b * BLK + n], T[b][:, 0:n]).then_inc(te[b], 1)
            dve.wait_ge(te[2], 1)
            signal(cols_ready)
            means(N_MEM, D)
            lo_unit(0, js=(0, 1))
            for tt in range(TT):
                h_lo(N_MEM, tt, "norm_mem", 0)
            lo_unit(0, js=(2, 3))
            means(N_X, D)
            lo_unit(1)
            for b in range(2):
                dve.wait_ge(tf[b], TB["kv"][b] + 1)
                own(V.tensor_copy(vbc[:, 2 * b:2 * b + 2, :], T2[b]))
                signal(te[b])
            signal(kT_copied)
            lo_unit(U_DT, HEADS)
            for tt in range(TT):
                h_lo(N_X, tt, "norm_pre", 0)
            for j in range(4):
                lo(4 * U_SSD, j, 2 * NST)

            dve.wait_ge(proj_evac, E_DT)
            dve.wait_ge(small_landed, 48)
            dve.wait_ge(kv_stored, 32)
            own(V.memset(yssq[:, 0, :], 0.0))
            t0 = sp_tmp[0].rearrange("p (a h) -> p a h", a=TT)
            own(V.tensor_tensor(t0, t0, dt_bias.unsqueeze(1).broadcast_to([P, TT, HEADS]), ALU.add))
            softplus(sp_tmp, 2)
            own(V.tensor_copy(vb[:, 0:128], sp_tmp[0]))
            V.scalar_tensor_tensor(da, dt, -1.0, a_log.unsqueeze(1).broadcast_to([P, TT, HEADS]), ALU.mult, ALU.mult)\
                .then_inc(da_ready, 1)

            def sums():
                dve.wait_ge(tf[2], TB["dt"][2] + 1)
                own(V.tensor_copy(vb[:, 256:384], T[2][:, 0:128]))
                own(V.tensor_tensor(dte, T[2][:, 128:192], acs[:, 0, :], ALU.subtract))
                signal(te[2])
                signal(exp_asked)
                dve.wait_ge(tf[3], TB["dt"][3] + 1)
                own(V.tensor_copy(acsT, T[3][0:HEADS, 0:L]))
                signal(te[3])
                signal(acsT_ready)
                dve.wait_ge(exp_done, 4)

            tb = TB["ssd"]

            def by_head(a, g, n=HPG):
                return a[:, bass.ds(g * HPG, HPG)].unsqueeze(2).broadcast_to([P, HPG, HD])

            heads = lambda a: a.rearrange("p (h d) -> p h d", d=HD)

            def bc_taps(g):
                dve.wait_ge(bc_tap, g + 1)
                for t in range(SSD_TAPS - 2, -1, -1):
                    for k in range(2):
                        ins = tap(bc[:, k, :], T2[0][:, k, :], SSD_TAPS - 1 - t, col("ssd_conv_w", g + (32 + 8 * k + t * CONV_CH)))
                    if t:
                        own(ins)
                ins.then_inc(te[0], 1)

            def xs_taps(g):
                dve.wait_ge(xs_tap, g + 1)
                for t in range(SSD_TAPS - 2, -1, -1):
                    for k in range(4):
                        ins = tap(xc[:, k, :], T2[k // 2][:, k % 2, :], SSD_TAPS - 1 - t, col("ssd_conv_w", g * 4 + (k + t * CONV_CH)))
                        if t == 0 and k % 2:
                            ins.then_inc(te[k // 2], 1)
                    if t:
                        own(ins)

            def cb_out(g):
                dve.wait_ge(tf[1], g * 4 + (tb[1] + 1))
                V.tensor_tensor(cbm, T[1][:, 0:2 * P].rearrange("p (a t) -> p a t", a=TT),
                                triu[:, :].unsqueeze(1).broadcast_to([P, TT, P]), ALU.mult)
                V.tensor_copy(bm, T[1][:, 2 * P:3 * P]).then_inc(te[1], 1)

            def decayed(g):
                dve.wait_ge(te[1], g * 4 + (tb[1] + 1))
                dve.wait_ge(decay_ready, g + 1)
                for c in range(TT):
                    m = ssd_m[:, :, c * P:(c + 1) * P]
                    ins = V.tensor_tensor(m, m, cbm[:, c, :].unsqueeze(1).broadcast_to([P, HPG, P]), ALU.mult)
                ins.then_inc(m_ready, 1)

            def xs_back(g, first):
                for tt in range(TT):
                    dve.wait_ge(tf[tt], g * 4 + (tb[tt] + 3))
                    if not first:
                        dve.wait_ge(tf[2 + tt], g * 2 + tb[2 + tt])
                for tt in range(TT):
                    V.tensor_tensor(heads(xdt[:, tt, :]), heads(T[tt][:, :]), by_head(dt[:, tt, :], g), ALU.mult)
                    ins = V.tensor_tensor(heads(yg[:, tt, :]), heads(T[tt][:, :]), by_head(d_skip, g), ALU.mult)
                    ins.then_inc(te[tt], 1)
                dve.wait_ge(te[1], g * 4 + (tb[1] + 3))
                V.tensor_tensor(heads(bd), heads(xdt[:, 0, :]), by_head(dte, g), ALU.mult).then_inc(bd_ready, 1)

            def gather(g):
                dve.wait_ge(tf[1], g * 4 + (tb[1] + 4))
                V.tensor_tensor(heads(bd), heads(T[1][:, :]), by_head(eacs, g), ALU.mult).then_inc(te[1], 1)
                dve.wait_ge(te[1], g * 4 + (tb[1] + 4))
                own(V.tensor_tensor(bd, bd, yg[:, 1, :], ALU.add))
                for c in range(TT):
                    dve.wait_ge(tf[2 + c], g * 2 + (tb[2 + c] + 1))
                    V.tensor_tensor(yg[:, c, :], T[2 + c][:, :], (yg[:, 0, :], bd)[c], ALU.add).then_inc(te[2 + c], 1)
                dve.wait_ge(proj_evac, g * 3 + (E_SSD + 2))
                for c in range(TT):
                    dve.wait_ge(te[2 + c], g * 2 + (tb[2 + c] + 1))
                V.tensor_tensor(yg, yg, zs, ALU.mult).then_inc(yg_ready, 1)
                dve.wait_ge(yg_ready, g + 1)
                for c in range(TT):
                    own(V.tensor_tensor_reduce(bd, yg[:, c, :], yg[:, c, :], 1.0, 0.0, ALU.mult, ALU.add,
                                               accum_out=yssq[:, 1, c:c + 1]))
                own(V.tensor_tensor(yssq[:, 0, :], yssq[:, 0, :], yssq[:, 1, :], ALU.add))

            def group(g, prev, nxt, first=False):
                q = g * 12 + 4 * U_SSD

                def lo_next(j):
                    if nxt:
                        lo(q + 12, j, 2 * NST)
                    else:
                        lo(4 * U_WOUT, j)

                for j in range(4):
                    lo(q + 4, j)
                    if j == 1 and prev:
                        xs_back(g - 1, first)
                if not prev:
                    sums()
                lo(q + 8, 0)
                if prev:
                    gather(g - 1)
                lo(q + 8, 1)
                bc_taps(g)
                lo(q + 8, 2)
                lo(q + 8, 3)
                lo_next(0)
                cb_out(g)
                lo_next(1)
                xs_taps(g)
                lo_next(2)
                decayed(g)
                lo_next(3)

            group(0, False, True)
            group(1, True, True, True)
            with V.Fori(0, GROUPS - 3) as i:
                own.enter(i, 8)
                group(i + 2, True, True)
            own.leave(GROUPS - 3)
            group(GROUPS - 1, True, False)
            xs_back(GROUPS - 1, False)
            gather(GROUPS - 1)
            own(V.tensor_copy(ssq(N_Y), yssq[:, 0, :]))
            for tt in range(TT):
                mean(N_Y, tt, DI)
            down_first("wout")
            down_rest("wout")
            dve.wait_ge(rstd_done, nth(N_Y, TT - 1))
            dve.wait_ge(x_back, 16)
            after_down(U_XQ, lambda tt: branch_added(N_P1, tt, 1, rstd(N_Y)), N_H1, "norm_pre", KC)

            lo_unit(U_XO)
            for b in range(2):
                dve.wait_ge(tf[b], TB["xa"][b] + 1)
                V.tensor_copy(xa_qT[:, 2 * b:2 * b + 2, :], T2[b]).then_inc(te[b], 1)

            def scale_probs(k):
                par = k % 2
                own(V.reciprocal(rden[:, 2 * par:2 * par + 2], den[:, 2 * par:2 * par + 2]))
                for tt in range(TT):
                    ins = V.tensor_scalar(prob[par][:, tt, :], prob[par][:, tt, :], rden[:, 2 * par + tt:2 * par + tt + 1], None, ALU.mult)
                ins.then_inc(p_ready, 1)

            for h in range(XH + 2):
                if h < XH:
                    b = h % 2
                    dve.wait_ge(tf[b], TB["xa"][b] + 1 + h // 2 + 1)
                    V.tensor_reduce(mx[:, 2 * b:2 * b + 2], T2[b], AX_X, ALU.max, negate=True).then_inc(s_max, 1)
                if 1 <= h <= XH:
                    b = (h - 1) % 2
                    dve.wait_ge(te[b], TB["xa"][b] + 1 + (h - 1) // 2 + 1)
                    scale_probs(h - 1)
                if h >= 2:
                    dve.wait_ge(pv_done, h - 1)
                    V.tensor_copy(xa_oT[:, h - 2, :], PB[h % 2][:, 0:L]).then_inc(pv_taken, 1)
            down_first("xo")
            after_down(U_UP1, lambda tt: branch_added(N_P2, tt, 2, None), N_H2, "norm_pre", 2 * KC)

            def ffn(n, down_name):
                unit, _, tb, cw, cb = FFN[n]
                m0 = (n - 1) * FB

                def gate_taps(i):
                    dve.wait_ge(gate_tap, i + (m0 + 1))
                    for t in range(FFN_TAPS - 2, -1, -1):
                        for k in range(4):
                            c = i * 4 + k
                            ins = tap(chunk(bigc, c), T2[k // 2][:, k % 2, :], FFN_TAPS - 1 - t, col(cw, c + t * 2 * FC))
                            if t == 0 and k % 2:
                                ins.then_inc(te[k // 2], 1)
                        if t:
                            own(ins)

                def val_taps(i):
                    dve.wait_ge(val_tap, i + (m0 + 1))
                    for t in range(FFN_TAPS - 2, -1, -1):
                        for k in range(4):
                            ins = tap(vbc[:, k, :], T2[2 + k // 2][:, k % 2, :], FFN_TAPS - 1 - t, col(cw, i * 4 + (k + FC + t * 2 * FC)))
                            if t == 0 and k % 2:
                                ins.then_inc(te[2 + k // 2], 1)
                        if t:
                            own(ins)
                    dve.wait_ge(te[3], i + (tb[3] + 1))
                    dve.wait_ge(gate_act, i + (m0 + 1))
                    g = big[:, bass.ds(i * (4 * L), 4 * L)]
                    V.tensor_tensor(g, g, vb[:, :], ALU.mult).then_inc(ffn_mul, 1)

                def pair(i, prev):
                    q = i * 8 + 4 * unit
                    for j in range(4):
                        lo(q + 4, j)
                        if j == 1 and prev:
                            val_taps(i - 1)
                    for j in range(4):
                        lo(q + 8, j)
                        if j == 1:
                            gate_taps(i)

                pair(0, False)
                with V.Fori(0, FB - 1) as i:
                    own.enter(i, 2)
                    pair(i + 1, True)
                own.leave(FB - 1)
                down_first(down_name)
                val_taps(FB - 1)
                dve.wait_ge(ffn_mul, m0 + FB)
                down_rest(down_name)

            ffn(1, "dn1")
            after_down(U_IN2, lambda tt: branch_added(N_P3, tt, 3, None), N_1, "norm1_g_2", 0)

            units = IN2_UNITS
            dest = {"aq": aqT, "aiq": aiqT, "bq": bqT, "bk": bkT}
            factor = {"aq": SCALE, "bq": SCALE}

            def unit_out(k):
                unit, kind, half_ = units[k]
                s = IN2_SLOT[kind]
                for b in range(2):
                    t = 2 * s + b
                    dve.wait_ge(tf[t], TB["in2"][t] + IN2_USE[kind][b] + half_ + 1)
                    c = 4 * half_ + 2 * b
                    V.tensor_scalar(dest[kind][:, c:c + 2, :], T2[t], factor.get(kind, 1.0), None, ALU.mult).then_inc(te[t], 1)

            def odd_in():
                dve.wait_ge(proj_evac, E_ODD)
                for tt in range(TT):
                    for k in range(2):
                        V.tensor_copy(aik2[:, tt, k, :], odd[:, tt, RANK:RANK + ID])
                V.tensor_scalar(iw, odd[:, :, RANK + ID:RANK + ID + IH], float(IH) ** -0.5, None, ALU.mult)
                f0 = fox_tmp[0].rearrange("p (a h) -> p a h", a=TT)
                own(V.scalar_tensor_tensor(f0, odd[:, :, RANK + ID + IH:ODD], -1.0,
                                           fg_bias.unsqueeze(1).broadcast_to([P, TT, BH]), ALU.mult, ALU.subtract))
                softplus(fox_tmp, 5)
                own(V.tensor_copy(x[:, 2560:2576], fox_tmp[0]))
                means(N_CKV, RANK)
                dve.wait_ge(rstd_done, nth(N_CKV, TT - 1))
                for tt in range(TT):
                    ins = V.scalar_tensor_tensor(ckv[:, tt, :], odd[:, tt, 0:RANK], rstd(N_CKV)[:, tt:tt + 1], kv_gain, ALU.mult, ALU.mult)
                ins.then_inc(odd_ready, 1)

            def odd_out():
                dve.wait_ge(tf[0], TB["in2"][0] + 3)
                V.tensor_copy(ckvT, T2[0]).then_inc(te[0], 1)
                dve.wait_ge(tf[1], TB["in2"][1] + 3)
                V.tensor_copy(aikT, T[1][:, 0:L]).then_inc(te[1], 1)
                dve.wait_ge(tf[2], TB["in2"][2] + 3)
                own(V.tensor_copy(cumT, T[2][0:BH, 0:L]))
                signal(te[2])
                signal(decay_sum_ready)

            dve.wait_ge(m2_landed, 64)
            for k, (unit, kind, half_) in enumerate(units):
                nxt = ODD if unit + 1 == U_ODD else 4 * BLK
                for j in range(4):
                    lo(4 * (unit + 1), j, nxt)
                    if j == 1 and k and units[k - 1][1] in IN2_SLOT:
                        unit_out(k - 1)
                if kind == "odd":
                    odd_in()
                if k and units[k - 1][1] == "odd":
                    odd_out()
            dve.wait_ge(tf[3], TB["line"][3] + 1)
            own(V.tensor_copy(line, T[3][0:AH, :]))
            signal(te[3])
            signal(line_ready)

            for n in range(IH):
                dve.wait_ge(te[n % 4], TB["idx"][n % 4] + n // 4 + 1)
                if n:
                    dve.wait_ge(relu_used, n)
                for tt in range(TT):
                    w = iw[:, tt, n:n + 1]
                    if n == 0:
                        ins = V.tensor_scalar(score[:, tt, :], rl[0][:, tt, :], w, None, ALU.mult)
                    else:
                        ins = V.scalar_tensor_tensor(score[:, tt, :], rl[n % 4][:, tt, :], w, score[:, tt, :], ALU.mult, ALU.add)
                ins.then_inc(relu_used, 1)
            dve.wait_ge(relu_used, IH)
            dve.wait_ge(m2_consts, 2)
            own(V.tensor_tensor(sel, score, mask, ALU.add))

            def top_round(r):
                src = sel if r == 0 else score
                for tt in range(TT):
                    ins = V.max(top8[:, tt, :], src[:, tt, :])
                own(ins)
                for tt in range(TT):
                    ins = V.match_replace(score[:, tt, :], top8[:, tt, :], src[:, tt, :], TAKEN)
                own(ins)

            def attention(name, k0, bias, extra, end):
                for h in range(BH + 2):
                    if h < BH:
                        b = h % 2
                        dve.wait_ge(tf[b], TB[name][b] + h // 2 + 1)
                        if h >= 2:
                            dve.wait_ge(tf[2 + b], TB[name][2 + b] + h // 2)
                        for tt in range(TT):
                            ins = V.tensor_tensor_reduce(prob[b][:, tt, :], T2[b][:, tt, :], bias[:, tt, :], 1.0, TAKEN, ALU.add, ALU.max,
                                                         accum_out=mx[:, 2 * b + tt:2 * b + tt + 1])
                        ins.then_inc(te[b], 1)
                        dve.wait_ge(te[b], TB[name][b] + h // 2 + 1)
                        V.tensor_scalar(mx[:, 2 * b:2 * b + 2], mx[:, 2 * b:2 * b + 2], -1.0, None, ALU.mult).then_inc(s_max, 1)
                        extra(h)
                    if 1 <= h <= BH:
                        dve.wait_ge(p_exp, k0 + h)
                        scale_probs(h - 1)
                    if h >= 2:
                        end(h - 2)

            def fox_end(h):
                dve.wait_ge(pv_done, XH + h + 1)
                V.tensor_copy(mixT[:, AH + h, :], PB[h % 2][:, 0:L]).then_inc(pv_taken, 1)

            attention("fox", 0, mask, top_round, fox_end)
            assert TOPK == 8 * BH
            own(V.tensor_scalar(sel, score, TAKEN, -1.0, ALU.is_equal, ALU.add))
            own(V.scalar_tensor_tensor(sel, sel, -NEG, mask, ALU.mult, ALU.add))

            def mix_out(g):
                dve.wait_ge(uv_done, g + 1)
                V.tensor_copy(mixT[:, g, :], PB[2 + g % 2][:, 0:L]).then_inc(uv_taken, 1)

            def dsa_end(h):
                dve.wait_ge(pv_done, XH + BH + h + 1)
                if h:
                    mix_out(h - 1)
                V.tensor_copy(o_lat, PB[h % 2][:, :].rearrange(bank2, t=L)).then_inc(pv_taken, 1)

            attention("dsa", BH, sel, lambda h: None, dsa_end)
            mix_out(AH - 1)
            down_first("wo2")
            down_rest("wo2")
            dve.wait_ge(x_back, 32)
            after_down(U_UP2, lambda tt: product_added(tt, 4, U_UP2, xn_big), N_2, "norm2_g_2", 0)
            ffn(2, "dn2")
            for tt in range(TT):
                product_added(tt, 5, U_END, xt)
                bank_sums(N_FIN, tt)
                mean(N_FIN, tt, D)
            dve.wait_ge(gain_landed, 64)
            for tt in range(TT):
                dve.wait_ge(rstd_done, nth(N_FIN, tt))
                V.scalar_tensor_tensor(tmp_big[:, tt, :], xt[:, tt, :], rstd(N_FIN)[:, tt:tt + 1], u[:, :], ALU.mult, ALU.mult)\
                    .then_inc(out_ready, 1)


_INS = ["x", "mem", "norm_pre", "norm_post", "norm_mem", "ssd_w_in", "ssd_conv_w", "ssd_conv_b", "ssd_dt_bias",
        "ssd_a_log", "ssd_d", "ssd_norm_g", "ssd_w_out", "xa_w_q", "xa_w_kv", "xa_w_o", "ffn_w_up", "ffn_conv_w",
        "ffn_conv_b", "ffn_w_down", "w_in_2", "kv_norm_g_2", "w_uk_2", "w_uv_2", "t5_table_2", "fgate_b_2", "w_o_2",
        "norm1_g_2", "norm2_g_2", "w_up_2", "conv_w_2", "conv_b_2", "w_down_2", "final_g_2"]


def _bucket_onehot():
    d = np.maximum(L - 1 - np.arange(BLK), 0)
    exact = NBUCKET // 2
    far = exact + (np.log(np.maximum(d, 1) / exact) / np.log(MAXDIST / exact) * (NBUCKET - exact)).astype(np.int32)
    bucket = np.where(d < exact, d, np.minimum(far, NBUCKET - 1))
    return (bucket[None, :] == np.arange(NBUCKET)[:, None]).astype(np.float32)


def kernel(**inputs):
    import concourse.bacc as _bacc
    from concourse.bass_utils import run_bass_kernel_spmd as _run

    nc = _bacc.Bacc("TRN2", target_bir_lowering=False, num_devices=1)
    arrays, aps = {}, {}
    for name in _INS + ["bucket_onehot"]:
        a = _bucket_onehot() if name == "bucket_onehot" else np.ascontiguousarray(inputs[name])
        arrays[f"in_{name}_dram"] = a
        aps[name] = nc.dram_tensor(f"in_{name}_dram", a.shape, mybir.dt.from_np(a.dtype), kind="ExternalInput").ap()
    out = nc.dram_tensor("out_0_dram", (1, L, D), F32, kind="ExternalOutput").ap()
    program(nc, aps, out)
    r = _run(nc, [arrays], core_ids=[0])
    return r.results[0]["out_0_dram"]
```

```python
from contextlib import ExitStack

import numpy as np

import concourse.bass as bass
from concourse import mybir

F32 = mybir.dt.float32
F32R = mybir.dt.float32r
ALU = mybir.AluOpType
ACT = mybir.ActivationFunctionType
AX_X = mybir.AxisListType.X

P = 128
L = 256
TT = L // P
D = 2048
KC = D // P
BLK = 512
NB = D // BLK
EPS = 1e-6
NEG = -1e30
TAKEN = -3e38

GROUPS, HPG, HD, NST = 8, 8, 64, 128
HEADS = GROUPS * HPG
DI = HEADS * HD
XS_COL, B_COL, C_COL, DT_COL = DI, 2 * DI, 2 * DI + GROUPS * NST, 2 * DI + 2 * GROUPS * NST
CONV_CH = (DI + 2 * GROUPS * NST) // P
SSD_TAPS = 4
XH = 4
XW = XH * P
F = 5632
FC = F // P
FB = F // BLK
FFN_TAPS = 3
AH, BH, RANK, IH, ID = 8, 8, 256, 16, 64
TOPK = min(256, L // 4)
NBUCKET, MAXDIST = 32, 128
AKV = AH * P
AIQ = AKV + RANK
AIK = AIQ + IH * ID
AIW = AIK + ID
BQ = AIW + IH
BK = BQ + BH * P
BV = BK + BH * P
BF = BV + BH * P
ODD = RANK + ID + IH + BH
SCALE = float(P) ** -0.5

COLS = {}
_n = 0
for _name, _rows in (("norm_pre", 3 * KC), ("norm_mem", KC), ("ssd_conv_w", SSD_TAPS * CONV_CH),
                     ("ssd_conv_b", CONV_CH), ("ssd_norm_g", DI // P), ("ffn_conv_w", FFN_TAPS * 2 * FC),
                     ("ffn_conv_b", 2 * FC), ("norm1_g_2", KC), ("norm2_g_2", KC),
                     ("conv_w_2", FFN_TAPS * 2 * FC), ("conv_b_2", 2 * FC)):
    COLS[_name] = (_n, _rows)
    _n += _rows
NCOL = _n
NROWT = -(-NCOL // P)
ROW_LOADS = []
for _name, (_r0, _rows) in COLS.items():
    _r = _r0
    while _r < _r0 + _rows:
        _k = min(_r0 + _rows - _r, P - _r % P)
        ROW_LOADS.append((_name, _r - _r0, _r, _k))
        _r += _k

U_KV, U_DT, U_SSD = 0, 2, 3
U_WOUT = U_SSD + 3 * GROUPS
U_XQ = U_WOUT + DI // P // 4
U_XO = U_XQ + 1
U_UP1 = U_XO + 1
U_DN1 = U_UP1 + 2 * FB
U_IN2 = U_DN1 + FC // 4
U_ODD = U_IN2 + 4
U_B = U_ODD + 1
U_WO2 = U_B + 6
U_UP2 = U_WO2 + 4
U_DN2 = U_UP2 + 2 * FB
U_END = U_DN2 + FC // 4

E_KV, E_DT, E_SSD = 1, 3, 4
E_XQ = E_SSD + 3 * GROUPS
E_UP1 = E_XQ + 1
E_IN2 = E_UP1 + 2 * FB
E_ODD = E_IN2 + 4
E_B = E_ODD + 1
E_UP2 = E_B + 6

X_WOUT = 0
X_XO = X_WOUT + DI // P
X_DN1 = X_XO + XH
X_WO2 = X_DN1 + FC
X_DN2 = X_WO2 + KC

N_MEM, N_X, N_Y, N_P1, N_H1, N_P2, N_H2, N_P3, N_1, N_CKV, N_2, N_FIN = range(12)
TRANSPOSED = [N_MEM, N_X, N_H1, N_H2, N_1, N_2]
BY_TILE = [N_H1, N_H2, N_1, N_2]
DIAGONAL = [(n, tt) for n in TRANSPOSED for tt in range(TT) if n not in BY_TILE or tt == 0]
POST = [N_P1, N_P2, N_P3]


def nth(n, tt):
    if n in POST:
        return 2 * n + 2 * tt + 1
    if n - 1 in POST:
        return 2 * (n - 1) + 2 * tt + 2
    return 2 * n + tt + 1


T_PLAN = [("params0", (0, 0, 1, 0)), (N_MEM, (2,) * 4), ("params", (1, 1, 0, 0)), ("kv", (1, 1, 0, 0)), (N_X, (2,) * 4),
          ("dt", (0, 0, 1, 1)), ("ssd", (4 * GROUPS, 4 * GROUPS, 2 * GROUPS, 2 * GROUPS)), (N_H1, (1,) * 4),
          ("xa", (3, 3, 2, 2)), (N_H2, (1,) * 4), ("up1", (FB,) * 4), (N_1, (1,) * 4), ("in2", (5, 5, 5, 4)),
          ("line", (0, 0, 0, 1)), ("qlat", (2,) * 4), ("idx", (4,) * 4), ("fox", (4,) * 4), ("dsa", (4,) * 4),
          (N_2, (1,) * 4), ("up2", (FB,) * 4), ("end", (0,) * 4)]
TB = {}
_at = [0] * 4
for _name, _uses in T_PLAN:
    TB[_name] = tuple(_at)
    _at = [a + u for a, u in zip(_at, _uses)]


IN2_UNITS = [(U_IN2, "aq", 0), (U_IN2 + 1, "aiq", 0), (U_IN2 + 2, "aq", 1), (U_IN2 + 3, "aiq", 1), (U_ODD, "odd", 0),
             (U_B, "bq", 0), (U_B + 1, "bk", 0), (U_B + 2, "bv", 0), (U_B + 3, "bq", 1), (U_B + 4, "bk", 1), (U_B + 5, "bv", 1)]
IN2_SLOT = {"aq": 0, "aiq": 1, "bq": 0, "bk": 1}
IN2_USE = {"aq": (0, 0), "aiq": (0, 0), "bq": (3, 3), "bk": (3, 2)}
IN2_TURN = {"aq": 0, "aiq": 0, "bq": 2, "bk": 2}


class Chain:

    def __init__(self, eng, sem):
        self.eng, self.sem, self.n, self.reg, self.per = eng, sem, 0, None, 0

    def __call__(self, ins):
        self.n += 1
        ins.then_inc(self.sem, 1)
        self.eng.wait_ge(self.sem, self.n if self.reg is None else self.reg * self.per + self.n)

    def mark(self, ins):
        self.n += 1
        ins.then_inc(self.sem, 1)
        return self.n

    def enter(self, reg, per):
        self.reg, self.per, self.start = reg, per, self.n

    def leave(self, turns):
        assert self.n - self.start == self.per, (self.n - self.start, self.per)
        self.n = self.start + self.per * turns
        self.reg = None


def program(nc, I, out):
    with ExitStack() as ctx:
        def sb(name, shape, dt=F32):
            return ctx.enter_context(nc.sbuf_tensor(name, shape, dt))

        def sem(name):
            return ctx.enter_context(nc.semaphore(name))

        hT_at = -(-nc.sbuf_base // 32) * 32
        hT_hi = sb("hT_hi", [P, KC, L], F32R)
        hT_lo = sb("hT_lo", [P, KC, L], F32R)
        attn = nc.alloc_sbuf_tensor_at("attn", [P, 2 * KC * L], F32, offset=hT_at)
        raw = sb("raw", [P, 4, 4 * BLK])
        w_hi = sb("w_hi", [P, 4, 4 * BLK], F32R)
        w_lo = sb("w_lo", [P, 4, 4 * BLK], F32R)
        big = sb("big", [P, FC * L])
        x = sb("x", [P, TT * D])
        u = sb("u", [P, 4 * BLK])
        vb = sb("vb", [P, 4 * L])
        cols = sb("cols", [P, NCOL])
        ident = sb("ident", [P, P])
        triu = sb("triu", [P, P])
        ones = sb("ones", [P, P])
        small = sb("small", [P, 3 * HEADS])
        misc = sb("misc", [P, L])
        diag = misc[:, :].rearrange("p (a t) -> p a t", a=TT)
        stat = sb("stat", [P, 48])

        bigc = big[:, :].rearrange("p (c t) -> p c t", t=L)
        xt = x[:, :].rearrange("p (a n) -> p a n", a=TT)
        u2 = u[:, :].rearrange("p (s a n) -> p s a n", s=2, a=TT)
        vbc = vb[:, :].rearrange("p (c t) -> p c t", t=L)
        xn_big = big[:, 0:TT * D].rearrange("p (a n) -> p a n", a=TT)
        tmp_big = big[:, TT * D:2 * TT * D].rearrange("p (a n) -> p a n", a=TT)
        bank2 = "p (c t) -> p c t"

        ssq = lambda n: stat[:, 2 * n:2 * n + 2]
        rstd = lambda n: stat[:, 24 + 2 * n:24 + 2 * n + 2]
        ssq_parts = sb("ssq_parts", [P, TT * NB])
        half = sb("half", [P, 2])
        mx = sb("mx", [P, 4])
        den = sb("den", [P, 4])
        rden = sb("rden", [P, 4])

        idle = sb("idle", [P, 14])
        rows = tmp_big[:, 0, 0:NROWT * P].rearrange("p (r f) -> p r f", f=P)

        ssd_m = x[:, 0:8 * L].rearrange("p (h t) -> p h t", t=L)
        xdt = x[:, 2048:3072].rearrange("p (a n) -> p a n", a=TT)
        yg = x[:, 3072:4096].rearrange("p (a n) -> p a n", a=TT)
        zs = big[:, 8192:9216].rearrange("p (a n) -> p a n", a=TT)
        xc = big[:, 9216:10240].rearrange(bank2, t=L)
        bc = big[:, 10240:10752].rearrange(bank2, t=L)
        bd = big[:, 10752:11264]
        u_xs = u2[:, 0]
        u_bc = u[:, 1024:1536].rearrange("p (a n) -> p a n", a=TT)
        states = u[:, 1536:2048]
        dt = vb[:, 0:128].rearrange("p (a h) -> p a h", a=TT)
        da = vb[:, 128:256].rearrange("p (a h) -> p a h", a=TT)
        acs = vb[:, 256:384].rearrange("p (a h) -> p a h", a=TT)
        dte = vb[:, 384:448]
        eacs = vb[:, 448:512]
        bm = vb[:, 512:640]
        cbm = vb[:, 640:896].rearrange("p (a t) -> p a t", a=TT)
        yssq = vb[:, 896:900].rearrange("p (k a) -> p k a", k=2)
        dt_bias, a_log, d_skip = (small[:, k * HEADS:(k + 1) * HEADS] for k in range(3))
        acsT = misc[0:HEADS, :]
        sp_tmp = [big[:, 4096 + 128 * k:4096 + 128 * (k + 1)] for k in range(8)]

        xa_kT = big[:, 4096:5120].rearrange(bank2, t=L)
        xa_v = big[:, 5120:6144].rearrange("p (a n) -> p a n", a=TT)
        xa_qT = big[:, 6144:7168].rearrange(bank2, t=L)
        xa_oT = big[:, 7168:8192].rearrange(bank2, t=L)
        prob = [u[:, 512 * k:512 * (k + 1)].rearrange("p (a s) -> p a s", a=TT) for k in range(2)]
        probT = [u[:, 1024 + 512 * k:1024 + 512 * (k + 1)] for k in range(2)]

        aqT = big[:, 0:2048].rearrange(bank2, t=L)
        aiqT = big[:, 2048:4096].rearrange(bank2, t=L)
        bqT = big[:, 4096:6144].rearrange(bank2, t=L)
        bkT = big[:, 6144:8192].rearrange(bank2, t=L)
        bv = big[:, 8192:10240].rearrange("p (a n) -> p a n", a=TT)
        ckv = big[:, 10240:10752].rearrange("p (a r) -> p a r", a=TT)
        ckvT = big[:, 10752:11264].rearrange(bank2, t=L)
        w_uv = big[:, 0:2048].rearrange("p (h c d) -> p h c d", h=AH, c=2)
        w_uk = x[:, 2048:4096].rearrange("p (h r) -> p h r", h=AH)
        qlT = attn[:, 0:4096].rearrange("p (h c t) -> p h c t", h=AH, c=2)
        skew = attn[:, 4096:6144].rearrange("p (h s) -> p h s", h=AH)
        score = attn[:, 7168:7680].rearrange("p (a s) -> p a s", a=TT)
        sel = attn[:, 7680:8192].rearrange("p (a s) -> p a s", a=TT)
        mixT = x[:, :].rearrange(bank2, t=L)
        odd = x[:, 0:2 * ODD].rearrange("p (a n) -> p a n", a=TT)
        aik2 = x[:, 768:1024].rearrange("p (a k n) -> p a k n", a=TT, k=2)
        onehot = x[0:NBUCKET, 1024:1536]
        line = x[0:AH, 1536:2048]
        kv_gain = x[:, 2048:2048 + RANK]
        table = x[0:NBUCKET, 2 * ODD:2 * ODD + AH]
        fg_bias = x[:, 2320:2320 + BH]
        fox_tmp = [x[:, 2400 + 16 * k:2416 + 16 * k] for k in range(8)]
        lf = x[:, 2560:2576].rearrange("p (a h) -> p a h", a=TT)
        mask = vb[:, 0:512].rearrange("p (a s) -> p a s", a=TT)
        aikT = vb[:, 512:768]
        cum_row = vb[0:BH, 768:1024]
        anti = small[:, 0:P]
        iw = small[:, 128:160].rearrange("p (a h) -> p a h", a=TT)
        top8 = small[:, 160:176].rearrange("p (a k) -> p a k", a=TT)
        cumT = misc[0:BH, :]
        o_lat = attn[:, 7168:7680].rearrange(bank2, t=L)
        rl = [u[:, 512 * k:512 * k + P + L] for k in range(4)]

        PB = [ctx.enter_context(nc.psum_tensor(f"PB{k}", [P, BLK], F32)) for k in range(4)]
        T = [ctx.enter_context(nc.psum_tensor(f"T{k}", [P, BLK], F32)) for k in range(4)]
        T2 = [t[:, :].rearrange(bank2, t=L) for t in T]
        acc = [PB, T]

        kT_d = nc.dram_tensor("kT_d", (P, XH * L), F32, kind="Internal").ap()
        v_d = nc.dram_tensor("v_d", (P, TT * XW), F32, kind="Internal").ap()
        acsT_d = nc.dram_tensor("acsT_d", (HEADS, L), F32, kind="Internal").ap()
        x_d = nc.dram_tensor("x_d", (P, TT * D), F32, kind="Internal").ap()
        line_d = nc.dram_tensor("line_d", (AH, BLK), F32, kind="Internal").ap()

        raw_landed = [sem(f"raw_landed{j}") for j in range(4)]
        c_landed = [sem(f"c_landed{j}") for j in range(4)]
        odd_landed = [sem(f"odd_landed{j}") for j in range(4)]
        hi_ready, lo_ready = sem("hi_ready"), sem("lo_ready")
        quad_used = sem("quad_used")
        proj_evac = sem("proj_evac")
        tf = [sem(f"t{b}_full") for b in range(4)]
        te = [sem(f"t{b}_empty") for b in range(4)]
        xs_hi, xs_lo = sem("xs_hi"), sem("xs_lo")
        consts_ready, cols_ready = sem("consts_ready"), sem("cols_ready")
        rows0_landed, rows_landed = sem("rows0_landed"), sem("rows_landed")
        x_landed = [sem(f"x_landed{tt}") for tt in range(TT)]
        mem_landed = [sem(f"mem_landed{tt}") for tt in range(TT)]
        small_landed = sem("small_landed")
        sq_done, ms_done, rstd_done = sem("sq_done"), sem("ms_done"), sem("rstd_done")
        ph_full = [sem(f"ph{b}_full") for b in range(4)]
        ph_empty = [sem(f"ph{b}_empty") for b in range(4)]
        diag_ready = sem("diag_ready")
        xn_ready = sem("xn_ready")
        tile0_done = sem("tile0_done")
        h_hi_done = sem("h_hi_done")
        kT_copied, kv_stored, kv_loaded = sem("kT_copied"), sem("kv_stored"), sem("kv_loaded")
        exp_asked, exp_done = sem("exp_asked"), sem("exp_done")
        da_ready, acsT_ready, acsT_stored = sem("da_ready"), sem("acsT_ready"), sem("acsT_stored")
        acs_landed, diff_made, diff_ready = sem("acs_landed"), sem("diff_made"), sem("diff_ready")
        decay_ready, m_ready = sem("decay_ready"), sem("m_ready")
        bc_tap, bc_ready, xs_tap, xc_ready = sem("bc_tap"), sem("bc_ready"), sem("xs_tap"), sem("xc_ready")
        bd_ready, yg_ready = sem("bd_ready"), sem("yg_ready")
        x_back, gain_landed, x_new, x_spilled = sem("x_back"), sem("gain_landed"), sem("x_new"), sem("x_spilled")
        gate_tap, val_tap, gate_act, ffn_mul = sem("gate_tap"), sem("val_tap"), sem("gate_act"), sem("ffn_mul")
        s_max, p_exp, p_ready = sem("s_max"), sem("p_exp"), sem("p_ready")
        pv_done, pv_taken = sem("pv_done"), sem("pv_taken")
        uv_done, uv_taken = sem("uv_done"), sem("uv_taken")
        m2_landed, m2_consts = sem("m2_landed"), sem("m2_consts")
        odd_ready, decay_sum_ready = sem("odd_ready"), sem("decay_sum_ready")
        line_ready, line_stored, skew_landed = sem("line_ready"), sem("line_stored"), sem("skew_landed")
        uk_landed, uv_landed, cum_row_ready = sem("uk_landed"), sem("uv_landed"), sem("cum_row_ready")
        relu_used = sem("relu_used")
        out_ready, out_stored = sem("out_ready"), sem("out_stored")
        dve_own, pool_own = sem("dve_own"), sem("pool_own")

        def quad(buf, j, n):
            return buf[:, j, :].rearrange("p (c n) -> p c n", c=4)[:, :, 0:n]

        def col(name, k):
            return cols[:, bass.ds(k + COLS[name][0], 1)]

        def landed(unit):
            return 16 * (unit + 1 - (unit > U_ODD))

        def chunk(a, k):
            return a[:, bass.ds(k, 1), :].rearrange("p c t -> p (c t)")

        def keys(tt, causal=True):
            return P * (tt + 1) if causal else L

        def blocks(causal):
            return [(0, 0, 0), (0, 1, P), (1, 1, L)] if causal else [(0, 0, 0), (0, 1, P), (1, 0, L), (1, 1, L + P)]

        ragged = [slice(0, P), slice(P, P + L)]

        def sq_count(n, tt):
            return nth(n, tt) - TT * (n > N_Y)

        def h_bank(n, tt, b):
            if tt == 0 and n in BY_TILE:
                return PB[b], ph_full[b], ph_empty[b], BY_TILE.index(n)
            return T[b], tf[b], te[b], TB[n][b] + (tt if n not in BY_TILE else 0)

        def t_idx(n):
            return TRANSPOSED.index(n)

        rows3 = lambda w: w.rearrange("(c p) n -> p c n", p=P)
        w_ssd, w_kv, w_q = rows3(I["ssd_w_in"][0]), rows3(I["xa_w_kv"][0]), rows3(I["xa_w_q"][0])
        w_up = {1: rows3(I["ffn_w_up"][0]), 2: rows3(I["w_up_2"][0])}
        w_in2 = rows3(I["w_in_2"][0])
        down_w = {"wout": rows3(I["ssd_w_out"][0]), "xo": rows3(I["xa_w_o"][0]), "dn1": rows3(I["ffn_w_down"][0]),
                  "wo2": rows3(I["w_o_2"][0]), "dn2": rows3(I["w_down_2"][0])}
        DOWN = {"wout": (U_WOUT, X_WOUT, DI // P // 4, bigc), "xo": (U_XO, X_XO, 1, xa_oT),
                "dn1": (U_DN1, X_DN1, FC // 4, bigc), "wo2": (U_WO2, X_WO2, KC // 4, mixT),
                "dn2": (U_DN2, X_DN2, FC // 4, bigc)}
        FFN = {1: (U_UP1, E_UP1, TB["up1"], "ffn_conv_w", "ffn_conv_b"),
               2: (U_UP2, E_UP2, TB["up2"], "conv_w_2", "conv_b_2")}
        tokens = lambda a: a.rearrange("(a p) n -> p a n", p=P)

        block = ctx.enter_context(nc.Block())

        @block.sync
        def _(sp):
            def load_up(q, w, c0, n, first=False, js=range(4)):
                for j in js:
                    if not first:
                        sp.wait_ge(lo_ready, q - 3 + j)
                    sp.dma_start(quad(raw, j, n), w[:, 4 * j:4 * j + 4, bass.ds(c0, n)]).then_inc(raw_landed[j], 16)

            def load_down(name):
                unit, _, n, _ = DOWN[name]

                def rows(q, chunk):
                    for j in range(4):
                        sp.wait_ge(lo_ready, q - 3 + j)
                        sp.dma_start(raw[:, j, :], down_w[name][:, bass.ds(chunk + j, 1), :].rearrange("p c n -> p (c n)"))\
                            .then_inc(raw_landed[j], 16)

                if n == 1:
                    rows(4 * unit, 0)
                else:
                    with nc.sync.Fori(0, n) as i:
                        rows(i * 4 + 4 * unit, i * 4)

            def load_ffn(n):
                unit = FFN[n][0]
                with nc.sync.Fori(0, FB) as i:
                    load_up(i * 8 + 4 * unit, w_up[n], i * BLK, BLK)
                    load_up(i * 8 + 4 * (unit + 1), w_up[n], i * BLK + F, BLK)

            def load_rows(first_tile):
                for name, a0, r, k in ROW_LOADS:
                    if (r < P) == first_tile:
                        a = I[name]
                        flat = a.rearrange("a b (c f) -> (a b c) f", f=P) if len(a.shape) == 3 \
                            else a.rearrange("a (c f) -> (a c) f", f=P)
                        sp.dma_start(rows[r % P:r % P + k, r // P, :], flat[a0:a0 + k, :])\
                            .then_inc(rows0_landed if first_tile else rows_landed, 16)

            load_rows(True)
            for tt in range(TT):
                sp.dma_start(xn_big[:, tt, :], I["mem"][0, tt * P:(tt + 1) * P, :]).then_inc(mem_landed[tt], 16)
            load_up(0, w_kv, 0, BLK, first=True, js=(0,))
            load_rows(False)
            load_up(0, w_kv, 0, BLK, first=True, js=(1, 2, 3))
            for tt in range(TT):
                sp.dma_start(xt[:, tt, :], I["x"][0, tt * P:(tt + 1) * P, :]).then_inc(x_landed[tt], 16)
            load_up(4, w_kv, XW, BLK)
            load_up(4 * U_DT, w_ssd, DT_COL, HEADS)
            with nc.sync.Fori(1, GROUPS + 1) as g1:
                q = g1 * 12 + (4 * U_SSD - 12)
                for j in range(4):
                    sp.wait_ge(lo_ready, q - 3 + j)
                    for k in range(2):
                        sp.dma_start(quad(raw, j, 2 * NST)[:, :, k * NST:(k + 1) * NST],
                                     w_ssd[:, 4 * j:4 * j + 4, bass.ds(g1 * NST + ((B_COL, C_COL)[k] - NST), NST)])\
                            .then_inc((raw_landed, c_landed)[k][j], 16)
                load_up(q + 4, w_ssd, g1 * BLK + (XS_COL - BLK), BLK)
                load_up(q + 8, w_ssd, g1 * BLK + (-BLK), BLK)
            load_down("wout")
            load_up(4 * U_XQ, w_q, 0, XW)
            load_down("xo")
            load_ffn(1)
            load_down("dn1")
            for k in range(2):
                load_up(4 * (U_IN2 + 2 * k), w_in2, k * BLK, BLK)
                load_up(4 * (U_IN2 + 2 * k + 1), w_in2, AIQ + k * BLK, BLK)
            for j in range(4):
                sp.wait_ge(lo_ready, 4 * U_ODD - 3 + j)
                for c0, n, at in ((AKV, RANK, 0), (AIK, ID + IH, RANK), (BF, BH, RANK + ID + IH)):
                    sp.dma_start(quad(raw, j, ODD)[:, :, at:at + n], w_in2[:, 4 * j:4 * j + 4, c0:c0 + n])\
                        .then_inc(odd_landed[j], 16)
            for k in range(2):
                for m, c0 in enumerate((BQ, BK, BV)):
                    load_up(4 * (U_B + 3 * k + m), w_in2, c0 + k * BLK, BLK)
            load_down("wo2")
            load_ffn(2)
            load_down("dn2")
            for tt in range(TT):
                sp.wait_ge(out_ready, tt + 1)
                sp.dma_start(out[0, tt * P:(tt + 1) * P, :], tmp_big[:, tt, :]).then_inc(out_stored, 16)
            sp.wait_ge(out_stored, 16 * TT)

        @block.gpsimd
        def _(pool):
            nc.gpsimd.memset(ident[:, :], 0.0).then_inc(pool_own, 1)
            nc.gpsimd.memset(ones[:, :], 1.0).then_inc(pool_own, 1)
            nc.gpsimd.memset(half[:, :], -0.5).then_inc(pool_own, 1)
            pool.wait_ge(pool_own, 3)
            nc.gpsimd.affine_select(out=ident[:, :], in_=ident[:, :], compare_op=ALU.not_equal, fill=1.0, base=0,
                                    pattern=[[-1, P]], channel_multiplier=1).then_inc(consts_ready, 1)
            nc.gpsimd.affine_select(out=triu[:, :], in_=ones[:, :], compare_op=ALU.is_ge, fill=0.0, base=0,
                                    pattern=[[1, P]], channel_multiplier=-1).then_inc(consts_ready, 1)

            for dst, name in ((dt_bias, "ssd_dt_bias"), (a_log, "ssd_a_log"), (d_skip, "ssd_d")):
                pool.dma_start(dst, I[name][0].partition_broadcast(P)).then_inc(small_landed, 16)

            def inverse_root(n, tiles=range(TT)):
                for tt in tiles:
                    r = rstd(n)[:, tt:tt + 1]
                    pool.wait_ge(ms_done, nth(n, tt))
                    nc.gpsimd.tensor_tensor(r, ssq(n)[:, tt:tt + 1], half[:, 0:1], ALU.pow).then_inc(rstd_done, 1)
                    if (n, tt) in DIAGONAL:
                        pool.wait_ge(rstd_done, nth(n, tt))
                        nc.gpsimd.tensor_tensor(diag[:, tt, :], ident[:, :], r.broadcast_to([P, P]), ALU.mult)\
                            .then_inc(diag_ready, 1)

            def inverse_roots(post, n):
                for tt in range(TT):
                    inverse_root(post, (tt,))
                    inverse_root(n, (tt,))

            def load_gain(src):
                pool.dma_start(u[:, :], src.partition_broadcast(P)).then_inc(gain_landed, 16)

            inverse_root(N_MEM)
            inverse_root(N_X)
            pool.wait_ge(kT_copied, 1)
            pool.wait_ge(proj_evac, E_KV + 1)
            pool.dma_start(kT_d, vb[:, :]).then_inc(kv_stored, 16)
            pool.dma_start(v_d, u[:, 1024:2048]).then_inc(kv_stored, 16)
            pool.wait_ge(acsT_ready, 1)
            pool.dma_start(acsT_d, acsT).then_inc(acsT_stored, 16)
            pool.wait_ge(acsT_stored, 16)

            def exponents(g):
                pool.dma_start(ssd_m, bass.AP(acsT_d.tensor, g * (HPG * L), [[0, P], [L, HPG], [1, L]]))\
                    .then_inc(acs_landed, 16)
                pool.wait_ge(acs_landed, g * 16 + 16)
                for c in range(TT):
                    e = ssd_m[:, :, c * P:(c + 1) * P]
                    at_s = acs[:, c, bass.ds(g * HPG, HPG)].unsqueeze(2).broadcast_to([P, HPG, P])
                    ins = nc.gpsimd.tensor_tensor(e, e, at_s, ALU.subtract)
                ins.then_inc(diff_made, 1)
                pool.wait_ge(diff_made, g + 1)
                nc.gpsimd.tensor_tensor(idle[:, 0:1], half[:, 0:1], half[:, 1:2], ALU.add)
                nc.gpsimd.tensor_scalar(x[:, 0:2048], x[:, 0:2048], 0.0, None, ALU.min).then_inc(diff_ready, 1)

            exponents(0)
            with nc.gpsimd.Fori(0, GROUPS - 1) as i:
                pool.wait_ge(tf[3], i * 2 + (TB["ssd"][3] + 1))
                nc.gpsimd.tensor_tensor(idle[:, 0:1], half[:, 0:1], half[:, 1:2], ALU.add)
                exponents(i + 1)

            inverse_root(N_Y)
            pool.wait_ge(te[3], TB["ssd"][3] + 2 * GROUPS)
            pool.dma_start(xt, tokens(I["x"][0])).then_inc(x_back, 16)
            load_gain(I["norm_post"][0, 0])
            inverse_roots(N_P1, N_H1)
            pool.wait_ge(kv_stored, 32)
            pool.wait_ge(x_new, TT * NB)
            pool.dma_start(big[:, 4096:5120], kT_d).then_inc(kv_loaded, 16)
            pool.dma_start(big[:, 5120:6144], v_d).then_inc(kv_loaded, 16)
            pool.wait_ge(pv_done, XH)
            load_gain(I["norm_post"][0, 1])
            inverse_roots(N_P2, N_H2)
            pool.wait_ge(tf[3], TB["up1"][3] + FB)
            load_gain(I["norm_post"][0, 2])
            inverse_roots(N_P3, N_1)
            pool.wait_ge(x_new, 3 * TT * NB)
            pool.dma_start(x_d, x[:, :]).then_inc(x_spilled, 16)
            pool.wait_ge(x_spilled, 16)
            for b in range(4):
                pool.wait_ge(tf[b], TB[N_1][b] + 1)
            for dst, src in ((onehot, I["bucket_onehot"]), (table, I["t5_table_2"]),
                             (kv_gain, I["kv_norm_g_2"][0].partition_broadcast(P)),
                             (fg_bias, I["fgate_b_2"][0].partition_broadcast(P))):
                pool.dma_start(dst, src).then_inc(m2_landed, 16)
            nc.gpsimd.memset(anti, 0.0).then_inc(pool_own, 1)
            nc.gpsimd.memset(vb[:, 0:512], 0.0).then_inc(pool_own, 1)
            pool.wait_ge(pool_own, 5)
            nc.gpsimd.affine_select(out=anti, in_=anti, compare_op=ALU.not_equal, fill=1.0, base=-(P - 1),
                                    pattern=[[1, P]], channel_multiplier=1).then_inc(m2_consts, 1)
            nc.gpsimd.affine_select(out=mask, in_=mask, compare_op=ALU.is_ge, fill=NEG, base=0,
                                    pattern=[[P, TT], [-1, L]], channel_multiplier=1).then_inc(m2_consts, 1)
            inverse_root(N_CKV)
            pool.wait_ge(te[2], TB["in2"][2] + 3)
            pool.dma_start(w_uk, I["w_uk_2"][0].rearrange("h d r -> d h r")).then_inc(uk_landed, 16)
            pool.wait_ge(line_ready, 1)
            pool.dma_start(line_d, line).then_inc(line_stored, 16)
            pool.wait_ge(line_stored, 16)
            pool.wait_ge(quad_used, 4 * U_WO2)
            pool.dma_start(skew, bass.AP(line_d.tensor, 0, [[1, P], [BLK, AH], [1, L]])).then_inc(skew_landed, 16)
            for b in range(4):
                pool.wait_ge(tf[b], TB["qlat"][b] + 2)
            pool.dma_start(w_uv, I["w_uv_2"][0].rearrange("h (c p) d -> p h c d", p=P)).then_inc(uv_landed, 16)
            pool.wait_ge(decay_sum_ready, 1)
            for h in range(BH):
                if h:
                    b = (h - 1) % 2
                    pool.wait_ge(tf[b], TB["fox"][b] + (h - 1) // 2 + 1)
                nc.gpsimd.tensor_scalar(cum_row, cumT, ident[0:BH, h:h + 1], None, ALU.mult).then_inc(cum_row_ready, 1)
            pool.wait_ge(uv_done, AH)
            pool.dma_start(xn_big, x_d.rearrange("p (a n) -> p a n", a=TT)).then_inc(x_back, 16)
            inverse_root(N_2)
            pool.wait_ge(tf[3], TB["up2"][3] + FB)
            load_gain(I["final_g_2"])
            inverse_root(N_FIN)

        @block.scalar
        def _(act):
            def hi(q, land, j, n=4 * BLK, land_sem=None, first=False):
                act.wait_ge(land_sem or raw_landed[j], land)
                if not first:
                    act.wait_ge(quad_used, q - 3 + j)
                dst, src = (w_hi[:, j, :], raw[:, j, :]) if n == 4 * BLK else (quad(w_hi, j, n), quad(raw, j, n))
                nc.scalar.activation(dst, src, ACT.Copy).then_inc(hi_ready, 1)

            def hi_unit(unit, n=4 * BLK, js=range(4), first=False):
                for j in js:
                    hi(4 * unit, landed(unit), j, n, None, first)

            def hi_bc(g, j):
                act.wait_ge(c_landed[j], g * 16 + 16)
                hi(g * 12 + 4 * U_SSD, g * 48 + landed(U_SSD), j, 2 * NST)

            def evac(q, pair, dst, n=BLK, func=ACT.Copy, scale=1.0):
                act.wait_ge(quad_used, q + 4)
                for tt in range(TT):
                    ins = nc.scalar.activation(dst[:, tt, 0:n], PB[2 * pair + tt][:, 0:n], func, scale=scale)
                ins.then_inc(proj_evac, 1)

            def square(n, tt, src, scratch):
                nc.scalar.activation(scratch, src, ACT.Square, accum_out=ssq(n)[:, tt:tt + 1]).then_inc(sq_done, 1)

            def h_hi(n, tt, gain, k0, quads=None):
                for b in range(4):
                    if quads is not None:
                        act.wait_ge(quad_used, quads + b)
                    bank, full, _, uses = h_bank(n, tt, b)
                    act.wait_ge(full, uses + 1)
                    for c in range(4):
                        k = 4 * b + c
                        ins = nc.scalar.activation(hT_hi[:, k, tt * P:(tt + 1) * P], bank[:, c * P:(c + 1) * P], ACT.Copy,
                                                   scale=col(gain, k0 + k))
                    ins.then_inc(h_hi_done, 1)

            def down_first(name, ready):
                unit, _, _, src = DOWN[name]
                act.wait_ge(quad_used, 4 * unit - 3)
                for j in range(4):
                    ready(j)
                    nc.scalar.activation(hT_hi[:, j, :], src[:, j, :], ACT.Copy).then_inc(xs_hi, 1)

            def down_rest(name):
                unit, _, n, src = DOWN[name]
                with nc.scalar.Fori(0, n - 1) as i:
                    for j in range(4):
                        hi(i * 4 + 4 * (unit + 1), i * 16 + landed(unit + 1), j)
                        nc.scalar.activation(hT_hi[:, j, :], chunk(src, i * 4 + (4 + j)), ACT.Copy).then_inc(xs_hi, 1)

            def square_bank(n, tt, nb, src, scratch):
                k = tt * NB + nb
                ins = nc.scalar.activation(scratch[:, tt, nb * BLK:(nb + 1) * BLK], src, ACT.Square, accum_out=ssq_parts[:, k:k + 1])
                if nb == NB - 1:
                    ins.then_inc(sq_done, 1)

            def square_sums(post, k, unit, tt):
                if tt == 0:
                    act.wait_ge(tile0_done, k)
                else:
                    act.wait_ge(quad_used, 4 * unit)
                for nb in range(NB):
                    square_bank(post, tt, nb, acc[tt][nb][:, :], xn_big)

            def square_residual(n, k, tt, scratch):
                for nb in range(NB):
                    act.wait_ge(x_new, ((k - 1) * TT + tt) * NB + nb + 1)
                    square_bank(n, tt, nb, xt[:, tt, nb * BLK:(nb + 1) * BLK], scratch)

            def after_down(unit, post, n, k, gain, k0, scratch=xn_big):
                if post is not None:
                    square_sums(post, k, unit, 0)
                hi_unit(unit, js=(0, 1))
                square_residual(n, k, 0, scratch)
                hi_unit(unit, js=(2,))
                act.wait_ge(quad_used, 4 * unit)
                h_hi(n, 0, gain, k0)
                if post is not None:
                    square_sums(post, k, unit, 1)
                hi_unit(unit, js=(3,))
                square_residual(n, k, 1, scratch)
                act.wait_ge(rstd_done, nth(n, 1))
                for nb in range(NB):
                    s = slice(nb * BLK, (nb + 1) * BLK)
                    nc.scalar.activation(scratch[:, 1, s], xt[:, 1, s], ACT.Copy, scale=rstd(n)[:, 1:2]).then_inc(xn_ready, 1)
                h_hi(n, 1, gain, k0)

            for tt in range(TT):
                act.wait_ge(mem_landed[tt], 16)
                square(N_MEM, tt, xn_big[:, tt, :], (u[:, :], tmp_big[:, 1, :])[tt])
            act.wait_ge(cols_ready, 1)
            h_hi(N_MEM, 0, "norm_mem", 0)
            hi_unit(0, js=(0,), first=True)
            h_hi(N_MEM, 1, "norm_mem", 0)
            hi_unit(0, js=(1, 2, 3), first=True)
            for tt in range(TT):
                act.wait_ge(x_landed[tt], 16)
                square(N_X, tt, xt[:, tt, :], xn_big[:, tt, :])
            hi_unit(1)
            evac(0, 0, u2[:, 0])
            hi_unit(U_DT, HEADS)
            h_hi(N_X, 0, "norm_pre", 0, 4 * U_DT - 3)
            evac(4, 1, u2[:, 1])
            h_hi(N_X, 1, "norm_pre", 0)
            for j in range(4):
                hi_bc(0, j)
            act.wait_ge(cols_ready, 2)
            evac(4 * U_DT, 0, sp_tmp[0].rearrange("p (a h) -> p a h", a=TT), HEADS)
            act.wait_ge(small_landed, 48)
            nc.scalar.activation(a_log, a_log, ACT.Exp).then_inc(exp_done, 1)
            act.wait_ge(exp_asked, 1)
            nc.scalar.activation(sp_tmp[2], sp_tmp[2], ACT.Exp).then_inc(exp_done, 1)
            tb = TB["ssd"]

            def decays(g):
                act.wait_ge(diff_ready, g + 1)
                nc.scalar.activation(x[:, 0:2048], x[:, 0:2048], ACT.Exp).then_inc(decay_ready, 1)

            def states_out(uses):
                act.wait_ge(tf[0], uses)
                nc.scalar.activation(states, T[0][:, :], ACT.Copy).then_inc(te[0], 1)

            def y_out(g, after):
                for b in range(2):
                    act.wait_ge(tf[2 + b], after * 2 + tb[2 + b])
                    for c in range(2):
                        k = g * 4 + (2 * b + c)
                        ins = nc.scalar.activation(chunk(bigc, k), T2[2 + b][:, c, :], ACT.Copy, scale=col("ssd_norm_g", k))
                    ins.then_inc(te[2 + b], 1)

            def group(g, odd_group, prev, nxt):
                q = g * 12 + 4 * U_SSD
                land = lambda k: g * 48 + landed(U_SSD + k)
                pair = [(U_SSD + odd_group + k) % 2 for k in range(3)]

                def hi_next(j):
                    if nxt:
                        hi_bc(g + 1, j)
                    else:
                        hi(4 * U_WOUT, landed(U_WOUT), j)

                for j in range(4):
                    hi(q + 4, land(1), j)
                evac(q, pair[0], u_bc, 2 * NST)
                if prev:
                    states_out(g * 4 + tb[0])
                else:
                    act.wait_ge(exp_asked, 2)
                    nc.scalar.activation(dte, dte, ACT.Exp).then_inc(exp_done, 1)
                    nc.scalar.activation(eacs, acs[:, 1, :], ACT.Exp).then_inc(exp_done, 1)
                for j in range(2):
                    hi(q + 8, land(2), j)
                act.wait_ge(tf[0], g * 4 + (tb[0] + 1))
                if prev:
                    act.wait_ge(tf[1], g * 4 + tb[1])
                for k in range(2):
                    c = g + (32 + 8 * k)
                    ins = nc.scalar.activation(bc[:, k, :], T2[0][:, k, :], ACT.Identity, bias=col("ssd_conv_b", c),
                                               scale=col("ssd_conv_w", c + (SSD_TAPS - 1) * CONV_CH))
                ins.then_inc(bc_tap, 1)
                hi(q + 8, land(2), 2)
                act.wait_ge(te[0], g * 4 + (tb[0] + 1))
                nc.scalar.activation(big[:, 10240:10752], big[:, 10240:10752], ACT.Silu).then_inc(bc_ready, 1)
                if prev:
                    y_out(g - 1, g)
                hi(q + 8, land(2), 3)
                evac(q + 4, pair[1], u_xs)
                hi_next(0)
                decays(g)
                hi_next(1)
                for b in range(2):
                    act.wait_ge(tf[b], g * 4 + (tb[b] + 2))
                for k in range(4):
                    c = g * 4 + k
                    ins = nc.scalar.activation(xc[:, k, :], T2[k // 2][:, k % 2, :], ACT.Identity, bias=col("ssd_conv_b", c),
                                               scale=col("ssd_conv_w", c + (SSD_TAPS - 1) * CONV_CH))
                ins.then_inc(xs_tap, 1)
                hi_next(2)
                act.wait_ge(te[1], g * 4 + (tb[1] + 2))
                nc.scalar.activation(big[:, 9216:10240], big[:, 9216:10240], ACT.Silu).then_inc(xc_ready, 1)
                if not nxt:
                    down_first("wout", lambda j: act.wait_ge(te[3], tb[3] + 2))
                hi_next(3)
                evac(q + 8, pair[2], zs, BLK, ACT.Silu)

            act.wait_ge(kv_stored, 32)
            group(0, 0, False, True)
            with nc.scalar.Fori(0, GROUPS // 2 - 1) as i:
                group(i * 2 + 1, 1, True, True)
                group(i * 2 + 2, 0, True, True)
            group(GROUPS - 1, 1, True, False)
            states_out(GROUPS * 4 + tb[0])
            y_out(GROUPS - 1, GROUPS)
            act.wait_ge(te[3], tb[3] + 2 * GROUPS)
            down_rest("wout")
            after_down(U_XQ, N_P1, N_H1, 1, "norm_pre", KC)

            hi_unit(U_XO, js=(0, 1, 2))
            evac(4 * U_XQ, 0, u2[:, 0], XW, ACT.Copy, SCALE)
            hi_unit(U_XO, js=(3,))

            def exps(k, src, then, causal=True):
                par = k % 2
                for tt in range(TT):
                    n = keys(tt, causal)
                    ins = nc.scalar.activation(prob[par][:, tt, 0:n], src(tt)[:, 0:n], ACT.Exp,
                                               bias=mx[:, 2 * par + tt:2 * par + tt + 1],
                                               accum_out=den[:, 2 * par + tt:2 * par + tt + 1])
                ins.then_inc(then, 1)

            def prob_out(h, name, pv0, n=L + P):
                b = 2 + h % 2
                act.wait_ge(tf[b], TB[name][b] + h // 2 + 1)
                if h >= 2:
                    act.wait_ge(pv_done, pv0 + h - 1)
                nc.scalar.activation(probT[h % 2][:, 0:n], T[b][:, 0:n], ACT.Copy).then_inc(te[b], 1)

            for h in range(XH + 1):
                if h < XH:
                    act.wait_ge(s_max, h + 1)
                    if h < 2:
                        act.wait_ge(tf[1], TB["xa"][1] + 1)
                    else:
                        act.wait_ge(tf[2 + h % 2], TB["xa"][2 + h % 2] + h // 2)
                    exps(h, lambda tt: T2[h % 2][:, tt, :], te[h % 2], False)
                if h >= 1:
                    prob_out(h - 1, "xa", 0, 2 * L)
            down_first("xo", lambda j: act.wait_ge(pv_taken, j + 1))
            after_down(U_UP1, N_P2, N_H2, 2, "norm_pre", 2 * KC)

            def ffn(n, down_name):
                unit, _, tb, cw, cb = FFN[n]
                m0 = (n - 1) * FB

                def gate_conv(i):
                    for b in range(2):
                        act.wait_ge(tf[b], i + (tb[b] + 1))
                    for k in range(4):
                        c = i * 4 + k
                        ins = nc.scalar.activation(chunk(bigc, c), T2[k // 2][:, k % 2, :], ACT.Identity, bias=col(cb, c),
                                                   scale=col(cw, c + (FFN_TAPS - 1) * 2 * FC))
                    ins.then_inc(gate_tap, 1)

                def gate_silu(i):
                    for b in range(2):
                        act.wait_ge(te[b], i + (tb[b] + 1))
                    g = big[:, bass.ds(i * (4 * L), 4 * L)]
                    nc.scalar.activation(g, g, ACT.Silu).then_inc(gate_act, 1)

                def val_conv(i, first):
                    for b in range(2, 4):
                        act.wait_ge(tf[b], i + (tb[b] + 1))
                    if not first:
                        act.wait_ge(ffn_mul, i + m0)
                    for k in range(4):
                        c = i * 4 + (k + FC)
                        ins = nc.scalar.activation(vbc[:, k, :], T2[2 + k // 2][:, k % 2, :], ACT.Identity, bias=col(cb, c),
                                                   scale=col(cw, c + (FFN_TAPS - 1) * 2 * FC))
                    ins.then_inc(val_tap, 1)

                def pair(i, prev, val_first=False):
                    q, land = i * 8 + 4 * unit, i * 32 + landed(unit)
                    for j in range(2):
                        hi(q + 4, land + 16, j)
                    if prev:
                        val_conv(i - 1, val_first)
                    for j in range(2, 4):
                        hi(q + 4, land + 16, j)
                    evac(q, 0, u2[:, 0])
                    for j in range(2):
                        hi(q + 8, land + 32, j)
                    gate_conv(i)
                    hi(q + 8, land + 32, 2)
                    gate_silu(i)
                    hi(q + 8, land + 32, 3)
                    evac(q + 4, 1, u2[:, 1])

                pair(0, False)
                pair(1, True, True)
                with nc.scalar.Fori(0, FB - 2) as i:
                    pair(i + 2, True)
                down_first(down_name, lambda j: act.wait_ge(ffn_mul, m0 + 1))
                val_conv(FB - 1, False)
                act.wait_ge(ffn_mul, m0 + FB)
                down_rest(down_name)

            ffn(1, "dn1")
            after_down(U_IN2, N_P3, N_1, 3, "norm1_g_2", 0)

            units = IN2_UNITS
            for k, (unit, kind, half_) in enumerate(units):
                if k + 1 < len(units) and units[k + 1][0] == U_ODD:
                    for j in range(4):
                        hi(4 * U_ODD, 48, j, ODD, odd_landed[j])
                else:
                    hi_unit(unit + 1)
                pr = k % 2
                if kind in IN2_SLOT:
                    s, turn = IN2_SLOT[kind], IN2_TURN[kind] + half_
                    if turn:
                        act.wait_ge(tf[2 * s + 1], TB["in2"][2 * s + 1] + IN2_USE[kind][1] + half_)
                    evac(4 * unit, pr, u2[:, s])
                elif kind == "odd":
                    act.wait_ge(m2_landed, 64)
                    evac(4 * unit, pr, odd, ODD)
                    act.wait_ge(proj_evac, E_ODD)
                    for tt in range(TT):
                        square(N_CKV, tt, odd[:, tt, 0:RANK], x[:, 3072 + RANK * tt:3072 + RANK * (tt + 1)])
                    act.wait_ge(exp_asked, 3)
                    nc.scalar.activation(fox_tmp[2], fox_tmp[2], ACT.Exp).then_inc(exp_done, 1)
                else:
                    evac(4 * unit, pr, bv[:, :, half_ * BLK:(half_ + 1) * BLK])

            for h in range(AH):
                b = h % 4
                act.wait_ge(tf[b], TB["qlat"][b] + h // 4 + 1)
                nc.scalar.activation(qlT[:, h], T2[b], ACT.Copy).then_inc(te[b], 1)
            for n in range(IH):
                b = n % 4
                act.wait_ge(tf[b], TB["idx"][b] + n // 4 + 1)
                if n >= 4:
                    act.wait_ge(relu_used, n - 3)
                nc.scalar.activation(rl[b], T[b][:, 0:P + L], ACT.Relu, scale=float(ID) ** -0.5).then_inc(te[b], 1)
            for name, k0 in (("fox", 0), ("dsa", BH)):
                for h in range(AH + 1):
                    if h < AH:
                        act.wait_ge(s_max, XH + k0 + h + 1)
                        exps(k0 + h, lambda tt: prob[h % 2][:, tt, :], p_exp)
                    if h >= 1:
                        prob_out(h - 1, name, XH + k0)
            down_first("wo2", lambda j: act.wait_ge(uv_taken, AH))
            down_rest("wo2")
            after_down(U_UP2, None, N_2, 4, "norm2_g_2", 0, tmp_big)
            ffn(2, "dn2")
            for tt in range(TT):
                square_residual(N_FIN, 5, tt, xn_big)

        @block.tensor
        def _(pe):
            def bank_free(b, uses):
                if not isinstance(uses, int) or uses:
                    pe.wait_ge(te[b], uses)

            def up(q, pair, n, evac_before, after=None, norm=None, turned=False):
                def products(j, tt):
                    wh, wl = quad(w_hi, j, n), quad(w_lo, j, n)
                    for c in range(4):
                        k = 4 * j + c
                        for t in tt:
                            o = PB[2 * pair + t][:, 0:n]
                            h, l = (a[:, k, t * P:(t + 1) * P] for a in (hT_hi, hT_lo))
                            nc.tensor.matmul(o, h, wh[:, c, :], start=(k == 0), stop=False)
                            nc.tensor.matmul(o, h, wl[:, c, :], start=False, stop=False)
                            ins = nc.tensor.matmul(o, l, wh[:, c, :], start=False, stop=(k == KC - 1))
                    return ins

                by_tile = norm is not None and norm[0] in BY_TILE

                def split(tt, j):
                    _, _, empty, uses = h_bank(norm[0], tt, j)
                    pe.wait_ge(empty, uses + 1)

                if norm is not None and not turned:
                    norm_transposes(norm[0], norm[1], (0,))
                if norm is not None and not by_tile:
                    norm_transposes(norm[0], norm[1], (1,))
                if evac_before is not None:
                    pe.wait_ge(proj_evac, evac_before)
                if by_tile:
                    for j in range(4):
                        split(0, j)
                        pe.wait_ge(lo_ready, q + j + 1)
                        products(j, (0,))
                        if j == 1:
                            norm_transposes(norm[0], norm[1], (1,), norm[2])
                for j in range(4):
                    if norm is not None:
                        split(1, j)
                    if not by_tile:
                        pe.wait_ge(lo_ready, q + j + 1)
                    ins = products(j, (1,) if by_tile else (0, 1))
                    ins.then_inc(quad_used, 1)
                    if after and j in after:
                        after[j]()

            def down(name, free, k, after=None):
                unit, xi, n, _ = DOWN[name]

                def tile(j, tt, first, last):
                    h, l = (t[:, j, tt * P:(tt + 1) * P] for t in (hT_hi, hT_lo))
                    for a, w in ((h, w_hi), (h, w_lo), (l, w_hi)):
                        for nb in range(NB):
                            ins = nc.tensor.matmul(acc[tt][nb][:, :], a, w[:, j, nb * BLK:(nb + 1) * BLK],
                                                   start=(first and j == 0 and a is h and w is w_hi),
                                                   stop=(last and j == 3 and a is l))
                    return ins

                def operands(q, xq, j):
                    pe.wait_ge(xs_lo, xq + j + 1)
                    pe.wait_ge(lo_ready, q + j + 1)

                def by_tile(q, xq, tiles, first, last):
                    for m, tt in enumerate(tiles):
                        if first:
                            free[tt]()
                        for j in range(4):
                            if m == 0:
                                operands(q, xq, j)
                            ins = tile(j, tt, first, last)
                            if m == 1:
                                ins.then_inc(quad_used, 1)
                            elif first and after and j in after:
                                after[j]()
                        if last and m == 0:
                            ins.then_inc(tile0_done, 1)

                if n == 1:
                    by_tile(4 * unit, xi, (0, 1), True, True)
                else:
                    by_tile(4 * unit, xi, (0, 1), True, False)
                    with nc.tensor.Fori(0, n - 2) as i:
                        for j in range(4):
                            operands(i * 4 + 4 * (unit + 1), i * 4 + (xi + 4), j)
                            tile(j, 0, False, False)
                            tile(j, 1, False, False).then_inc(quad_used, 1)
                    by_tile(4 * (unit + n - 1), xi + 4 * (n - 1), (0, 1), False, True)

            def banks_free(phase):
                for b in range(4):
                    bank_free(b, TB[phase][b])

            def norm_transposes(n, src, tiles, scratch=None):
                for tt in tiles:
                    diagonal = (n, tt) in DIAGONAL
                    if diagonal:
                        pe.wait_ge(diag_ready, DIAGONAL.index((n, tt)) + 1)
                    for b in range(4):
                        bank, full, empty, uses = h_bank(n, tt, b)
                        if uses:
                            pe.wait_ge(empty, uses)
                        if not diagonal:
                            pe.wait_ge(xn_ready, NB * BY_TILE.index(n) + b + 1)
                        for c in range(4):
                            k = 4 * b + c
                            o, f = bank[:, c * P:(c + 1) * P], slice(k * P, (k + 1) * P)
                            if diagonal:
                                ins = nc.tensor.matmul(o, src[:, tt, f], diag[:, tt, :], start=True, stop=True)
                            else:
                                ins = nc.tensor.transpose(o, scratch[:, tt, f], ident[:, :])
                        ins.then_inc(full, 1)

            def turn_block(b0, uses, stage):
                for b in range(2):
                    bank_free(b0 + b, uses[b])
                    for c in range(2):
                        for tt in range(TT):
                            ins = nc.tensor.transpose(T2[b0 + b][:, c, tt * P:(tt + 1) * P],
                                                      stage[:, tt, (2 * b + c) * P:(2 * b + c + 1) * P], ident[:, :])
                    ins.then_inc(tf[b0 + b], 1)

            pe.wait_ge(consts_ready, 2)
            def turn_rows(r, b, c):
                k = min(P, NCOL - r * P)
                return nc.tensor.transpose(T[b][:, c * P:c * P + k], rows[0:k, r, :], ident[0:k, 0:k])

            pe.wait_ge(rows0_landed, 16 * sum(r < P for _, _, r, _ in ROW_LOADS))
            turn_rows(0, 2, 0).then_inc(tf[2], 1)

            def turn_keys():
                pe.wait_ge(proj_evac, E_KV)
                turn_block(0, TB["kv"], u2[:, 0])

            def turn_other_rows():
                pe.wait_ge(rows_landed, 16 * sum(r >= P for _, _, r, _ in ROW_LOADS))
                for b in range(2):
                    bank_free(b, TB["params"][b])
                    for c in range(4):
                        ins = turn_rows(1 + 4 * b + c, b, c)
                    ins.then_inc(tf[b], 1)

            up(0, 0, BLK, None, {0: turn_other_rows}, (N_MEM, xn_big))
            up(4, 1, BLK, None, {1: turn_keys, 2: lambda: norm_transposes(N_X, xt, (0,))})
            up(4 * U_DT, 0, HEADS, E_KV, None, (N_X, xt), True)
            tb = TB["ssd"]

            def cumulative_sums():
                pe.wait_ge(da_ready, 1)
                bank_free(2, TB["dt"][2])
                for c in range(TT):
                    nc.tensor.matmul(T[2][:, c * HEADS:(c + 1) * HEADS], triu[:, :], da[:, c, :], start=True, stop=True)
                nc.tensor.matmul(T[2][:, TT * HEADS:(TT + 1) * HEADS], ones[:, :], da[:, 0, :], start=True, stop=True)\
                    .then_inc(tf[2], 1)
                bank_free(3, TB["dt"][3])
                for c in range(TT):
                    ins = nc.tensor.matmul(T[3][0:HEADS, c * P:(c + 1) * P], da[:, c, :], triu[:, :], start=True, stop=True)
                ins.then_inc(tf[3], 1)

            def turn_bc(g):
                pe.wait_ge(proj_evac, g * 3 + E_SSD)
                bank_free(0, g * 4 + tb[0])
                for k in range(2):
                    for tt in range(TT):
                        ins = nc.tensor.transpose(T2[0][:, k, tt * P:(tt + 1) * P], u_bc[:, tt, k * NST:(k + 1) * NST], ident[:, :])
                ins.then_inc(tf[0], 1)

            def cb_products(g):
                pe.wait_ge(bc_ready, g + 1)
                bank_free(1, g * 4 + tb[1])
                for c in range(TT):
                    nc.tensor.matmul(T[1][:, c * P:(c + 1) * P], bc[:, 0, c * P:(c + 1) * P], bc[:, 1, c * P:(c + 1) * P],
                                     start=True, stop=True)
                nc.tensor.transpose(T[1][:, TT * P:(TT + 1) * P], bc[:, 0, 0:P], ident[:, :]).then_inc(tf[1], 1)

            def turn_xs(g):
                pe.wait_ge(proj_evac, g * 3 + (E_SSD + 1))
                turn_block(0, [g * 4 + (tb[b] + 1) for b in range(2)], u_xs)

            def back_xs(g):
                pe.wait_ge(xc_ready, g + 1)
                for tt in range(TT):
                    bank_free(tt, g * 4 + (tb[tt] + 2))
                    for k in range(4):
                        ins = nc.tensor.transpose(T[tt][:, k * P:(k + 1) * P], xc[:, k, tt * P:(tt + 1) * P], ident[:, :])
                    ins.then_inc(tf[tt], 1)

            def states_and_diagonal(g):
                pe.wait_ge(bd_ready, g + 1)
                bank_free(0, g * 4 + (tb[0] + 3))
                nc.tensor.matmul(T[0][:, :], bm, bd, start=True, stop=True).then_inc(tf[0], 1)
                pe.wait_ge(m_ready, g + 1)
                for c in range(TT):
                    bank_free(2 + c, g * 2 + tb[2 + c])
                    for h in range(HPG):
                        ins = nc.tensor.matmul(T[2 + c][:, h * HD:(h + 1) * HD], ssd_m[:, h, c * P:(c + 1) * P],
                                               xdt[:, c, h * HD:(h + 1) * HD], start=True, stop=True)
                    ins.then_inc(tf[2 + c], 1)

            def from_states(g):
                pe.wait_ge(te[0], g * 4 + (tb[0] + 4))
                bank_free(1, g * 4 + (tb[1] + 3))
                nc.tensor.matmul(T[1][:, :], bc[:, 1, P:2 * P], states, start=True, stop=True).then_inc(tf[1], 1)

            def turn_y(g):
                pe.wait_ge(yg_ready, g + 1)
                turn_block(2, [g * 2 + (tb[2 + b] + 1) for b in range(2)], yg)

            def group(g, odd_group, prev):
                q = g * 12 + 4 * U_SSD
                late = (lambda f: lambda: f(g - 1)) if prev else (lambda f: lambda: None)
                pair = [(U_SSD + odd_group + k) % 2 for k in range(3)]
                up(q, pair[0], 2 * NST, g * 3 + (E_SSD - 2), {1: late(back_xs)})
                if not prev:
                    cumulative_sums()
                up(q + 4, pair[1], BLK, g * 3 + (E_SSD - 1),
                   {0: late(states_and_diagonal), 1: late(from_states), 2: lambda: turn_bc(g), 3: late(turn_y)})
                up(q + 8, pair[2], BLK, g * 3 + E_SSD, {0: lambda: cb_products(g), 1: lambda: turn_xs(g)})

            group(0, 0, False)
            with nc.tensor.Fori(0, GROUPS // 2 - 1) as i:
                group(i * 2 + 1, 1, True)
                group(i * 2 + 2, 0, True)
            last = GROUPS - 1
            group(last, 1, True)
            back_xs(last)
            down("wout", [lambda: pe.wait_ge(proj_evac, E_SSD + 3 * GROUPS - 1), lambda: banks_free(N_H1)], 1,
                 {1: lambda: states_and_diagonal(last), 2: lambda: from_states(last), 3: lambda: turn_y(last)})
            up(4 * U_XQ, 0, XW, None, norm=(N_H1, xt, xn_big))
            pe.wait_ge(proj_evac, E_XQ)
            turn_block(0, TB["xa"], u2[:, 0])
            pe.wait_ge(kv_loaded, 32)

            def turn_probs(h, name, k, causal=True):
                b = 2 + h % 2
                pe.wait_ge(p_ready, k + 1)
                bank_free(b, TB[name][b] + h // 2)
                for s, tt, c in blocks(causal):
                    ins = nc.tensor.transpose(T[b][:, c:c + P], prob[h % 2][:, tt, s * P:(s + 1) * P], ident[:, :])
                ins.then_inc(tf[b], 1)

            def weighted(h, name, k, vals, parts=1, causal=True):
                pe.wait_ge(te[2 + h % 2], TB[name][2 + h % 2] + h // 2 + 1)
                if h >= 2:
                    pe.wait_ge(pv_taken, k - 1)
                for r in range(parts):
                    for tt in range(TT):
                        o = PB[h % 2][:, r * L + tt * P:r * L + (tt + 1) * P]
                        of_tile = [(s, c) for s, t, c in blocks(causal) if t == tt]
                        for s, c in of_tile:
                            ins = nc.tensor.matmul(o, vals(s, r), probT[h % 2][:, c:c + P], start=(s == 0), stop=(s == of_tile[-1][0]))
                ins.then_inc(pv_done, 1)

            for b in range(2):
                pe.wait_ge(te[b], TB["xa"][b] + 1)
            for h in range(XH + 2):
                if h < XH:
                    b = h % 2
                    bank_free(b, TB["xa"][b] + 1 + h // 2)
                    for tt in range(TT):
                        ins = nc.tensor.matmul(T2[b][:, tt, :], xa_qT[:, h, tt * P:(tt + 1) * P], xa_kT[:, h, :], start=True, stop=True)
                    ins.then_inc(tf[b], 1)
                if 1 <= h <= XH:
                    turn_probs(h - 1, "xa", h - 1, False)
                if h >= 2:
                    weighted(h - 2, "xa", h - 2, lambda s, r: xa_v[:, s, (h - 2) * P:(h - 1) * P], 1, False)

            down("xo", [lambda: pe.wait_ge(pv_taken, XH), lambda: banks_free(N_H2)], 2)

            def ffn(n, norm, scratch, down_name, done, down_k):
                unit, e0, tb, _, _ = FFN[n]

                def turn(i, val):
                    pe.wait_ge(proj_evac, i * 2 + (e0 + val))
                    turn_block(2 * val, [i + tb[2 * val + b] for b in range(2)], u2[:, val])

                def pair(i, first):
                    q = i * 8 + 4 * unit
                    up(q, 0, BLK, None if first else i * 2 + (e0 - 2), None if first else {1: lambda: turn(i - 1, 1)},
                       (norm, xt, scratch) if first else None)
                    up(q + 4, 1, BLK, None if first else i * 2 + (e0 - 1), {1: lambda: turn(i, 0)})

                pair(0, True)
                with nc.tensor.Fori(0, FB - 1) as i:
                    pair(i + 1, False)
                turn(FB - 1, 1)

                down(down_name, [lambda: pe.wait_ge(proj_evac, e0 + 2 * FB - 1), lambda: banks_free(done)], down_k)

            ffn(1, N_H2, xn_big, "dn1", N_1, 3)

            units = IN2_UNITS

            def turn_unit(k):
                unit, kind, half_ = units[k]
                pe.wait_ge(proj_evac, E_IN2 + k)
                s = IN2_SLOT[kind]
                turn_block(2 * s, [TB["in2"][2 * s + b] + IN2_USE[kind][b] + half_ for b in range(2)], u2[:, s])

            def turn_odd():
                pe.wait_ge(odd_ready, 1)
                bank_free(0, TB["in2"][0] + 2)
                for r in range(2):
                    for tt in range(TT):
                        ins = nc.tensor.transpose(T2[0][:, r, tt * P:(tt + 1) * P], ckv[:, tt, r * P:(r + 1) * P], ident[:, :])
                ins.then_inc(tf[0], 1)
                bank_free(1, TB["in2"][1] + 2)
                for tt in range(TT):
                    ins = nc.tensor.transpose(T[1][:, tt * P:(tt + 1) * P], aik2[:, tt].rearrange("p k n -> p (k n)"), ident[:, :])
                ins.then_inc(tf[1], 1)
                bank_free(2, TB["in2"][2] + 2)
                c = T[2][0:BH, :]
                nc.tensor.matmul(c[:, 0:P], lf[:, 0, :], triu[:, :], start=True, stop=True)
                nc.tensor.matmul(c[:, P:L], lf[:, 0, :], ones[:, :], start=True, stop=False)
                nc.tensor.matmul(c[:, P:L], lf[:, 1, :], triu[:, :], start=False, stop=True).then_inc(tf[2], 1)

            for k, (unit, kind, half_) in enumerate(units):
                after = {}
                if k and units[k - 1][1] in IN2_SLOT:
                    after[1] = lambda k=k: turn_unit(k - 1)
                if k and units[k - 1][1] == "odd":
                    after[3] = turn_odd
                up(4 * unit, k % 2, ODD if kind == "odd" else BLK, E_IN2 + k - 2 if k >= 2 else None, after,
                   (N_1, xt, xn_big) if k == 0 else None)
            pe.wait_ge(m2_landed, 64)
            bank_free(3, TB["line"][3])
            nc.tensor.matmul(T[3][0:AH, :], table, onehot, start=True, stop=True).then_inc(tf[3], 1)
            pe.wait_ge(uk_landed, 16)
            pe.wait_ge(te[0], TB["in2"][0] + 5)
            for h in range(AH):
                b = h % 4
                bank_free(b, TB["qlat"][b] + h // 4)
                for r in range(2):
                    ins = nc.tensor.matmul(T2[b][:, r, :], w_uk[:, h, r * P:(r + 1) * P], aqT[:, h, :], start=True, stop=True)
                ins.then_inc(tf[b], 1)
            for n in range(IH):
                b = n % 4
                bank_free(b, TB["idx"][b] + n // 4)
                half_ = slice(n % 2 * ID, n % 2 * ID + ID)
                for tt in range(TT):
                    ins = nc.tensor.matmul(T[b][:, ragged[tt]], aiqT[half_, n // 2, tt * P:(tt + 1) * P], aikT[half_, 0:keys(tt)],
                                           start=True, stop=True)
                ins.then_inc(tf[b], 1)
            pe.wait_ge(proj_evac, E_IN2 + len(units) - 1)
            for h in range(BH + 2):
                if h < BH:
                    b = h % 2
                    bank_free(b, TB["fox"][b] + h // 2)
                    pe.wait_ge(cum_row_ready, h + 1)
                    for tt in range(TT):
                        n = keys(tt)
                        nc.tensor.matmul(T2[b][:, tt, 0:n], bqT[:, h, tt * P:(tt + 1) * P], bkT[:, h, 0:n], start=True, stop=False)
                        ins = nc.tensor.matmul(T2[b][:, tt, 0:n], ones[0:BH, :], cum_row[:, 0:n], start=False, stop=True)
                    ins.then_inc(tf[b], 1)
                if 1 <= h <= BH:
                    turn_probs(h - 1, "fox", XH + h - 1)
                if h >= 2:
                    weighted(h - 2, "fox", XH + h - 2, lambda s, r: bv[:, s, (h - 2) * P:(h - 1) * P])
            pe.wait_ge(uv_landed, 16)
            pe.wait_ge(skew_landed, 16)
            pe.wait_ge(m2_consts, 2)
            pe.wait_ge(pv_taken, XH + BH)
            for h in range(AH + 3):
                if h < AH:
                    b = h % 2
                    bank_free(b, TB["dsa"][b] + h // 2)
                    for tt in range(TT):
                        n = keys(tt)
                        for r in range(2):
                            nc.tensor.matmul(T2[b][:, tt, 0:n], qlT[:, h, r, tt * P:(tt + 1) * P], ckvT[:, r, 0:n], start=(r == 0), stop=False)
                        ins = nc.tensor.matmul(T2[b][:, tt, 0:n], anti, skew[:, h, (1 - tt) * P:(1 - tt) * P + n], start=False, stop=True)
                    ins.then_inc(tf[b], 1)
                if 1 <= h <= AH:
                    turn_probs(h - 1, "dsa", XH + BH + h - 1)
                if 2 <= h <= AH + 1:
                    weighted(h - 2, "dsa", XH + BH + h - 2, lambda s, r: ckv[:, s, r * P:(r + 1) * P], 2)
                if h >= 3:
                    g = h - 3
                    pe.wait_ge(pv_taken, XH + BH + g + 1)
                    if g >= 2:
                        pe.wait_ge(uv_taken, g - 1)
                    for r in range(2):
                        ins = nc.tensor.matmul(PB[2 + g % 2][:, 0:L], w_uv[:, g, r, :], o_lat[:, r, :], start=(r == 0), stop=(r == 1))
                    ins.then_inc(uv_done, 1)

            down("wo2", [lambda: pe.wait_ge(uv_taken, AH), lambda: banks_free(N_2)], 4)
            ffn(2, N_2, tmp_big, "dn2", "end", 5)

        @block.vector
        def _(dve):
            own = Chain(dve, dve_own)
            V = nc.vector
            marks = iter(range(1, idle.shape[1]))

            def signal(semaphore):
                k = next(marks)
                V.memset(idle[:, k:k + 1], 0.0).then_inc(semaphore, 1)

            def lo(q, j, n=4 * BLK):
                dve.wait_ge(hi_ready, q + j + 1)
                dst, src, h = (w_lo[:, j, :], raw[:, j, :], w_hi[:, j, :]) if n == 4 * BLK else \
                    (quad(w_lo, j, n), quad(raw, j, n), quad(w_hi, j, n))
                V.tensor_tensor(dst, src, h.bitcast(F32), ALU.subtract).then_inc(lo_ready, 1)

            def lo_unit(unit, n=4 * BLK, js=range(4)):
                for j in js:
                    lo(4 * unit, j, n)

            def mean(n, tt, width):
                s = ssq(n)[:, tt:tt + 1]
                V.tensor_scalar(s, s, 1.0 / width, EPS, ALU.mult, ALU.add).then_inc(ms_done, 1)

            def means(n, width):
                for tt in range(TT):
                    dve.wait_ge(sq_done, sq_count(n, tt))
                    mean(n, tt, width)

            def bank_sums(n, tt):
                dve.wait_ge(sq_done, sq_count(n, tt))
                own(V.tensor_reduce(ssq(n)[:, tt:tt + 1], ssq_parts[:, tt * NB:(tt + 1) * NB], AX_X, ALU.add))

            def h_lo(n, tt, gain, k0, banks=range(4)):
                for b in banks:
                    bank, _, empty, _ = h_bank(n, tt, b)
                    dve.wait_ge(h_hi_done, 8 * t_idx(n) + 4 * tt + b + 1)
                    for c in range(4):
                        k = 4 * b + c
                        s = slice(tt * P, (tt + 1) * P)
                        ins = V.scalar_tensor_tensor(hT_lo[:, k, s], bank[:, c * P:(c + 1) * P], col(gain, k0 + k),
                                                     hT_hi[:, k, s].bitcast(F32), ALU.mult, ALU.subtract)
                    ins.then_inc(empty, 1)

            def down_first(name):
                _, xi, _, src = DOWN[name]
                for j in range(4):
                    dve.wait_ge(xs_hi, xi + j + 1)
                    V.tensor_tensor(hT_lo[:, j, :], src[:, j, :], hT_hi[:, j, :].bitcast(F32), ALU.subtract).then_inc(xs_lo, 1)

            def down_rest(name):
                unit, xi, n, src = DOWN[name]
                with V.Fori(0, n - 1) as i:
                    for j in range(4):
                        lo(i * 4 + 4 * (unit + 1), j)
                        dve.wait_ge(xs_hi, i * 4 + (xi + 4 + j + 1))
                        V.tensor_tensor(hT_lo[:, j, :], chunk(src, i * 4 + (4 + j)), hT_hi[:, j, :].bitcast(F32), ALU.subtract)\
                            .then_inc(xs_lo, 1)

            def branch_added(post, tt, k, scale):
                s1, r1 = ssq(post)[:, tt:tt + 1], rstd(post)[:, tt:tt + 1]
                bank_sums(post, tt)
                if scale is not None:
                    own(V.tensor_tensor(s1, s1, scale[:, tt:tt + 1], ALU.mult))
                    own(V.tensor_tensor(s1, s1, scale[:, tt:tt + 1], ALU.mult))
                mean(post, tt, D)
                dve.wait_ge(rstd_done, nth(post, tt))
                if scale is not None:
                    own(V.tensor_tensor(r1, r1, scale[:, tt:tt + 1], ALU.mult))
                dve.wait_ge(gain_landed, 16 * k)
                s = [slice(nb * BLK, (nb + 1) * BLK) for nb in range(NB)]
                scaled = []
                for nb in range(NB + 1):
                    if nb < NB:
                        scaled.append(own.mark(V.scalar_tensor_tensor(tmp_big[:, tt, s[nb]], acc[tt][nb][:, :], r1, u[:, s[nb]],
                                                                      ALU.mult, ALU.mult)))
                    if nb:
                        dve.wait_ge(dve_own, scaled[nb - 1])
                        V.tensor_tensor(xt[:, tt, s[nb - 1]], xt[:, tt, s[nb - 1]], tmp_big[:, tt, s[nb - 1]], ALU.add)\
                            .then_inc(x_new, 1)

            def product_added(tt, k, unit, src):
                if tt == 0:
                    dve.wait_ge(tile0_done, k)
                else:
                    dve.wait_ge(quad_used, 4 * unit)
                for nb in range(NB):
                    s = slice(nb * BLK, (nb + 1) * BLK)
                    V.tensor_tensor(xt[:, tt, s], acc[tt][nb][:, :], src[:, tt, s], ALU.add).then_inc(x_new, 1)

            def after_down(unit, add, n, gain, k0):
                for tt in range(TT):
                    add(tt)
                    bank_sums(n, tt)
                    mean(n, tt, D)
                    lo_unit(unit, js=(2 * tt,))
                    h_lo(n, 0, gain, k0, (2 * tt,))
                    if tt == 0:
                        lo_unit(unit, js=(1,))
                        h_lo(n, 0, gain, k0, (1,))
                h_lo(n, 0, gain, k0, (3,))
                lo_unit(unit, js=(3,))
                h_lo(n, 1, gain, k0)

            def softplus(tmp, ask):
                terms = 7
                own(V.tensor_scalar(tmp[1], tmp[0], 0.0, None, ALU.max))
                V.scalar_tensor_tensor(tmp[2], tmp[0], -1.0, tmp[0], ALU.mult, ALU.min).then_inc(exp_asked, 1)
                dve.wait_ge(exp_done, ask)
                own(V.tensor_scalar(tmp[3], tmp[2], 2.0, None, ALU.add))
                own(V.reciprocal(tmp[4], tmp[3]))
                own(V.tensor_tensor(tmp[5], tmp[2], tmp[4], ALU.mult))
                own(V.tensor_tensor(tmp[6], tmp[5], tmp[5], ALU.mult))
                own(V.tensor_scalar(tmp[7], tmp[6], 1.0 / (2 * terms + 1), None, ALU.mult))
                for k in range(terms - 1, 0, -1):
                    own(V.scalar_tensor_tensor(tmp[7], tmp[7], 1.0 / (2 * k + 1), tmp[6], ALU.add, ALU.mult))
                own(V.scalar_tensor_tensor(tmp[7], tmp[7], 1.0, tmp[5], ALU.add, ALU.mult))
                own(V.scalar_tensor_tensor(tmp[0], tmp[7], 2.0, tmp[1], ALU.mult, ALU.add))

            def tap(dst, src, shift, w):
                return V.scalar_tensor_tensor(dst[:, shift:L], src[:, 0:L - shift], w, dst[:, shift:L], ALU.mult, ALU.add)

            dve.wait_ge(tf[2], 1)
            V.tensor_copy(cols[:, 0:P], T[2][:, 0:P]).then_inc(te[2], 1)
            dve.wait_ge(te[2], 1)
            signal(cols_ready)
            means(N_MEM, D)
            h_lo(N_MEM, 0, "norm_mem", 0)
            lo_unit(0, js=(0,))
            h_lo(N_MEM, 1, "norm_mem", 0)
            lo_unit(0, js=(1,))
            for b in range(2):
                dve.wait_ge(tf[b], TB["params"][b] + 1)
                c0 = P + b * BLK
                n = min(BLK, NCOL - c0)
                V.tensor_copy(cols[:, c0:c0 + n], T[b][:, 0:n]).then_inc(te[b], 1)
            dve.wait_ge(te[1], TB["params"][1] + 1)
            signal(cols_ready)
            lo_unit(0, js=(2, 3))
            means(N_X, D)
            lo_unit(1)
            for b in range(2):
                dve.wait_ge(tf[b], TB["kv"][b] + 1)
                own(V.tensor_copy(vbc[:, 2 * b:2 * b + 2, :], T2[b]))
                signal(te[b])
            signal(kT_copied)
            lo_unit(U_DT, HEADS)
            for tt in range(TT):
                h_lo(N_X, tt, "norm_pre", 0)
            for j in range(4):
                lo(4 * U_SSD, j, 2 * NST)

            dve.wait_ge(proj_evac, E_DT)
            dve.wait_ge(small_landed, 48)
            dve.wait_ge(kv_stored, 32)
            own(V.memset(yssq[:, 0, :], 0.0))
            t0 = sp_tmp[0].rearrange("p (a h) -> p a h", a=TT)
            own(V.tensor_tensor(t0, t0, dt_bias.unsqueeze(1).broadcast_to([P, TT, HEADS]), ALU.add))
            softplus(sp_tmp, 2)
            own(V.tensor_copy(vb[:, 0:128], sp_tmp[0]))
            V.scalar_tensor_tensor(da, dt, -1.0, a_log.unsqueeze(1).broadcast_to([P, TT, HEADS]), ALU.mult, ALU.mult)\
                .then_inc(da_ready, 1)

            def sums():
                dve.wait_ge(tf[2], TB["dt"][2] + 1)
                own(V.tensor_copy(vb[:, 256:384], T[2][:, 0:128]))
                own(V.tensor_tensor(dte, T[2][:, 128:192], acs[:, 0, :], ALU.subtract))
                signal(te[2])
                signal(exp_asked)
                dve.wait_ge(tf[3], TB["dt"][3] + 1)
                own(V.tensor_copy(acsT, T[3][0:HEADS, 0:L]))
                signal(te[3])
                signal(acsT_ready)
                dve.wait_ge(exp_done, 4)

            tb = TB["ssd"]

            def by_head(a, g, n=HPG):
                return a[:, bass.ds(g * HPG, HPG)].unsqueeze(2).broadcast_to([P, HPG, HD])

            heads = lambda a: a.rearrange("p (h d) -> p h d", d=HD)

            def bc_taps(g):
                dve.wait_ge(bc_tap, g + 1)
                for t in range(SSD_TAPS - 2, -1, -1):
                    for k in range(2):
                        ins = tap(bc[:, k, :], T2[0][:, k, :], SSD_TAPS - 1 - t, col("ssd_conv_w", g + (32 + 8 * k + t * CONV_CH)))
                    if t:
                        own(ins)
                ins.then_inc(te[0], 1)

            def xs_taps(g):
                dve.wait_ge(xs_tap, g + 1)
                for t in range(SSD_TAPS - 2, -1, -1):
                    for k in range(4):
                        ins = tap(xc[:, k, :], T2[k // 2][:, k % 2, :], SSD_TAPS - 1 - t, col("ssd_conv_w", g * 4 + (k + t * CONV_CH)))
                        if t == 0 and k % 2:
                            ins.then_inc(te[k // 2], 1)
                    if t:
                        own(ins)

            def cb_out(g):
                dve.wait_ge(tf[1], g * 4 + (tb[1] + 1))
                V.tensor_tensor(cbm, T[1][:, 0:2 * P].rearrange("p (a t) -> p a t", a=TT),
                                triu[:, :].unsqueeze(1).broadcast_to([P, TT, P]), ALU.mult)
                V.tensor_copy(bm, T[1][:, 2 * P:3 * P]).then_inc(te[1], 1)

            def decayed(g):
                dve.wait_ge(te[1], g * 4 + (tb[1] + 1))
                dve.wait_ge(decay_ready, g + 1)
                for c in range(TT):
                    m = ssd_m[:, :, c * P:(c + 1) * P]
                    ins = V.tensor_tensor(m, m, cbm[:, c, :].unsqueeze(1).broadcast_to([P, HPG, P]), ALU.mult)
                ins.then_inc(m_ready, 1)

            def xs_back(g):
                for tt in range(TT):
                    dve.wait_ge(tf[tt], g * 4 + (tb[tt] + 3))
                    dve.wait_ge(tf[2 + tt], g * 2 + tb[2 + tt])
                for tt in range(TT):
                    V.tensor_tensor(heads(xdt[:, tt, :]), heads(T[tt][:, :]), by_head(dt[:, tt, :], g), ALU.mult)
                    ins = V.tensor_tensor(heads(yg[:, tt, :]), heads(T[tt][:, :]), by_head(d_skip, g), ALU.mult)
                    ins.then_inc(te[tt], 1)
                dve.wait_ge(te[1], g * 4 + (tb[1] + 3))
                V.tensor_tensor(heads(bd), heads(xdt[:, 0, :]), by_head(dte, g), ALU.mult).then_inc(bd_ready, 1)

            def gather(g):
                dve.wait_ge(tf[1], g * 4 + (tb[1] + 4))
                V.tensor_tensor(heads(bd), heads(T[1][:, :]), by_head(eacs, g), ALU.mult).then_inc(te[1], 1)
                dve.wait_ge(te[1], g * 4 + (tb[1] + 4))
                own(V.tensor_tensor(bd, bd, yg[:, 1, :], ALU.add))
                for c in range(TT):
                    dve.wait_ge(tf[2 + c], g * 2 + (tb[2 + c] + 1))
                    V.tensor_tensor(yg[:, c, :], T[2 + c][:, :], (yg[:, 0, :], bd)[c], ALU.add).then_inc(te[2 + c], 1)
                dve.wait_ge(proj_evac, g * 3 + (E_SSD + 2))
                for c in range(TT):
                    dve.wait_ge(te[2 + c], g * 2 + (tb[2 + c] + 1))
                V.tensor_tensor(yg, yg, zs, ALU.mult).then_inc(yg_ready, 1)
                dve.wait_ge(yg_ready, g + 1)
                for c in range(TT):
                    own(V.tensor_tensor_reduce(bd, yg[:, c, :], yg[:, c, :], 1.0, 0.0, ALU.mult, ALU.add,
                                               accum_out=yssq[:, 1, c:c + 1]))
                own(V.tensor_tensor(yssq[:, 0, :], yssq[:, 0, :], yssq[:, 1, :], ALU.add))

            def group(g, prev, nxt):
                q = g * 12 + 4 * U_SSD

                def lo_next(j):
                    if nxt:
                        lo(q + 12, j, 2 * NST)
                    else:
                        lo(4 * U_WOUT, j)

                for j in range(4):
                    lo(q + 4, j)
                    if j == 1 and prev:
                        xs_back(g - 1)
                if not prev:
                    sums()
                lo(q + 8, 0)
                if prev:
                    gather(g - 1)
                lo(q + 8, 1)
                bc_taps(g)
                lo(q + 8, 2)
                lo(q + 8, 3)
                lo_next(0)
                cb_out(g)
                lo_next(1)
                xs_taps(g)
                lo_next(2)
                if not nxt:
                    down_first("wout")
                decayed(g)
                lo_next(3)

            group(0, False, True)
            with V.Fori(0, GROUPS // 2 - 1) as i:
                own.enter(i, 16)
                group(i * 2 + 1, True, True)
                group(i * 2 + 2, True, True)
            own.leave(GROUPS // 2 - 1)
            group(GROUPS - 1, True, False)
            xs_back(GROUPS - 1)
            gather(GROUPS - 1)
            own(V.tensor_copy(ssq(N_Y), yssq[:, 0, :]))
            for tt in range(TT):
                mean(N_Y, tt, DI)
            down_rest("wout")
            dve.wait_ge(rstd_done, nth(N_Y, TT - 1))
            dve.wait_ge(x_back, 16)
            after_down(U_XQ, lambda tt: branch_added(N_P1, tt, 1, rstd(N_Y)), N_H1, "norm_pre", KC)

            lo_unit(U_XO, js=(0, 1, 2))
            for b in range(2):
                dve.wait_ge(tf[b], TB["xa"][b] + 1)
                V.tensor_copy(xa_qT[:, 2 * b:2 * b + 2, :], T2[b]).then_inc(te[b], 1)
            lo_unit(U_XO, js=(3,))

            def scale_probs(k, causal=True):
                par = k % 2
                own(V.reciprocal(rden[:, 2 * par:2 * par + 2], den[:, 2 * par:2 * par + 2]))
                for tt in range(TT):
                    p = prob[par][:, tt, 0:keys(tt, causal)]
                    ins = V.tensor_scalar(p, p, rden[:, 2 * par + tt:2 * par + tt + 1], None, ALU.mult)
                ins.then_inc(p_ready, 1)

            for h in range(XH + 2):
                if 1 <= h <= XH:
                    b = (h - 1) % 2
                    dve.wait_ge(te[b], TB["xa"][b] + 1 + (h - 1) // 2 + 1)
                    scale_probs(h - 1, False)
                if h < XH:
                    b = h % 2
                    dve.wait_ge(tf[b], TB["xa"][b] + 1 + h // 2 + 1)
                    V.tensor_reduce(mx[:, 2 * b:2 * b + 2], T2[b], AX_X, ALU.max, negate=True).then_inc(s_max, 1)
                if h >= 2:
                    dve.wait_ge(pv_done, h - 1)
                    V.tensor_copy(xa_oT[:, h - 2, :], PB[h % 2][:, 0:L]).then_inc(pv_taken, 1)
            down_first("xo")
            after_down(U_UP1, lambda tt: branch_added(N_P2, tt, 2, None), N_H2, "norm_pre", 2 * KC)

            def ffn(n, down_name):
                unit, _, tb, cw, cb = FFN[n]
                m0 = (n - 1) * FB

                def gate_taps(i):
                    dve.wait_ge(gate_tap, i + (m0 + 1))
                    for t in range(FFN_TAPS - 2, -1, -1):
                        for k in range(4):
                            c = i * 4 + k
                            ins = tap(chunk(bigc, c), T2[k // 2][:, k % 2, :], FFN_TAPS - 1 - t, col(cw, c + t * 2 * FC))
                            if t == 0 and k % 2:
                                ins.then_inc(te[k // 2], 1)
                        if t:
                            own(ins)

                def val_taps(i):
                    dve.wait_ge(val_tap, i + (m0 + 1))
                    for t in range(FFN_TAPS - 2, -1, -1):
                        for k in range(4):
                            ins = tap(vbc[:, k, :], T2[2 + k // 2][:, k % 2, :], FFN_TAPS - 1 - t, col(cw, i * 4 + (k + FC + t * 2 * FC)))
                            if t == 0 and k % 2:
                                ins.then_inc(te[2 + k // 2], 1)
                        if t:
                            own(ins)
                    dve.wait_ge(te[3], i + (tb[3] + 1))
                    dve.wait_ge(gate_act, i + (m0 + 1))
                    g = big[:, bass.ds(i * (4 * L), 4 * L)]
                    V.tensor_tensor(g, g, vb[:, :], ALU.mult).then_inc(ffn_mul, 1)

                def pair(i, prev):
                    q = i * 8 + 4 * unit
                    for j in range(4):
                        lo(q + 4, j)
                        if j == 1 and prev:
                            val_taps(i - 1)
                    for j in range(4):
                        lo(q + 8, j)
                        if j == 1:
                            gate_taps(i)

                pair(0, False)
                with V.Fori(0, FB - 1) as i:
                    own.enter(i, 2)
                    pair(i + 1, True)
                own.leave(FB - 1)
                down_first(down_name)
                val_taps(FB - 1)
                dve.wait_ge(ffn_mul, m0 + FB)
                down_rest(down_name)

            ffn(1, "dn1")
            after_down(U_IN2, lambda tt: branch_added(N_P3, tt, 3, None), N_1, "norm1_g_2", 0)

            units = IN2_UNITS
            dest = {"aq": aqT, "aiq": aiqT, "bq": bqT, "bk": bkT}
            factor = {"aq": SCALE, "bq": SCALE}

            def unit_out(k):
                unit, kind, half_ = units[k]
                s = IN2_SLOT[kind]
                for b in range(2):
                    t = 2 * s + b
                    dve.wait_ge(tf[t], TB["in2"][t] + IN2_USE[kind][b] + half_ + 1)
                    c = 4 * half_ + 2 * b
                    V.tensor_scalar(dest[kind][:, c:c + 2, :], T2[t], factor.get(kind, 1.0), None, ALU.mult).then_inc(te[t], 1)

            def odd_in():
                dve.wait_ge(proj_evac, E_ODD)
                for tt in range(TT):
                    for k in range(2):
                        V.tensor_copy(aik2[:, tt, k, :], odd[:, tt, RANK:RANK + ID])
                V.tensor_scalar(iw, odd[:, :, RANK + ID:RANK + ID + IH], float(IH) ** -0.5, None, ALU.mult)
                f0 = fox_tmp[0].rearrange("p (a h) -> p a h", a=TT)
                own(V.scalar_tensor_tensor(f0, odd[:, :, RANK + ID + IH:ODD], -1.0,
                                           fg_bias.unsqueeze(1).broadcast_to([P, TT, BH]), ALU.mult, ALU.subtract))
                softplus(fox_tmp, 5)
                own(V.tensor_copy(x[:, 2560:2576], fox_tmp[0]))
                means(N_CKV, RANK)
                dve.wait_ge(rstd_done, nth(N_CKV, TT - 1))
                for tt in range(TT):
                    ins = V.scalar_tensor_tensor(ckv[:, tt, :], odd[:, tt, 0:RANK], rstd(N_CKV)[:, tt:tt + 1], kv_gain, ALU.mult, ALU.mult)
                ins.then_inc(odd_ready, 1)

            def odd_out():
                dve.wait_ge(tf[0], TB["in2"][0] + 3)
                V.tensor_copy(ckvT, T2[0]).then_inc(te[0], 1)
                dve.wait_ge(tf[1], TB["in2"][1] + 3)
                V.tensor_copy(aikT, T[1][:, 0:L]).then_inc(te[1], 1)
                dve.wait_ge(tf[2], TB["in2"][2] + 3)
                own(V.tensor_copy(cumT, T[2][0:BH, 0:L]))
                signal(te[2])
                signal(decay_sum_ready)

            dve.wait_ge(m2_landed, 64)
            for k, (unit, kind, half_) in enumerate(units):
                nxt = ODD if unit + 1 == U_ODD else 4 * BLK
                for j in range(4):
                    lo(4 * (unit + 1), j, nxt)
                    if j == 1 and k and units[k - 1][1] in IN2_SLOT:
                        unit_out(k - 1)
                if kind == "odd":
                    odd_in()
                if k and units[k - 1][1] == "odd":
                    odd_out()
            dve.wait_ge(tf[3], TB["line"][3] + 1)
            own(V.tensor_copy(line, T[3][0:AH, :]))
            signal(te[3])
            signal(line_ready)

            for n in range(IH):
                dve.wait_ge(te[n % 4], TB["idx"][n % 4] + n // 4 + 1)
                if n:
                    dve.wait_ge(relu_used, n)
                for tt in range(TT):
                    w, s, r = iw[:, tt, n:n + 1], score[:, tt, 0:keys(tt)], rl[n % 4][:, ragged[tt]]
                    if n == 0:
                        ins = V.tensor_scalar(s, r, w, None, ALU.mult)
                    else:
                        ins = V.scalar_tensor_tensor(s, r, w, s, ALU.mult, ALU.add)
                ins.then_inc(relu_used, 1)
            dve.wait_ge(relu_used, IH)
            dve.wait_ge(m2_consts, 2)
            for tt in range(TT):
                n = keys(tt)
                own(V.tensor_tensor(sel[:, tt, 0:n], score[:, tt, 0:n], mask[:, tt, 0:n], ALU.add))

            def top_round(r):
                src = sel if r == 0 else score
                for tt in range(TT):
                    ins = V.max(top8[:, tt, :], src[:, tt, 0:keys(tt)])
                own(ins)
                for tt in range(TT):
                    n = keys(tt)
                    ins = V.match_replace(score[:, tt, 0:n], top8[:, tt, :], src[:, tt, 0:n], TAKEN)
                own(ins)

            def attention(name, k0, bias, extra, end):
                for h in range(BH + 2):
                    if 1 <= h <= BH:
                        dve.wait_ge(p_exp, k0 + h)
                        scale_probs(h - 1)
                    if h < BH:
                        b = h % 2
                        dve.wait_ge(tf[b], TB[name][b] + h // 2 + 1)
                        if h >= 2:
                            dve.wait_ge(tf[2 + b], TB[name][2 + b] + h // 2)
                        for tt in range(TT):
                            n = keys(tt)
                            ins = V.tensor_tensor_reduce(prob[b][:, tt, 0:n], T2[b][:, tt, 0:n], bias[:, tt, 0:n], 1.0, TAKEN, ALU.add, ALU.max,
                                                         accum_out=mx[:, 2 * b + tt:2 * b + tt + 1])
                        ins.then_inc(te[b], 1)
                        dve.wait_ge(te[b], TB[name][b] + h // 2 + 1)
                        V.tensor_scalar(mx[:, 2 * b:2 * b + 2], mx[:, 2 * b:2 * b + 2], -1.0, None, ALU.mult).then_inc(s_max, 1)
                        extra(h)
                    if h >= 2:
                        end(h - 2)

            def fox_end(h):
                dve.wait_ge(pv_done, XH + h + 1)
                V.tensor_copy(mixT[:, AH + h, :], PB[h % 2][:, 0:L]).then_inc(pv_taken, 1)

            attention("fox", 0, mask, top_round, fox_end)
            assert TOPK == 8 * BH
            for tt in range(TT):
                s, m = sel[:, tt, 0:keys(tt)], mask[:, tt, 0:keys(tt)]
                own(V.tensor_scalar(s, score[:, tt, 0:keys(tt)], TAKEN, -1.0, ALU.is_equal, ALU.add))
                own(V.scalar_tensor_tensor(s, s, -NEG, m, ALU.mult, ALU.add))

            def mix_out(g):
                dve.wait_ge(uv_done, g + 1)
                V.tensor_copy(mixT[:, g, :], PB[2 + g % 2][:, 0:L]).then_inc(uv_taken, 1)

            def dsa_end(h):
                dve.wait_ge(pv_done, XH + BH + h + 1)
                if h:
                    mix_out(h - 1)
                V.tensor_copy(o_lat, PB[h % 2][:, :].rearrange(bank2, t=L)).then_inc(pv_taken, 1)

            attention("dsa", BH, sel, lambda h: None, dsa_end)
            mix_out(AH - 1)
            down_first("wo2")
            down_rest("wo2")
            dve.wait_ge(x_back, 32)
            after_down(U_UP2, lambda tt: product_added(tt, 4, U_UP2, xn_big), N_2, "norm2_g_2", 0)
            ffn(2, "dn2")
            for tt in range(TT):
                product_added(tt, 5, U_END, xt)
                bank_sums(N_FIN, tt)
                mean(N_FIN, tt, D)
            dve.wait_ge(gain_landed, 64)
            for tt in range(TT):
                dve.wait_ge(rstd_done, nth(N_FIN, tt))
                V.scalar_tensor_tensor(tmp_big[:, tt, :], xt[:, tt, :], rstd(N_FIN)[:, tt:tt + 1], u[:, :], ALU.mult, ALU.mult)\
                    .then_inc(out_ready, 1)


_INS = ["x", "mem", "norm_pre", "norm_post", "norm_mem", "ssd_w_in", "ssd_conv_w", "ssd_conv_b", "ssd_dt_bias",
        "ssd_a_log", "ssd_d", "ssd_norm_g", "ssd_w_out", "xa_w_q", "xa_w_kv", "xa_w_o", "ffn_w_up", "ffn_conv_w",
        "ffn_conv_b", "ffn_w_down", "w_in_2", "kv_norm_g_2", "w_uk_2", "w_uv_2", "t5_table_2", "fgate_b_2", "w_o_2",
        "norm1_g_2", "norm2_g_2", "w_up_2", "conv_w_2", "conv_b_2", "w_down_2", "final_g_2"]


def _bucket_onehot():
    d = np.maximum(L - 1 - np.arange(BLK), 0)
    exact = NBUCKET // 2
    far = exact + (np.log(np.maximum(d, 1) / exact) / np.log(MAXDIST / exact) * (NBUCKET - exact)).astype(np.int32)
    bucket = np.where(d < exact, d, np.minimum(far, NBUCKET - 1))
    return (bucket[None, :] == np.arange(NBUCKET)[:, None]).astype(np.float32)


def kernel(**inputs):
    import concourse.bacc as _bacc
    from concourse.bass_utils import run_bass_kernel_spmd as _run

    nc = _bacc.Bacc("TRN2", target_bir_lowering=False, num_devices=1)
    arrays, aps = {}, {}
    for name in _INS + ["bucket_onehot"]:
        a = _bucket_onehot() if name == "bucket_onehot" else np.ascontiguousarray(inputs[name])
        arrays[f"in_{name}_dram"] = a
        aps[name] = nc.dram_tensor(f"in_{name}_dram", a.shape, mybir.dt.from_np(a.dtype), kind="ExternalInput").ap()
    out = nc.dram_tensor("out_0_dram", (1, L, D), F32, kind="ExternalOutput").ap()
    program(nc, aps, out)
    r = _run(nc, [arrays], core_ids=[0])
    return r.results[0]["out_0_dram"]
```
